# Optimizing a Trainium2 kernel written in Bass

```python
import math
import jax
import jax.numpy as jnp
from jax import lax
import numpy as np

D_MODEL = 1024
BATCH = 1
SEQ = 512
DEPTH = 2
DEC_BATCH = 8
DEC_SEQ = 8
PAST_LEN = 1024
PAGE_SIZE = 128

N_AB = (DEPTH + 1) // 2
N_C = DEPTH // 2
HA = 4
DVA = D_MODEL // (2 * HA)
DQA = DVA // 2
HB = 4
DKB = D_MODEL // (2 * HB)
DVB = DKB
HC = 8
KVC = 2
DHC = D_MODEL // HC
HI = 8
DI = 64
HX = 4
DHX = D_MODEL // HX
N_MEM = 256
D_FF = 256 * ((8 * D_MODEL // 3 + 255) // 256)
CONV_W = 3
ROPE_THETA = 500000.0
ROT_DIV = 4
Q_BLOCK = 128
HGRN_CHUNK = 64
DSA_TOPK_MAX = 256
EPS = 1e-6
AB_SPLITS = (2 * HA * DQA, 2 * HA * DQA, HA * DVA, HB * DKB, HB * DKB, HB * DVB, HB * DVB)
C_SPLITS = (HC * DHC, KVC * DHC, KVC * DHC, HI * DI, DI, HI)
AB_WIDTH = sum(AB_SPLITS)
C_WIDTH = sum(C_SPLITS)

kernel_name = 'hybrid_diffattn_hgrn2_dsa_decode_step'

def _rms(x, g):
    xf = x.astype(jnp.float32)
    y = xf * lax.rsqrt(jnp.mean(xf * xf, axis=-1, keepdims=True) + EPS)
    return (y * g.astype(jnp.float32)).astype(x.dtype)

def _split(z, sizes):
    return jnp.split(z, np.cumsum(sizes)[:-1].tolist(), axis=-1)

def _rope(x, pos):
    half = x.shape[-1] // ROT_DIV // 2
    rot = 2 * half
    inv = jnp.exp(jnp.arange(half, dtype=jnp.float32) * (-math.log(ROPE_THETA) / half))
    ang = pos.astype(jnp.float32)[:, None] * inv[None, :]
    cos = jnp.cos(ang)[None, :, None, :]
    sin = jnp.sin(ang)[None, :, None, :]
    x1 = x[..., :half].astype(jnp.float32)
    x2 = x[..., half:rot].astype(jnp.float32)
    xr = jnp.concatenate([x1 * cos - x2 * sin, x2 * cos + x1 * sin], axis=-1).astype(x.dtype)
    return jnp.concatenate([xr, x[..., rot:]], axis=-1)

def _gather_pages(pool, j, pt):
    g = pool[j, pt]
    return g.reshape(pt.shape[0], pt.shape[1] * pool.shape[2], *pool.shape[3:])

def _sweep_queries(fn, q_arrays, q_pos):
    T = q_pos.shape[0]
    if T <= Q_BLOCK or T % Q_BLOCK != 0:
        return fn(q_arrays, q_pos)
    nb = T // Q_BLOCK

    def split(a):
        return jnp.moveaxis(a.reshape(a.shape[0], nb, Q_BLOCK, *a.shape[2:]), 1, 0)

    blocks = tuple(split(a) for a in q_arrays)
    out = lax.map(lambda args: fn(args[0], args[1]), (blocks, q_pos.reshape(nb, Q_BLOCK)))
    out = jnp.moveaxis(out, 0, 1)
    return out.reshape(out.shape[0], T, *out.shape[3:])

def _diff_attention(q1, q2, k1, k2, v, q_pos, k_pos, lam):
    scale = DQA ** -0.5

    def blk(qs, qp):
        a, b = qs
        mask = (k_pos[None, :] <= qp[:, None])[None, None]

        def probs(q, k):
            s = jnp.einsum('bthd,bshd->bhts', q, k).astype(jnp.float32) * scale
            return jax.nn.softmax(jnp.where(mask, s, -jnp.inf), axis=-1)

        p = probs(a, k1) - lam * probs(b, k2)
        return jnp.einsum('bhts,bshd->bthd', p.astype(v.dtype), v)

    return _sweep_queries(blk, (q1, q2), q_pos)

def _hgrn2(q, k, v, logf, s0):
    B, T, H, _ = q.shape
    C = math.gcd(T, HGRN_CHUNK)
    n = T // C

    def chunks(a):
        return jnp.moveaxis(a.astype(jnp.float32).reshape(B, n, C, *a.shape[2:]), 1, 0)

    tri = jnp.tril(jnp.ones((C, C), dtype=bool))[None, :, :, None, None]

    def step(S, inp):
        qc, kc, vc, lc = inp
        b = jnp.cumsum(lc, axis=1)
        dec = jnp.exp(jnp.where(tri, b[:, :, None] - b[:, None, :], -jnp.inf))
        att = jnp.einsum('bthk,bshk,btshk->bhts', qc, kc, dec)
        o = jnp.einsum('bthk,bhkv->bthv', qc * jnp.exp(b), S) + jnp.einsum('bhts,bshv->bthv', att, vc)
        bl = b[:, -1]
        S = jnp.exp(bl)[..., None] * S + jnp.einsum('bshk,bshv->bhkv', kc * jnp.exp(bl[:, None] - b), vc)
        return S, o

    S, o = lax.scan(step, s0.astype(jnp.float32), (chunks(q), chunks(k), chunks(v), chunks(logf)))
    o = jnp.moveaxis(o, 0, 1).reshape(B, T, H, v.shape[-1])
    return o, S

def _ab_mixer(h, pos, l, j, W, past_kv, s0):
    B, T, _ = h.shape
    qa, ka, va, qb, fb, ib, gb = _split(h @ W['w_in_ab'][j], AB_SPLITS)
    qa = qa.reshape(B, T, HA, 2, DQA)
    ka = ka.reshape(B, T, HA, 2, DQA)
    q1 = _rope(qa[:, :, :, 0], pos)
    q2 = _rope(qa[:, :, :, 1], pos)
    k_rows = jnp.concatenate([_rope(ka[:, :, :, 0], pos), _rope(ka[:, :, :, 1], pos)], axis=-1)
    v_rows = va.reshape(B, T, HA, DVA)
    if past_kv is None:
        k_all, v_all = k_rows, v_rows
    else:
        k_all = jnp.concatenate([past_kv[0].astype(k_rows.dtype), k_rows], axis=1)
        v_all = jnp.concatenate([past_kv[1].astype(v_rows.dtype), v_rows], axis=1)
    lam_init = 0.8 - 0.6 * math.exp(-0.3 * l)
    f32 = jnp.float32
    lam = (jnp.exp(jnp.sum(W['diff_lq1'][j].astype(f32) * W['diff_lk1'][j].astype(f32)))
           - jnp.exp(jnp.sum(W['diff_lq2'][j].astype(f32) * W['diff_lk2'][j].astype(f32))) + lam_init)
    o_a = _diff_attention(q1, q2, k_all[..., :DQA], k_all[..., DQA:], v_all, pos,
                          jnp.arange(k_all.shape[1]), lam)
    o_a = _rms(o_a, W['diff_subln'][j]) * (1.0 - lam_init)
    lb = W['hgrn_lb'][j]
    fgate = lb + (1.0 - lb) * jax.nn.sigmoid(fb.astype(f32))

    def hd(a):
        return a.reshape(B, T, HB, a.shape[-1] // HB)

    qh = hd(jax.nn.silu(qb.astype(f32))) * DKB ** -0.5
    o_b, s_new = _hgrn2(qh, hd(1.0 - fgate), hd(ib.astype(f32)), hd(jnp.log(fgate)), s0)
    o_b = _rms(o_b.astype(h.dtype), W['hgrn_onorm'][j]) * jax.nn.silu(hd(gb))
    y = jnp.concatenate([o_a.reshape(B, T, HA * DVA), o_b.reshape(B, T, HB * DVB)], axis=-1) @ W['w_out_ab'][j]
    return y, k_rows, v_rows, s_new

def _dsa_attend(q, iq, iw, q_pos, ik_all, fetch, topk):
    k_pos = jnp.arange(ik_all.shape[1])
    scale = DHC ** -0.5

    def blk(qs, qp):
        qb, iqb, iwb = qs
        B, Tb = qb.shape[:2]
        isc = jax.nn.relu(jnp.einsum('bthd,bsd->bths', iqb, ik_all).astype(jnp.float32))
        isc = jnp.einsum('bths,bth->bts', isc, iwb.astype(jnp.float32))
        isc = jnp.where((k_pos[None, :] <= qp[:, None])[None], isc, -jnp.inf)
        top, sel = lax.top_k(isc, topk)
        ksel, vsel = fetch(sel)
        qg = qb.reshape(B, Tb, KVC, HC // KVC, DHC)
        s = jnp.einsum('btkgd,btjkd->btkgj', qg, ksel).astype(jnp.float32) * scale
        s = jnp.where(jnp.isfinite(top)[:, :, None, None, :], s, -jnp.inf)
        p = jax.nn.softmax(s, axis=-1).astype(vsel.dtype)
        return jnp.einsum('btkgj,btjkd->btkgd', p, vsel).reshape(B, Tb, HC, DHC)

    return _sweep_queries(blk, (q, iq, iw), q_pos)

def _c_mixer(h, pos, j, W, past):
    B, T, _ = h.shape
    q, k, v, iq, ik, iw = _split(h @ W['w_in_c'][j], C_SPLITS)
    q = _rope(q.reshape(B, T, HC, DHC), pos)
    k_rows = _rope(k.reshape(B, T, KVC, DHC), pos)
    v_rows = v.reshape(B, T, KVC, DHC)
    iq = _rope(iq.reshape(B, T, HI, DI), pos)
    ik_rows = _rope(_rms(ik, W['idx_k_norm'][j])[:, :, None, :], pos)[:, :, 0]
    iw = iw * (HI * DI) ** -0.5
    take = jax.vmap(lambda kb, vb, sb: (kb[sb], vb[sb]))
    if past is None:
        ik_all = ik_rows

        def fetch(sel):
            return take(k_rows, v_rows, sel)
    else:
        pool_k, pool_v, pool_ik, pt = past
        P = pt.shape[1] * PAGE_SIZE
        ik_all = jnp.concatenate([_gather_pages(pool_ik, j, pt).astype(ik_rows.dtype), ik_rows], axis=1)

        def fetch(sel):
            ps = jnp.minimum(sel, P - 1)
            phys = jax.vmap(lambda tb, sb: tb[sb])(pt, ps // PAGE_SIZE)
            slot = ps % PAGE_SIZE
            kn, vn = take(k_rows, v_rows, jnp.clip(sel - P, 0, T - 1))
            is_past = (sel < P)[..., None, None]
            return (jnp.where(is_past, pool_k[j, phys, slot].astype(kn.dtype), kn),
                    jnp.where(is_past, pool_v[j, phys, slot].astype(vn.dtype), vn))
    topk = min(DSA_TOPK_MAX, ik_all.shape[1] // 4)
    o = _dsa_attend(q, iq, iw, pos, ik_all, fetch, topk)
    y = o.reshape(B, T, HC * DHC) @ W['w_out_c'][j]
    return y, k_rows, v_rows, ik_rows

def _cross_attn(h, mk, mv, w_q, w_o):
    B, T, _ = h.shape
    q = (h @ w_q).reshape(B, T, HX, DHX)
    s = jnp.einsum('bthd,bmhd->bhtm', q, mk.astype(q.dtype)).astype(jnp.float32) * DHX ** -0.5
    p = jax.nn.softmax(s, axis=-1).astype(q.dtype)
    o = jnp.einsum('bhtm,bmhd->bthd', p, mv.astype(q.dtype)).reshape(B, T, HX * DHX)
    return o @ w_o

def _conv_ffn(h, l, W, prev):
    B, T, _ = h.shape
    g, u = jnp.split(h @ W['w_ffn_in'][l], 2, axis=-1)
    if prev is None:
        prev = jnp.zeros((B, CONV_W - 1, D_FF), g.dtype)
    gp = jnp.concatenate([prev.astype(g.dtype), g], axis=1)
    w = W['conv_ffn_w'][l]
    gc = W['conv_ffn_b'][l] + gp[:, 0:T] * w[0]
    for i in range(1, CONV_W):
        gc = gc + gp[:, i:i + T] * w[i]
    y = (jax.nn.silu(gc) * u) @ W['w_ffn_out'][l]
    return y, gp[:, T:]

def _trunk(x, pos, mem_k, mem_v, past, W):
    B = x.shape[0]
    new = {'diff_k': [], 'diff_v': [], 'hgrn': [], 'dsa_k': [], 'dsa_v': [], 'dsa_ik': [], 'conv': []}
    for l in range(DEPTH):
        j = l // 2
        h = _rms(x, W['norm_mix'][l])
        if l % 2 == 0:
            if past is None:
                past_kv = None
                s0 = jnp.zeros((B, HB, DKB, DVB), jnp.float32)
            else:
                past_kv = (_gather_pages(past['diff_k'], j, past['pt']), _gather_pages(past['diff_v'], j, past['pt']))
                s0 = past['hgrn'][j].astype(jnp.float32)
            y, k_rows, v_rows, s_new = _ab_mixer(h, pos, l, j, W, past_kv, s0)
            new['diff_k'].append(k_rows)
            new['diff_v'].append(v_rows)
            new['hgrn'].append(s_new)
        else:
            past_c = None if past is None else (past['dsa_k'], past['dsa_v'], past['dsa_ik'], past['pt'])
            y, k_rows, v_rows, ik_rows = _c_mixer(h, pos, j, W, past_c)
            new['dsa_k'].append(k_rows)
            new['dsa_v'].append(v_rows)
            new['dsa_ik'].append(ik_rows)
        x = x + y
        x = x + _cross_attn(_rms(x, W['norm_x'][l]), mem_k[l], mem_v[l], W['w_xq'][l], W['w_xo'][l])
        f, conv_state = _conv_ffn(_rms(x, W['norm_ffn'][l]), l, W, None if past is None else past['conv'][l])
        x = x + f
        new['conv'].append(conv_state)
    stacked = {name: jnp.stack(vals, axis=0) for name, vals in new.items()}
    return _rms(x, W['norm_final']), stacked

def setup_inputs(seed: int = 0) -> dict:
    key = jax.random.key(seed)
    ks = iter(jax.random.split(key, 64))
    f32 = jnp.float32

    def nrm(shape, scale=1.0):
        return scale * jax.random.normal(next(ks), shape, f32)

    def gain(shape):
        return 1.0 + 0.02 * jax.random.normal(next(ks), shape, f32)

    n_pages = PAST_LEN // PAGE_SIZE
    n_used = DEC_BATCH * n_pages
    n_pool = n_used + max(1, n_used // 4)
    page_table = jax.random.permutation(next(ks), n_pool)[:n_used].reshape(DEC_BATCH, n_pages).astype(jnp.int32)
    d = D_MODEL
    return {
        'x_prompt': nrm((BATCH, SEQ, d)),
        'x_sample': nrm((DEC_BATCH, DEC_SEQ, d)),
        'cache_diff_k': nrm((N_AB, n_pool, PAGE_SIZE, HA, 2 * DQA)),
        'cache_diff_v': nrm((N_AB, n_pool, PAGE_SIZE, HA, DVA)),
        'state_hgrn': nrm((N_AB, DEC_BATCH, HB, DKB, DVB), 0.5),
        'cache_dsa_k': nrm((N_C, n_pool, PAGE_SIZE, KVC, DHC)),
        'cache_dsa_v': nrm((N_C, n_pool, PAGE_SIZE, KVC, DHC)),
        'cache_dsa_ik': nrm((N_C, n_pool, PAGE_SIZE, DI)),
        'cache_mem_k': nrm((DEPTH, DEC_BATCH, N_MEM, HX, DHX)),
        'cache_mem_v': nrm((DEPTH, DEC_BATCH, N_MEM, HX, DHX)),
        'state_ffn_conv': nrm((DEPTH, DEC_BATCH, CONV_W - 1, D_FF)),
        'page_table': page_table,
        'mem_prompt': nrm((BATCH, N_MEM, d)),
        'norm_mix': gain((DEPTH, d)),
        'w_in_ab': nrm((N_AB, d, AB_WIDTH), d ** -0.5),
        'diff_lq1': nrm((N_AB, DQA), 0.1),
        'diff_lk1': nrm((N_AB, DQA), 0.1),
        'diff_lq2': nrm((N_AB, DQA), 0.1),
        'diff_lk2': nrm((N_AB, DQA), 0.1),
        'diff_subln': gain((N_AB, DVA)),
        'hgrn_lb_logits': nrm((N_AB + 1, HB * DKB)),
        'hgrn_onorm': gain((N_AB, DVB)),
        'w_out_ab': nrm((N_AB, HA * DVA + HB * DVB, d), (HA * DVA + HB * DVB) ** -0.5),
        'w_in_c': nrm((N_C, d, C_WIDTH), d ** -0.5),
        'idx_k_norm': gain((N_C, DI)),
        'w_out_c': nrm((N_C, HC * DHC, d), (HC * DHC) ** -0.5),
        'norm_x': gain((DEPTH, d)),
        'norm_mem': gain((DEPTH, d)),
        'w_xq': nrm((DEPTH, d, HX * DHX), d ** -0.5),
        'w_xk': nrm((DEPTH, d, HX * DHX), d ** -0.5),
        'w_xv': nrm((DEPTH, d, HX * DHX), d ** -0.5),
        'w_xo': nrm((DEPTH, HX * DHX, d), (HX * DHX) ** -0.5),
        'norm_ffn': gain((DEPTH, d)),
        'w_ffn_in': nrm((DEPTH, d, 2 * D_FF), d ** -0.5),
        'conv_ffn_w': nrm((DEPTH, CONV_W, D_FF), CONV_W ** -0.5),
        'conv_ffn_b': nrm((DEPTH, D_FF), 0.01),
        'w_ffn_out': nrm((DEPTH, D_FF, d), D_FF ** -0.5),
        'norm_final': gain((d,)),
    }

def reference(x_prompt, x_sample, cache_diff_k, cache_diff_v, state_hgrn, cache_dsa_k, cache_dsa_v, cache_dsa_ik,
              cache_mem_k, cache_mem_v, state_ffn_conv, page_table, mem_prompt,
              norm_mix, w_in_ab, diff_lq1, diff_lk1, diff_lq2, diff_lk2, diff_subln, hgrn_lb_logits, hgrn_onorm,
              w_out_ab, w_in_c, idx_k_norm, w_out_c, norm_x, norm_mem, w_xq, w_xk, w_xv, w_xo, norm_ffn,
              w_ffn_in, conv_ffn_w, conv_ffn_b, w_ffn_out, norm_final):
    hgrn_lb = jnp.cumsum(jax.nn.softmax(hgrn_lb_logits.astype(jnp.float32), axis=0), axis=0)[:N_AB]
    W = {
        'norm_mix': norm_mix, 'w_in_ab': w_in_ab, 'diff_lq1': diff_lq1, 'diff_lk1': diff_lk1,
        'diff_lq2': diff_lq2, 'diff_lk2': diff_lk2, 'diff_subln': diff_subln, 'hgrn_lb': hgrn_lb,
        'hgrn_onorm': hgrn_onorm, 'w_out_ab': w_out_ab, 'w_in_c': w_in_c, 'idx_k_norm': idx_k_norm,
        'w_out_c': w_out_c, 'norm_x': norm_x, 'w_xq': w_xq, 'w_xo': w_xo, 'norm_ffn': norm_ffn,
        'w_ffn_in': w_ffn_in, 'conv_ffn_w': conv_ffn_w, 'conv_ffn_b': conv_ffn_b, 'w_ffn_out': w_ffn_out,
        'norm_final': norm_final,
    }
    B, T, _ = x_prompt.shape
    Td = x_sample.shape[1]
    n_mem = mem_prompt.shape[1]
    mem_h = [_rms(mem_prompt, norm_mem[l]) for l in range(DEPTH)]
    mk_p = [(mem_h[l] @ w_xk[l]).reshape(B, n_mem, HX, DHX) for l in range(DEPTH)]
    mv_p = [(mem_h[l] @ w_xv[l]).reshape(B, n_mem, HX, DHX) for l in range(DEPTH)]
    y_prompt, sp = _trunk(x_prompt, jnp.arange(T), mk_p, mv_p, None, W)
    past_len = page_table.shape[1] * PAGE_SIZE
    past = {'diff_k': cache_diff_k, 'diff_v': cache_diff_v, 'hgrn': state_hgrn, 'dsa_k': cache_dsa_k,
            'dsa_v': cache_dsa_v, 'dsa_ik': cache_dsa_ik, 'conv': state_ffn_conv, 'pt': page_table}
    y_sample, ss = _trunk(x_sample, past_len + jnp.arange(Td), [cache_mem_k[l] for l in range(DEPTH)],
                          [cache_mem_v[l] for l in range(DEPTH)], past, W)
    return (y_prompt, y_sample,
            sp['diff_k'], sp['diff_v'], sp['hgrn'], sp['dsa_k'], sp['dsa_v'], sp['dsa_ik'],
            jnp.stack(mk_p, axis=0), jnp.stack(mv_p, axis=0), sp['conv'],
            ss['diff_k'], ss['diff_v'], ss['hgrn'], ss['dsa_k'], ss['dsa_v'], ss['dsa_ik'], ss['conv'])


_drawn_inputs = setup_inputs


def setup_inputs(seed=0):
    import zlib

    import numpy as np

    out = dict(_drawn_inputs(seed))
    spreads = {}
    factors = {'diff_lk2': 2.814,
     'diff_subln': 3.788,
     'hgrn_onorm': 4.659,
     'norm_x': 8.0,
     'norm_mem': 2.825,
     'conv_ffn_b': 5.41,
     'norm_final': 2.717}
    for name, (base, spread) in spreads.items():
        noise = np.random.default_rng([zlib.crc32(name.encode()), seed]).standard_normal(out[name].shape)
        drawn = base * np.exp(spread * noise) if base else spread * noise
        out[name] = jnp.asarray(drawn.astype(out[name].dtype))
    for name, factor in factors.items():
        out[name] = (out[name] * factor).astype(out[name].dtype)
    return out
```

```python
import math
import numpy as np
import concourse.bass as bass
from concourse import mybir
from contextlib import ExitStack

D = 1024
SEQ = 512
NB, TS = 8, 8
NSAMP = NB * TS
TOK = SEQ + NSAMP
NTILE = 5
PAST, PAGE = 1024, 128
NPAGE = PAST // PAGE
DEPTH = 2
H = 4
DFF = 2816
KC = D // 128
FC = DFF // 128
NMEM = 256
EPS = 1e-6
NEG = -1e30
LAM_INIT = 0.8 - 0.6 * math.exp(-0.3 * 0)
THETA = 500000.0
COLS = [(i * 128, 128) for i in range(4)] + [(SEQ, NSAMP)]
WC_Q, WC_K, WC_V, WC_IQ, WC_IK, WC_IW, WC_END = 0, 1024, 1280, 1536, 2048, 2112, 2120

CONST = {}
_at = 0
for _name, _n in (("ident", 128), ("ones", 128), ("causal", 128), ("newmask", 120), ("expand", 512),
                  ("rope8", 5 * 2 * 16), ("rope16", 5 * 2 * 32), ("reset", TOK), ("heads", 64), ("sameq", 64),
                  ("block64", 64), ("rowmask", 8), ("mapsel", 2)):
    CONST[_name] = (_at, _n)
    _at += _n
NCONST = _at
LEVELS = [0, 1, 2, 4, 8, 16, 32, 64]


def constants():
    c = np.zeros((128, NCONST), np.float32)

    def put(name, a):
        at, n = CONST[name]
        c[:a.shape[0], at:at + n] = a.reshape(a.shape[0], n)

    r = np.arange(128)
    put("ident", np.eye(128, dtype=np.float32))
    put("ones", np.full((128, 128), 1.0 / 128, np.float32))
    put("causal", np.where(r[None, :] <= r[:, None], 0.0, NEG).astype(np.float32))
    off = np.arange(120)[None, :] - 56
    put("newmask", np.where((off >= 0) & (off <= (r % 8)[:, None]), 0.0, NEG).astype(np.float32))
    e = np.zeros((64, 4, 128), np.float32)
    for p in range(4):
        for row in range(128):
            e[(2 * p + row // 64) * 8 + row % 8, p, row] = 1.0
    put("expand", e)
    pos = np.zeros((128, 5), np.float32)
    pos[:, :4] = np.arange(512).reshape(4, 128).T
    pos[:64, 4] = PAST + np.arange(64) % TS
    for name, half in (("rope8", 8), ("rope16", 16)):
        inv = np.exp(np.arange(half, dtype=np.float32) * np.float32(-math.log(THETA) / half)).astype(np.float32)
        ang = (pos[:, :, None] * inv).astype(np.float32)
        co, si = np.cos(ang), np.sin(ang)
        put(name, np.stack([np.concatenate([co, co], -1), np.concatenate([-si, si], -1)], 2).astype(np.float32))
    reset = np.ones(TOK, np.float32)
    reset[0:SEQ:128] = 0.0
    reset[SEQ::TS] = 0.0
    put("reset", np.tile(reset, (128, 1)))
    hq = np.arange(64)
    put("heads", (hq[None, :] // 8 == np.arange(8)[:, None]).astype(np.float32))
    put("sameq", (hq[None, :] % 8 == hq[:, None] % 8).astype(np.float32))
    put("block64", np.where((hq[None, :] // 8 == hq[:, None] // 8) & (hq[None, :] % 8 <= hq[:, None] % 8),
                            0.0, NEG).astype(np.float32))
    put("rowmask", (hq[:, None] // 8 == np.arange(8)[None, :]).astype(np.float32))
    put("mapsel", np.stack([(r % 16 < 8), (r % 16 >= 8)], 1).astype(np.float32))
    s, t = r[:, None], r[None, :]
    lev = np.zeros((128, len(LEVELS), 128), np.float32)
    for i, h in enumerate(LEVELS):
        if h == 0:
            lev[:, i] = s == t
        else:
            lev[:, i] = (s // (2 * h) == t // (2 * h)) & (s // h % 2 == 0) & (t // h % 2 == 1)
    return c, lev.reshape(128, -1)


class Turns:

    def __init__(self):
        self.who = []

    def add(self, w):
        self.who.append(w)
        return len(self.who) - 1

    def count(self, w, n):
        return sum(1 for x in self.who[:n] if x == w)


class Chain:

    def __init__(self, eng, sem):
        self.eng, self.sem, self.n = eng, sem, 0

    def __call__(self, ins):
        self.n += 1
        ins.then_inc(self.sem, 1)
        self.eng.wait_ge(self.sem, self.n)


def build(nc, A, O):
    f32, bf16, u8, i32 = mybir.dt.float32, mybir.dt.bfloat16, mybir.dt.uint8, mybir.dt.int32
    ALU, ACT, AX = mybir.AluOpType, mybir.ActivationFunctionType, mybir.AxisListType
    NW, NC_ = 5, 3
    AW = 18688
    ctx = ExitStack()
    with ctx:
        ctx.enter_context(nc.allow_non_contiguous_dma(reason="narrow rows of small operands"))

        def sb(name, shape, dt=f32):
            return ctx.enter_context(nc.sbuf_tensor(name, shape, dt))

        def sem(name):
            return ctx.enter_context(nc.semaphore(name))

        cst = sb("cst", [128, NCONST])
        lev = sb("lev", [128, len(LEVELS) * 128], u8)
        identb = sb("identb", [128, 128], bf16)
        causalb = sb("causalb", [128, 128], bf16)
        newmaskb = sb("newmaskb", [128, 120], bf16)
        x = sb("x", [128, NTILE, D])
        hT = sb("hT", [128, KC, TOK])
        oT = sb("oT", [128, KC, TOK])
        W = sb("W", [128, NW, 4, 512])
        C = sb("C", [128, NC_, 2048])
        arena = sb("arena", [128, AW])
        gains = sb("gains", [128, 8, 8])
        small = sb("small", [128, 10])
        misc = sb("misc", [128, 64])
        stat = sb("stat", [128, 64])
        pt = sb("pt", [1, 64], i32)
        gs_t = sb("gs_t", [128, 80])
        PS = ctx.enter_context(nc.psum_tensor("PS", [128, 8 * 512], f32))

        def const(name, rows=128):
            at, n = CONST[name]
            return cst[0:rows, at:at + n]

        ident = const("ident")
        rope8 = const("rope8").rearrange("p (i s c) -> p i s c", i=5, s=2)
        rope16 = const("rope16").rearrange("p (i s c) -> p i s c", i=5, s=2)
        levels = lev[:, :].rearrange("p (l t) -> p l t", t=128)

        def region(at, *shape):
            n = int(np.prod(shape))
            assert at + n <= AW, (at, n, AW)
            v = arena[:, at:at + n]
            if len(shape) == 1:
                return v
            if len(shape) == 2:
                return v.rearrange("p (a b) -> p a b", b=shape[1])
            if len(shape) == 3:
                return v.rearrange("p (a b c) -> p a b c", b=shape[1], c=shape[2])
            return v.rearrange("p (a b c d) -> p a b c d", b=shape[1], c=shape[2], d=shape[3])

        def bank(n):
            return PS[:, (n % 8) * 512:(n % 8) * 512 + 512]

        def tbank(n):
            return PS[:, 3072 + 512 * (n % 2):3584 + 512 * (n % 2)]

        def sreg(j):
            return PS[:, 1536 * (j % 2):1536 * (j % 2) + 1536]

        oflat = oT[:, :, :].rearrange("p c t -> p (c t)")
        hflat = hT[:, :, :].rearrange("p c t -> p (c t)")
        junk = oflat[:, 0:1024]
        xn = [oflat[:, 1024 + 1024 * i:2048 + 1024 * i] for i in range(2)]
        ss, ms, sd, rstd = (stat[:, 8 * i:8 * i + 5] for i in range(4))
        lam = misc[:, 0:1]
        sgn = misc[:, 1:2]
        eps_col = misc[:, 2:3]
        lb, omlb = misc[:, 4:8], misc[:, 8:12]
        subg = misc[:, 12:13]
        mx, nm, sm, rs = (stat[:, 32 + 4 * i:36 + 4 * i] for i in range(4))
        mx2, nm2, sm2 = ([v, stat[:, a:a + 4]] for v, a in ((mx, 48), (nm, 52), (sm, 56)))
        rs2 = [rs, stat[:, 60:64]]

        P = [region(0, 1088), region(1088, 1088)]
        PT = region(2176, 9, 128)
        L = {
            "grow": region(0, 1024), "srow": region(1024, 128), "lrow": region(1280, 4, 64), "lp": region(1536, 2, 64),
            "ls": region(1664, 2), "le": region(1668, 2), "ld": region(1672, 1), "lbm": region(1676, 4),
            "lbd": region(1680, 8), "lbe": region(1688, 8), "lbr": region(1696, 4), "lev_in": region(2048, len(LEVELS) * 128),
            "a_qk": region(3328, 5, 1024), "a_v": region(8448, 5, 512), "qT_a": region(11008, 4, TOK),
            "kT_a": region(13312, 4, TOK), "qz_a": region(15616, 8, 4, 32), "KT_a": region(3328, 4, 1024),
            "ropet": region(18176, 2, 256),
            "HQ": region(0, 4, TOK), "HK": region(2304, 4, TOK), "B": region(4608, 4, TOK), "QK": region(6912, 4, TOK),
            "ATT": region(9216, 5, 4, 128), "KD": region(11776, 5, 4, 128), "ib": region(14336, 5, 512),
            "SS": region(2304, 4, 4, 128), "Vz": region(0, 2, 1024), "OB": region(4608, 4, TOK),
            "edec": region(16896, 4, 8), "sq": region(9216, 2, TOK), "rt": region(10368, 2, TOK),
            "S0": hflat[:, 0:4096].rearrange("p (b h v) -> p b h v", b=8, h=4),
            "qxT": region(3328, 8, TOK), "mk": region(7936, 2, 1024), "mkK": region(7936, 8, 256), "mv": region(9984, 2, 1024),
            "mkT": region(12032, 8, 256), "qzx": region(14080, 8, TOK), "memT": region(14080, 8, 256),
            "mem": region(16128, 2, 1024),
            "act": region(0, FC, TOK), "frow": region(12672, DFF), "cstate": region(15488, FC, 18),
            "fcol": region(15884, FC, 20), "gc": region(16324, 2, TOK), "sil": region(17476, 2, TOK),
            "gs": gs_t[:, :].rearrange("p (b w) -> p b w", b=8),
            "i_tm": region(0, 5, 584), "iqT": region(2920, 8, TOK), "ikT": region(7528, TOK), "iwT": region(8104, 64),
            "relup": region(8168, 2, 512), "iscp": [region(9192, 256), region(9448, 384), region(9832, 512)],
            "wz": region(10344, TOK), "IKT": region(10920, 2, 1024), "relu": region(12968, 2, 1088),
            "iscs": region(15144, 1088), "iqs": region(16800, 8, 64), "qs_c": region(18176, 8, 2, 32), "ikn": region(16232, 64), "ikj": region(16296, 64),
            "work": region(0, 1088), "eq": region(1088, 1088), "rank": region(2176, 1088), "top": region(3264, 8),
            "cnt": region(3272, 8),
            "c_tm": region(3328, 5, 1280), "v_c": region(9728, 5, 256), "qT_c": region(11008, 8, TOK),
            "kT_c": region(15616, 2, TOK), "KT_c": region(3328, 4, 1024), "ropet_c": region(11008, 2, 320),
            "selp": [region(16800 + a, n).bitcast(bf16) for a, n in ((0, 128), (128, 192), (320, 256))],
            "sels": region(16800 + 576, 544).bitcast(bf16), "expb": region(16800 + 1120, 256).bitcast(bf16),
            "fin": region(0, D),
        }
        FIRST = 16 * 15
        ROWS = {"hgrn": 128, "mem0": 144, "ffn0": 192, "ikn": 208, "mem1": 224, "ffn1": 272, "fin": 288}
        JOBS_AP = [(i, h) for i in range(4) for h in range(H)]
        JOBS_CP = [(i, hp) for i in range(4) for hp in range(4)]

        first_in = sem("first_in")
        cast_in = sem("cast_in")
        rows_in = sem("rows_in")
        w_full = [sem(f"w_full{i}") for i in range(NW)]
        w_free = sem("w_free")
        c_full = [sem(f"c_full{i}") for i in range(NC_)]
        c_free = sem("c_free")
        proj_done = sem("proj_done")
        proj_act = sem("proj_act")
        proj_dve = sem("proj_dve")
        tr_done = sem("tr_done")
        tr_act = sem("tr_act")
        tr_dve = sem("tr_dve")
        squares = sem("squares")
        means = sem("means")
        roots = sem("roots")
        rstds = sem("rstds")
        xn_done = sem("xn_done")
        scores_ready = sem("scores_ready")
        rowmax_ready = sem("rowmax_ready")
        exp_done = sem("exp_done")
        probs_ready = sem("probs_ready")
        out_ready = sem("out_ready")
        out_copied = sem("out_copied")
        phase = {e: sem(f"phase_{e}") for e in ("pe", "act", "dve", "pool")}
        dve_step = sem("dve_step")
        act_step = sem("act_step")
        stores = sem("stores")
        handoff = {k: sem(k) for k in ("lam_in", "lam_e", "decay_d", "decay_e", "qk_ready", "qk_used", "f_ready", "logf",
                                       "relu_done", "relu_used", "isc_done", "silu_done", "sq_done", "onorm_mean", "onorm_root",
                                       "onorm_done", "gate_done", "u_used", "wz_ready", "kd_ready", "pool_rows")}

        def halves(w, cols, nk=KC):
            v = w.rearrange("(k p) n -> p k n", p=128)
            return [(v, k, min(4, nk - k), cols) for k in range(0, nk, 4)]

        blk = lambda a, b, step=512: [[(i, min(i + step, b))] for i in range(a, b, step)]
        ORDER = {}
        stream = []

        def add(name, w, blocks, nk=KC):
            ORDER[name] = [halves(w, cols, nk) for cols in blocks]
            for b in ORDER[name]:
                stream.extend(b)

        add("a_in", A["w_in_ab"][0], blk(0, 1536))
        add("b_in", A["w_in_ab"][0], blk(1536, 2560) + blk(3072, 3584) + blk(2560, 3072))
        add("ab_out", A["w_out_ab"][0], blk(0, D))

        def add_rest(l):
            add(f"xq{l}", A["w_xq"][l], blk(0, D))
            add(f"xk{l}", A["w_xk"][l], blk(0, D))
            add(f"xv{l}", A["w_xv"][l], blk(0, D))
            add(f"xo{l}", A["w_xo"][l], blk(0, D))
            add(f"up{l}", A["w_ffn_in"][l], [[(256 * j, 256 * j + 256), (DFF + 256 * j, DFF + 256 * j + 256)]
                                             for j in range(FC // 2)])
            add(f"down{l}", A["w_ffn_out"][l], blk(0, D), FC)

        add_rest(0)
        add("c_idx", A["w_in_c"][0], [[(WC_IQ, WC_IK)], [(WC_IK, WC_END)]])
        add("c_qkv", A["w_in_c"][0], blk(0, WC_IQ))
        add("c_out", A["w_out_c"][0], blk(0, D))
        add_rest(1)

        block = ctx.enter_context(nc.Block())

        @block.sync
        def _(sp):
            for n, (v, k0, nk, cols) in enumerate(stream):
                if n >= NW:
                    sp.wait_ge(w_free, n - NW + 1)
                at = 0
                for a, b in cols:
                    sp.dma_start(W[:, n % NW, 0:nk, at:at + b - a], v[:, k0:k0 + nk, a:b]).then_inc(w_full[n % NW], 16)
                    at += b - a

        def w_target(n):
            return 16 * sum(len(stream[m][3]) for m in range(n % NW, n + 1, NW))

        K_A, V_A = A["cache_diff_k"][0], A["cache_diff_v"][0]
        K_C, V_C, IK_C = A["cache_dsa_k"][0], A["cache_dsa_v"][0], A["cache_dsa_ik"][0]
        CL = []

        def diff_slots():
            for b in range(NB + 1):
                if b < NB:
                    CL.extend([("ka", b, 0), ("ka", b, 4)])
                if b > 0:
                    CL.extend([("va", b - 1, 0), ("va", b - 1, 4)])

        def cross_slots(l):
            CL.extend([(f"mk{l}", b, 0) for b in range(NB)])
            CL.extend([(f"mv{l}", b, 0) for b in range(NB)])

        diff_slots()
        cross_slots(0)
        CL.extend([("ik", b, 0) for b in range(NB)])
        CL.extend([("kc", 0, 0), ("kc", 1, 0)])
        for p in range(1, NB // 2 + 1):
            if p < NB // 2:
                CL.extend([("kc", 2 * p, 0), ("kc", 2 * p + 1, 0)])
            CL.extend([("vc", 2 * p - 2, 0), ("vc", 2 * p - 1, 0)])
        cross_slots(1)

        def c_pieces(kind):
            return {"ka": 4, "va": 4, "ik": 8, "kc": 8, "vc": 8}.get(kind, 1)

        def c_target(n):
            return 16 * sum(c_pieces(CL[m][0]) for m in range(n % NC_, n + 1, NC_))

        @block.gpsimd
        def _(pool):
            pool.dma_start(pt[0:1, :], A["page_table"].rearrange("b n -> (b n)").unsqueeze(0)).then_inc(handoff["pool_rows"], 16)
            pool.wait_ge(handoff["pool_rows"], 16)
            for n, (kind, b, first) in enumerate(CL):
                if n >= NC_:
                    pool.wait_ge(c_free, n - NC_ + 1)
                slot = C[:, n % NC_, :]
                if kind[0] == "m":
                    src = A["cache_mem_" + kind[1]][int(kind[2]), b].rearrange("(m p) h d -> p m (h d)", p=128)
                    pool.dma_start(slot.rearrange("p (m d) -> p m d", m=2), src).then_inc(c_full[n % NC_], 16)
                    continue
                pools = {"ka": K_A, "va": V_A, "kc": K_C, "vc": V_C, "ik": IK_C}[kind]
                v = pools.rearrange("g s d -> s g d") if kind == "ik" else pools.rearrange("g s h d -> s g (h d)")
                width = v.shape[2]
                for j in range(c_pieces(kind)):
                    at = b * NPAGE + first + j
                    page = pool.value_load(pt[0:1, at:at + 1], min_val=0, max_val=v.shape[1] - 1)
                    pool.dma_start(slot[:, j * width:(j + 1) * width],
                                   v[:, bass.ds(page, 1), :].rearrange("s g d -> s (g d)")).then_inc(c_full[n % NC_], 16)

        @block.tensor
        def _(pe):
            S = {"w": 0, "c": 0, "job": 0, "phase": 0, "xn": 0, "release": 0}
            pj, tj = Turns(), Turns()
            mm, tp = nc.tensor.matmul, nc.tensor.transpose

            def barrier():
                S["phase"] += 1
                pe.drain().then_inc(phase["pe"], 1)
                for e in ("act", "dve"):
                    pe.wait_ge(phase[e], S["phase"])

            def open_bank(who):
                n = pj.add(who)
                if n >= 8:
                    w = pj.who[n - 8]
                    pe.wait_ge(proj_act if w == "A" else proj_dve, pj.count(w, n - 7))
                return n

            def open_tr(who):
                n = tj.add(who)
                if n >= 2:
                    w = tj.who[n - 2]
                    pe.wait_ge(tr_act if w == "A" else tr_dve, tj.count(w, n - 1))
                return tbank(n)

            def wait_tr(n=None):
                n = len(tj.who) if n is None else n
                for w, s in (("A", tr_act), ("D", tr_dve)):
                    if tj.count(w, n):
                        pe.wait_ge(s, tj.count(w, n))

            def wait_projections():
                for w, s in (("A", proj_act), ("D", proj_dve)):
                    if pj.count(w, len(pj.who)):
                        pe.wait_ge(s, pj.count(w, len(pj.who)))

            def cache():
                n = S["c"]
                S["c"] += 1
                pe.wait_ge(c_full[n % NC_], c_target(n))
                return C[:, n % NC_, :]

            def project(name, src, tiles, who, feature=False):
                for b in ORDER[name]:
                    width = sum(y - x_ for x_, y in b[0][3])
                    if feature:
                        nch = width // 128
                        units = [open_bank(who) for _ in range(nch + 1)]
                    else:
                        units = [open_bank(who) for _ in tiles]
                    for s, (_, k0, nk, _) in enumerate(b):
                        n = S["w"]
                        S["w"] += 1
                        pe.wait_ge(w_full[n % NW], w_target(n))
                        last_slot = s == len(b) - 1
                        if feature:
                            for c in range(nch):
                                for k in range(nk):
                                    lw = W[:, n % NW, k, c * 128:c * 128 + 128]
                                    a, z = s == 0 and k == 0, last_slot and k == nk - 1
                                    ins = mm(bank(units[c])[:, 0:SEQ], lw, src[:, k0 + k, 0:SEQ], start=a, stop=z)
                                    if z:
                                        ins.then_inc(proj_done, 1)
                                    ins = mm(bank(units[nch])[:, c * 64:c * 64 + 64], lw, src[:, k0 + k, SEQ:TOK],
                                             start=a and c == 0, stop=z, skip_group_check=True)
                            ins.then_inc(proj_done if last_slot else w_free, 1)
                        else:
                            for u, (c0, rows) in zip(units, tiles):
                                for k in range(nk):
                                    a, z = s == 0 and k == 0, last_slot and k == nk - 1
                                    ins = mm(bank(u)[0:rows, 0:width], src[:, k0 + k, c0:c0 + rows],
                                             W[:, n % NW, k, 0:width], start=a, stop=z)
                                if last_slot:
                                    ins.then_inc(proj_done, 1)
                            if not last_slot:
                                ins.then_inc(w_free, 1)
                        if last_slot:
                            pe.drain().then_inc(w_free, 1)

            def norm_transposes(tiles):
                for i, (c0, rows) in enumerate(tiles):
                    S["xn"] += 1
                    pe.wait_ge(xn_done, S["xn"])
                    for g in range(2):
                        t = open_tr("D")
                        for c in range(4):
                            ins = tp(t[:, c * 128:c * 128 + rows], xn[i % 2][0:rows, (4 * g + c) * 128:(4 * g + c + 1) * 128],
                                     ident[0:rows, 0:rows])
                        ins.then_inc(tr_done, 1)

            def tr_unit(who, pieces):
                t = open_tr(who)
                for off, src in pieces:
                    rows, cols = src.shape[0], src.shape[1]
                    ins = tp(t[0:cols, off:off + rows], src, ident[0:rows, 0:rows])
                ins.then_inc(tr_done, 1)

            def attend(jobs, prep, scores, prob_units, values):
                def start(j):
                    n = S["job"] + j
                    if prep:
                        prep(j)
                    if n >= 2:
                        pe.wait_ge(out_copied, n - 1)
                    scores(j, sreg(n)).then_inc(scores_ready, 1)

                start(0)
                for j in range(len(jobs)):
                    if j + 1 < len(jobs):
                        start(j + 1)
                    n = S["job"] + j
                    pe.wait_ge(probs_ready, n + 1)
                    for who, pieces in prob_units(j, P[n % 2]):
                        tr_unit(who, pieces)
                    wait_tr()
                    values(j, sreg(n)).then_inc(out_ready, 1)
                    if S["release"]:
                        pe.drain().then_inc(c_free, S["release"])
                        S["release"] = 0
                S["job"] += len(jobs)

            pe.wait_ge(first_in, FIRST)
            tr_unit("D", [(8 * c, L["grow"][0:8, c * 128:c * 128 + 128]) for c in range(8)])
            tr_unit("D", [(0, L["srow"][0:10, 0:128])])
            barrier()

            norm_transposes(COLS)
            barrier()
            project("a_in", hT, COLS, "A")
            barrier()
            for i, (c0, rows) in enumerate(COLS):
                tr_unit("D", [(h * 128, L["a_qk"][0:rows, i, h * 128:h * 128 + 128]) for h in range(H)])
                tr_unit("A", [(h * 128, L["a_qk"][0:rows, i, 512 + h * 128:640 + h * 128]) for h in range(H)])
            barrier()
            qT, kT, qz, KT, a_v = L["qT_a"], L["kT_a"], L["qz_a"], L["KT_a"], L["a_v"]
            jobs = JOBS_AP

            def ap_scores(j, s):
                i, h = jobs[j]
                n = (i + 1) * 128
                for m in range(2):
                    r = slice(64 * m, 64 * m + 64)
                    mm(s[:, 512 * m:512 * m + n], qT[r, h, i * 128:i * 128 + 128], kT[r, h, 0:n], start=True, stop=False,
                       skip_group_check=True)
                    ins = mm(s[:, 512 * m + n - 128:512 * m + n], identb[:, :], causalb[:, :], start=False, stop=True,
                             skip_group_check=True)
                return ins

            def ap_units(j, p):
                i, h = jobs[j]
                return [("A", [(c * 128, p[:, c * 128:c * 128 + 128]) for c in range(i + 1)])]

            def ap_values(j, s):
                i, h = jobs[j]
                for c in range(i + 1):
                    ins = mm(s[:, 0:128], a_v[:, c, h * 128:h * 128 + 128], PT[:, c, :], start=c == 0, stop=c == i)
                return ins

            attend(jobs, None, ap_scores, ap_units, ap_values)

            def as_prep(b):
                for half in range(2):
                    k = cache().rearrange("p (g h d) -> p g h d", g=4, h=H)
                    for h in range(H):
                        t = open_tr("A" if h % 2 else "D")
                        for g in range(4):
                            ins = tp(t[:, g * 128:g * 128 + 128], k[:, g, h, :], ident)
                        ins.then_inc(tr_done, 1)
                    pe.drain().then_inc(c_free, 1)
                wait_tr()

            def as_scores(b, s):
                mm(s[:, 1024:1088], identb[:, :], newmaskb[:, 56 - 8 * b:120 - 8 * b], start=True, stop=False, skip_group_check=True)
                for h in range(H):
                    o = slice(32 * h, 32 * h + 32)
                    for c in range(2):
                        mm(s[o, 512 * c:512 * c + 512], qz[:, b, h, :], KT[:, h, 512 * c:512 * c + 512], start=True, stop=True)
                    ins = mm(s[o, 1024:1088], qz[:, b, h, :], kT[:, h, SEQ:TOK], start=False, stop=True, skip_group_check=True)
                return ins

            def past_units(j, p):
                return [("D", [(c * 128, p[:, c * 128:c * 128 + 128]) for c in range(4)]),
                        ("A", [(c * 128, p[:, (c + 4) * 128:(c + 5) * 128]) for c in range(4)]),
                        ("D", [(0, p[:, 1024:1088])])]

            def as_values(b, s):
                v = [cache().rearrange("p (g h d) -> p g h d", g=4, h=H) for _ in range(2)]
                for h in range(H):
                    o = s[:, 16 * h:16 * h + 16]
                    for c in range(NPAGE):
                        mm(o, v[c // 4][:, c % 4, h, :], PT[:, c, 32 * h:32 * h + 16], start=c == 0, stop=False)
                    ins = mm(o, a_v[0:64, 4, h * 128:h * 128 + 128], PT[0:64, 8, 32 * h:32 * h + 16],
                             start=False, stop=True)
                S["release"] = 2
                return ins

            attend(list(range(NB)), as_prep, as_scores, past_units, as_values)
            barrier()
            for q, feature in (((0, 3), True), ((3, 4), False)):
                ORDER["b_part"] = ORDER["b_in"][q[0]:q[1]]
                project("b_part", hT, COLS, "A", feature)
            barrier()

            HQ, HK, QK, ATT, KD, SS, ib = L["HQ"], L["HK"], L["QK"], L["ATT"], L["KD"], L["SS"], L["ib"]
            for n, h in enumerate(LEVELS):
                pe.wait_ge(handoff["qk_ready"], n + 1)
                for i, (c0, rows) in enumerate(COLS):
                    if i == 4 and h > 4:
                        continue
                    u = open_bank("D")
                    for e in range(H):
                        lhs = (HK if h == 0 else QK)[:, e, c0:c0 + rows]
                        rhs = (HQ if h == 0 else QK)[:, e, c0:c0 + rows]
                        ins = mm(bank(u)[0:rows, e * 128:e * 128 + rows], lhs, rhs, start=True, stop=True)
                    ins.then_inc(proj_done, 1)
                pe.drain().then_inc(handoff["qk_used"], 1)
            barrier()
            pe.wait_ge(handoff["qk_ready"], len(LEVELS) + 1)
            for i, (c0, rows) in enumerate(COLS):
                tr_unit("A", [(e * 128, QK[:, e, c0:c0 + rows]) for e in range(H)])
            barrier()
            for i in range(4):
                u = open_bank("D")
                for e in range(H):
                    ins = mm(bank(u)[:, e * 128:e * 128 + 128], KD[:, i, e, :], ib[:, i, e * 128:e * 128 + 128], start=True, stop=True)
                ins.then_inc(proj_done, 1)
            barrier()
            for i in range(4):
                u = open_bank("A")
                for e in range(H):
                    o = bank(u)[:, e * 128:e * 128 + 128]
                    ins = mm(o, ib[:, i, e * 128:e * 128 + 128], ATT[:, i, e, :], start=True, stop=i == 0)
                    if i > 0:
                        ins = mm(o, SS[:, i - 1, e, :], QK[:, e, i * 128:i * 128 + 128], start=False, stop=True)
                ins.then_inc(proj_done, 1)
            u = open_bank("A")
            pe.wait_ge(rows_in, ROWS["hgrn"])
            for e in range(H):
                o = bank(u)[:, e * 64:e * 64 + 64]
                mm(o, ib[0:64, 4, e * 128:e * 128 + 128], ATT[0:64, 4, e, 0:64], start=True, stop=False, skip_group_check=True)
                for b in range(NB):
                    ins = mm(o[:, 8 * b:8 * b + 8], L["S0"][:, b, e, :], QK[:, e, SEQ + 8 * b:SEQ + 8 * b + 8],
                             start=False, stop=b == NB - 1, skip_group_check=True)
            ins.then_inc(proj_done, 1)
            for e in range(H):
                pe.wait_ge(handoff["kd_ready"], e + 1)
                for c in range(2):
                    u = open_bank("D")
                    mm(bank(u)[:, 0:512], KD[0:64, 4, e, :], L["Vz"][0:64, e % 2, 512 * c:512 * c + 512],
                       start=True, stop=True).then_inc(proj_done, 1)
            barrier()
            for c in range(KC):
                pe.wait_ge(handoff["sq_done"], c + 1)
                if c >= 2:
                    pe.wait_ge(handoff["onorm_root"], c - 1)
                s = sreg(c)
                mm(s[:, 0:512], const("ones"), L["sq"][:, c % 2, 0:512], start=True, stop=True)
                mm(s[:, 512:576], const("ones"), L["sq"][:, c % 2, 512:576], start=True, stop=True).then_inc(handoff["onorm_mean"], 1)
            barrier()
            project("ab_out", oT, COLS, "D")
            barrier()

            def cross_and_ffn(l):
                norm_transposes(COLS)
                barrier()
                project(f"xq{l}", hT, COLS, "A", feature=True)
                wait_projections()
                norm_transposes(COLS[0:2])
                barrier()
                project(f"xk{l}", L["memT"], COLS[0:2], "A")
                project(f"xv{l}", L["memT"], COLS[0:2], "A")
                barrier()
                for g in range(4):
                    tr_unit("A", [((2 * c + m) * 128, L["mk"][:, m, (2 * g + c) * 128:(2 * g + c + 1) * 128])
                                  for c in range(2) for m in range(2)])
                barrier()
                qT, mkT, mv, qz = L["qxT"], L["mkT"], L["mv"], L["qzx"]
                KTs = [L["mkK"], L["mkT"]]

                def xp_scores(i, s):
                    for h in range(H):
                        for c in range(2):
                            ins = mm(s[:, h * 256:h * 256 + 256], qT[:, 2 * h + c, i * 128:i * 128 + 128],
                                     mkT[:, 2 * h + c, :], start=c == 0, stop=c == 1)
                    return ins

                def xp_units(i, p):
                    return [("A", [((2 * e + m) * 128, p[:, (4 * g + 2 * e + m) * 128:(4 * g + 2 * e + m + 1) * 128])
                                   for e in range(2) for m in range(2)]) for g in range(2)]

                def xp_values(i, s):
                    for h in range(H):
                        for dc in range(2):
                            for m in range(2):
                                ins = mm(s[:, (2 * h + dc) * 128:(2 * h + dc + 1) * 128],
                                         mv[:, m, (2 * h + dc) * 128:(2 * h + dc + 1) * 128], PT[:, 2 * h + m, :],
                                         start=m == 0, stop=m == 1)
                    return ins

                attend(list(range(4)), None, xp_scores, xp_units, xp_values)

                def xs_prep(b):
                    k = cache().rearrange("p (m d) -> p m d", m=2)
                    for g in range(4):
                        tr_unit("A" if g % 2 else "D",
                                [((2 * c + m) * 128, k[:, m, (2 * g + c) * 128:(2 * g + c + 1) * 128])
                                 for c in range(2) for m in range(2)])
                    pe.drain().then_inc(c_free, 1)

                def xs_scores(j, s):
                    xs_prep(0)
                    for b in range(NB):
                        done = len(tj.who)
                        if b + 1 < NB:
                            xs_prep(b + 1)
                        wait_tr(done)
                        for h in range(H):
                            for c in range(2):
                                ins = mm(s[64 * (h % 2):64 * (h % 2) + 64, 512 * (h // 2):512 * (h // 2) + 256],
                                         qz[:, 2 * h + c, b * 64:b * 64 + 64], KTs[b % 2][:, 2 * h + c, :],
                                         start=b == 0 and c == 0, stop=b == NB - 1 and c == 1, skip_group_check=True)
                    return ins

                def xs_units(j, p):
                    return [("A", [((2 * g + m) * 128, p[:, (2 * g + m) * 128:(2 * g + m + 1) * 128])
                                   for g in range(2) for m in range(2)])]

                def xs_values(j, s):
                    for b in range(NB):
                        v = cache().rearrange("p (m d) -> p m d", m=2)
                        for h in range(H):
                            for dc in range(2):
                                for m in range(2):
                                    ins = mm(s[:, (2 * h + dc) * 64 + 8 * b:(2 * h + dc) * 64 + 8 * b + 8],
                                             v[:, m, (2 * h + dc) * 128:(2 * h + dc + 1) * 128],
                                             PT[:, 2 * (h // 2) + m, 64 * (h % 2) + 8 * b:64 * (h % 2) + 8 * b + 8],
                                             start=m == 0, stop=m == 1)
                        if b < NB - 1:
                            ins.then_inc(c_free, 1)
                    S["release"] = 1
                    return ins

                attend([0], None, xs_scores, xs_units, xs_values)
                barrier()
                project(f"xo{l}", oT, COLS, "D")
                barrier()

                norm_transposes(COLS)
                pe.wait_ge(rows_in, ROWS[f"ffn{l}"])
                for c in range(0, FC, 4):
                    t = open_tr("D")
                    for e in range(min(4, FC - c)):
                        ins = tp(t[:, e * 20:e * 20 + 20], L["frow"][0:20, (c + e) * 128:(c + e + 1) * 128], ident[0:20, 0:20])
                    ins.then_inc(tr_done, 1)
                barrier()
                project(f"up{l}", hT, COLS, "D", feature=True)
                barrier()
                project(f"down{l}", L["act"], COLS, "D")
                wait_projections()
                for c in range(0, FC, 4):
                    tr_unit2("A", c)
                barrier()

            def tr_unit2(who, c):
                t = open_tr(who)
                for e in range(min(4, FC - c)):
                    ins = tp(t[0:18, e * 128:e * 128 + 128], L["cstate"][:, c + e, :], ident)
                ins.then_inc(tr_done, 1)

            cross_and_ffn(0)

            norm_transposes(COLS)
            barrier()
            project("c_idx", hT, COLS, "A")
            barrier()
            iT, ikT = L["iqT"], L["ikT"]
            for i, (c0, rows) in enumerate(COLS):
                for g in range(2):
                    tr_unit("A" if g else "D", [(e * 128, L["i_tm"][0:rows, i, (4 * g + e) * 64:(4 * g + e + 1) * 64])
                                                for e in range(4)])
            for i, (c0, rows) in enumerate(COLS):
                tr_unit("D", [(0, L["i_tm"][0:rows, i, 512:576])])
            tr_unit("D", [(0, L["i_tm"][0:64, 4, 576:584])])
            barrier()
            u = open_bank("D")
            mm(bank(u)[0:64, 0:64], const("heads", 8), L["iwT"][0:8, :], start=True, stop=True).then_inc(proj_done, 1)
            for i in range(1, 4):
                n = (i + 1) * 128
                for h in range(8):
                    u = open_bank("A")
                    mm(bank(u)[:, 0:n], iT[0:64, h, i * 128:i * 128 + 128], ikT[0:64, 0:n], start=True, stop=True)\
                        .then_inc(proj_done, 1)
            barrier()

            def ik_prep(b):
                k = cache()[:, 0:512].rearrange("p (g d) -> p g d", g=8)
                for g in range(2):
                    tr_unit("A" if g else "D", [(c * 128, k[:, 4 * g + c, :]) for c in range(4)])
                pe.drain().then_inc(c_free, 1)

            ik_prep(0)
            for b in range(NB):
                done = len(tj.who)
                wait_tr(done)
                if b > 0:
                    pe.wait_ge(handoff["relu_done"], b)
                s = sreg(0)
                q = L["iqs"][0:64, b, :]
                for c in range(2):
                    mm(s[0:64, 512 * c:512 * c + 512], q, L["IKT"][0:64, b % 2, 512 * c:512 * c + 512], start=True, stop=True)
                mm(s[0:64, 1024:1088], q, ikT[0:64, SEQ:TOK], start=True, stop=True).then_inc(handoff["isc_done"], 1)
                if b + 1 < NB:
                    ik_prep(b + 1)
                pe.wait_ge(handoff["relu_done"], b + 1)
                if b == 0:
                    pe.wait_ge(handoff["wz_ready"], 1)
                t = sreg(1)
                for c, (a, z) in enumerate(((0, 512), (512, 1024), (1024, 1088))):
                    ins = mm(t[0:64, a:z], L["wz"][0:64, b * 64:b * 64 + 64], L["relu"][0:64, b % 2, a:z],
                             start=b == 0, stop=b == NB - 1, skip_group_check=True)
                ins.then_inc(handoff["relu_used"], 1)
            barrier()
            barrier()
            project("c_qkv", hT, COLS, "A")
            barrier()
            for i, (c0, rows) in enumerate(COLS):
                for g in range(2):
                    tr_unit("D" if g else "A", [(e * 128, L["c_tm"][0:rows, i, (4 * g + e) * 128:(4 * g + e + 1) * 128])
                                                for e in range(4)])
                tr_unit("D", [(e * 128, L["c_tm"][0:rows, i, 1024 + e * 128:1152 + e * 128]) for e in range(2)])
            barrier()
            qT, kT, KT, v_tm = L["qT_c"], L["kT_c"], L["KT_c"], L["v_c"]
            jobs = JOBS_CP

            def cp_scores(j, s):
                i, hp = jobs[j]
                n = (i + 1) * 128
                for e in range(2):
                    h = 2 * hp + e
                    mm(s[:, 512 * e:512 * e + n], qT[:, h, i * 128:i * 128 + 128], kT[:, h // 4, 0:n], start=True, stop=False,
                       skip_group_check=True)
                    if i == 0:
                        ins = mm(s[:, 512 * e:512 * e + n], identb[:, :], causalb[:, :], start=False, stop=True, skip_group_check=True)
                    else:
                        ins = mm(s[:, 512 * e:512 * e + n], identb[:, :], L["selp"][i - 1], start=False, stop=True,
                                 skip_group_check=True)
                return ins

            def cp_units(j, p):
                i, hp = jobs[j]
                return [("A", [(c * 128, p[:, e * 512 + c * 128:e * 512 + c * 128 + 128]) for c in range(i + 1)]) for e in range(2)]

            def cp_values(j, s):
                i, hp = jobs[j]
                for e in range(2):
                    g = (2 * hp + e) // 4
                    for c in range(i + 1):
                        ins = mm(s[:, e * 128:e * 128 + 128], v_tm[:, c, g * 128:g * 128 + 128], PT[:, 4 * e + c, :],
                                 start=c == 0, stop=c == i)
                return ins

            attend(jobs, None, cp_scores, cp_units, cp_values)

            def cs_prep(p):
                for bb in range(2):
                    k = cache().rearrange("p (n g d) -> p n g d", n=8, g=2)
                    for g in range(2):
                        for half in range(2):
                            tr_unit("A" if half else "D", [(c * 128, k[:, 4 * half + c, g, :]) for c in range(4)])
                    pe.drain().then_inc(c_free, 1)
                wait_tr()

            def cs_scores(p, s):
                ex = L["expb"][0:64, p * 128:p * 128 + 128]
                for a, z in ((0, 512), (512, 1024), (1024, 1088)):
                    mm(s[:, a:z], ex, L["sels"][0:64, a:z], start=True, stop=False, skip_group_check=True)
                for bb in range(2):
                    b = 2 * p + bb
                    for g in range(2):
                        r = 2 * bb + g
                        q = L["qs_c"][:, b, g, :]
                        o = slice(32 * r, 32 * r + 32)
                        for c in range(2):
                            mm(s[o, 512 * c:512 * c + 512], q, KT[:, r, 512 * c:512 * c + 512], start=False, stop=True,
                               skip_group_check=True)
                        ins = mm(s[o, 1024:1088], q, kT[:, g, SEQ:TOK], start=False, stop=True, skip_group_check=True)
                return ins

            def cs_values(p, s):
                for bb in range(2):
                    v = cache().rearrange("p (n g d) -> p n g d", n=8, g=2)
                    for g in range(2):
                        r = 2 * bb + g
                        o = s[:, 32 * r:32 * r + 32]
                        for c in range(NPAGE):
                            mm(o, v[:, c, g, :], PT[:, c, 32 * r:32 * r + 32], start=c == 0, stop=False)
                        ins = mm(o, v_tm[0:64, 4, g * 128:g * 128 + 128], PT[0:64, 8, 32 * r:32 * r + 32], start=False, stop=True)
                    if bb == 0:
                        ins.then_inc(c_free, 1)
                S["release"] = 1
                return ins

            attend(list(range(NB // 2)), cs_prep, cs_scores, past_units, cs_values)
            barrier()
            project("c_out", oT, COLS, "D")
            barrier()
            cross_and_ffn(1)

        @block.scalar
        def _(act):
            S = {"phase": 0, "job": 0, "stores": 0, "roots": 0, "rows": 0, "means": 0, "rstds": 0}
            pj, tj = Turns(), Turns()
            step = Chain(act, act_step)
            fn = nc.scalar.activation

            def barrier():
                if S["stores"]:
                    act.wait_ge(stores, 16 * S["stores"])
                S["phase"] += 1
                act.drain().then_inc(phase["act"], 1)
                for e in ("pe", "dve"):
                    act.wait_ge(phase[e], S["phase"])

            def store(dst, src):
                S["stores"] += 1
                act.dma_start(dst, src).then_inc(stores, 16)

            def load(dst, src):
                act.dma_start(dst, src).then_inc(rows_in, 16)

            def banks(who, count):
                for _ in range(count):
                    n = pj.add(who)
                    if who == "A":
                        act.wait_ge(proj_done, n + 1)
                        yield bank(n)
                    else:
                        yield None

            def tr(who):
                n = tj.add(who)
                if who != "A":
                    return None
                act.wait_ge(tr_done, n + 1)
                return tbank(n)

            def tr_copy(who, out, rows=128, view=None):
                t = tr(who)
                if t is not None:
                    fn(out, t if view is None else view(t), ACT.Copy).then_inc(tr_act, 1)

            def copy_bank(n, out, b):
                fn(out, b, ACT.Copy).then_inc(proj_act, 1)

            def norm(src, tiles):
                for i, (c0, rows) in enumerate(tiles):
                    ins = fn(junk[0:rows, :], src[0:rows, i, :], ACT.Square, accum_out=ss[0:rows, i:i + 1])
                    if i < len(tiles) - 1:
                        step(ins)
                    else:
                        ins.then_inc(squares, 1)
                S["means"] += 1
                act.wait_ge(means, S["means"])
                fn(sd, ms, ACT.Sqrt).then_inc(roots, 1)
                act.wait_ge(rstds, S["means"])

            def normalise(src, tiles):
                norm(src, tiles)
                for i, (c0, rows) in enumerate(tiles):
                    if i >= 2:
                        act.wait_ge(tr_done, len(tj.who) - 2)
                    fn(xn[i % 2][0:rows, :], src[0:rows, i, :], ACT.Copy, scale=rstd[0:rows, i:i + 1]).then_inc(xn_done, 1)
                    tr("D"), tr("D")

            def copies(who, tiles, dst):
                for b, (a, z) in enumerate(dst):
                    for i, (c0, rows) in enumerate(tiles):
                        for v in banks(who, 1):
                            if v is not None:
                                fn(a(i)[0:rows], v[0:rows, 0:z], ACT.Copy).then_inc(proj_act, 1)

            def attend(count, exps, outs, prep=None):
                def start(j):
                    n = S["job"] + j
                    if prep:
                        prep(j)
                    act.wait_ge(rowmax_ready, n + 1)
                    exps(j, n, sreg(n), P[n % 2]).then_inc(exp_done, 1)

                start(0)
                for j in range(count):
                    if j + 1 < count:
                        start(j + 1)
                    outs(j)
                S["job"] += count

            act.dma_start(cst[:, :], A["consts"]).then_inc(first_in, 16)
            act.dma_start(L["lev_in"], A["levels"]).then_inc(first_in, 16)
            for r, name in ((0, "norm_mix"), (2, "norm_x"), (4, "norm_mem"), (6, "norm_ffn")):
                act.dma_start(L["grow"][r:r + 2, :], A[name]).then_inc(first_in, 16)
            act.dma_start(L["srow"][0:1, :], A["diff_subln"]).then_inc(first_in, 16)
            act.dma_start(L["srow"][1:2, :], A["hgrn_onorm"]).then_inc(first_in, 16)
            act.dma_start(L["srow"][2:10, :], A["hgrn_lb_logits"].rearrange("l (h k) -> (l h) k", h=H)).then_inc(first_in, 16)
            for i, name in enumerate(("diff_lq1", "diff_lk1", "diff_lq2", "diff_lk2")):
                act.dma_start(L["lrow"][:, i, :], A[name].to_broadcast([128, 64])).then_inc(first_in, 16)
            act.dma_start(x[:, 0:4, :], A["x_prompt"][0].rearrange("(i p) d -> p i d", p=128)).then_inc(first_in, 16)
            act.dma_start(x[0:64, 4, :], A["x_sample"].rearrange("b t d -> (b t) d")).then_inc(first_in, 16)
            act.wait_ge(first_in, FIRST)
            tr("D"), tr("D")
            act.wait_ge(handoff["lam_in"], 1)
            fn(L["le"][:, 0:2], L["ls"][:, 0:2], ACT.Exp).then_inc(handoff["lam_e"], 1)
            act.wait_ge(handoff["lam_in"], 2)
            fn(L["lbe"][:, 0:8], L["lbd"][:, 0:8], ACT.Exp).then_inc(handoff["lam_e"], 1)
            barrier()

            normalise(x, COLS)
            barrier()
            copies("A", COLS, [((lambda i, b=b: L["a_qk"][:, i, 512 * b:512 * b + 512]), 512) for b in range(2)]
                   + [((lambda i: L["a_v"][:, i, :]), 512)])
            barrier()
            for i, (c0, rows) in enumerate(COLS):
                tr("D")
                tr_copy("A", L["kT_a"][:, :, c0:c0 + rows], view=lambda t: t.rearrange("p (h t) -> p h t", h=H)[:, :, 0:rows])
            store(O["diff_k_p"].rearrange("(i p) h d -> p i (h d)", p=128), L["a_qk"][:, 0:4, 512:1024])
            store(O["diff_v_p"].rearrange("(i p) h d -> p i (h d)", p=128), L["a_v"][:, 0:4, :])
            store(O["diff_k_s"].rearrange("b t h d -> (b t) (h d)"), L["a_qk"][0:64, 4, 512:1024])
            store(O["diff_v_s"].rearrange("b t h d -> (b t) (h d)"), L["a_v"][0:64, 4, :])
            barrier()

            def two_exps(scale, width):
                def run(j, n, s, p):
                    m = width(j)
                    for e in range(2):
                        ins = fn(p[:, 512 * e:512 * e + m], s[:, 512 * e:512 * e + m], ACT.Exp, bias=nm2[n % 2][:, e:e + 1],
                                 scale=scale, accum_out=sm2[n % 2][:, e:e + 1])
                    return ins
                return run

            def ap_outs(j):
                i, h = JOBS_AP[j]
                tr_copy("A", PT[:, 0:i + 1, :], view=lambda t: t[:, 0:(i + 1) * 128].rearrange("p (c q) -> p c q", c=i + 1))

            attend(16, two_exps(64 ** -0.5, lambda j: (JOBS_AP[j][0] + 1) * 128), ap_outs)

            def as_prep(b):
                for half in range(2):
                    for h in range(H):
                        tr_copy("A" if h % 2 else "D", L["KT_a"][:, h, half * 512:half * 512 + 512])

            def one_exp(scale):
                return lambda j, n, s, p: fn(p[:, 0:1088], s[:, 0:1088], ACT.Exp, bias=nm2[n % 2][:, 0:1], scale=scale,
                                             accum_out=sm2[n % 2][:, 0:1])

            def past_outs(j):
                tr("D")
                tr_copy("A", PT[:, 4:8, :], view=lambda t: t.rearrange("p (c q) -> p c q", c=4))
                tr("D")

            attend(NB, one_exp(64 ** -0.5), past_outs, as_prep)
            barrier()
            HQ, HK = L["HQ"], L["HK"]
            for dst, f in ((HQ, ACT.Silu), (HK, ACT.Sigmoid), (oT[:, 4:8, :], ACT.Silu)):
                vs = []
                for c in range(4):
                    for v in banks("A", 1):
                        fn(dst[:, c, 0:SEQ], v, f).then_inc(proj_act, 1)
                for v in banks("A", 1):
                    fn(dst[:, :, SEQ:TOK], v[:, 0:256].rearrange("p (c t) -> p c t", c=4), f).then_inc(proj_act, 1)
            copies("A", COLS, [((lambda i: L["ib"][:, i, :]), 512)])
            barrier()
            for g in range(8):
                load(L["S0"][:, g], A["state_hgrn"][0, g].rearrange("h k v -> k h v"))
            act.wait_ge(handoff["f_ready"], 1)
            fn(L["QK"], L["B"], ACT.Ln).then_inc(handoff["logf"], 1)
            for n, h in enumerate(LEVELS):
                if h:
                    act.wait_ge(handoff["decay_d"], n)
                    e = L["QK"] if h <= 4 else L["QK"][:, :, 0:SEQ]
                    fn(e, e, ACT.Exp).then_inc(handoff["decay_e"], 1)
                for i in range(5 if h <= 4 else 4):
                    pj.add("D")
            barrier()
            act.wait_ge(handoff["decay_d"], len(LEVELS))
            fn(L["QK"], L["QK"], ACT.Exp).then_inc(handoff["decay_e"], 1)
            for i, (c0, rows) in enumerate(COLS):
                tr_copy("A", L["KD"][0:rows, i, :, :], view=lambda t: t[0:rows].rearrange("p (h k) -> p h k", h=H))
            barrier()
            for i in range(4):
                pj.add("D")
            fn(L["QK"], L["B"], ACT.Exp).then_inc(handoff["decay_e"], 1)
            barrier()
            for i in range(4):
                for v in banks("A", 1):
                    fn(L["OB"][:, :, i * 128:i * 128 + 128], v.rearrange("p (h t) -> p h t", h=H), ACT.Copy).then_inc(proj_act, 1)
            for v in banks("A", 1):
                fn(L["OB"][:, :, SEQ:TOK], v[:, 0:256].rearrange("p (h t) -> p h t", h=H), ACT.Copy).then_inc(proj_act, 1)
            for i in range(8):
                pj.add("D")
            barrier()
            store(O["hgrn_p"].rearrange("h k v -> k h v"), L["SS"][:, 3, :, :])
            for g in range(8):
                store(O["hgrn_s"][g].rearrange("h k v -> k h v"), L["S0"][:, g])
            for c in range(KC):
                src = oT[:, c, :] if c < 4 else L["OB"][:, c - 4, :]
                if c >= 2:
                    act.wait_ge(handoff["onorm_mean"], c - 1)
                fn(L["sq"][:, c % 2, :], src, ACT.Square).then_inc(handoff["sq_done"], 1)
                act.wait_ge(handoff["onorm_mean"], c + 1)
                if c >= 2:
                    act.wait_ge(handoff["onorm_done"], c - 1)
                fn(L["rt"][:, c % 2, :], sreg(c)[:, 0:TOK], ACT.Sqrt, bias=eps_col).then_inc(handoff["onorm_root"], 1)
            barrier()
            for b in range(2):
                for i in range(NTILE):
                    pj.add("D")
            barrier()

            def cross_and_ffn(l):
                load(L["mem"], A["mem_prompt"][0].rearrange("(m p) d -> p m d", p=128))
                normalise(x, COLS)
                barrier()
                for g in range(2):
                    for c in range(4):
                        for v in banks("A", 1):
                            fn(L["qxT"][:, 4 * g + c, 0:SEQ], v, ACT.Copy).then_inc(proj_act, 1)
                    for v in banks("A", 1):
                        fn(L["qxT"][:, 4 * g:4 * g + 4, SEQ:TOK], v[:, 0:256].rearrange("p (c t) -> p c t", c=4),
                           ACT.Copy).then_inc(proj_act, 1)
                act.wait_ge(rows_in, ROWS[f"mem{l}"])
                normalise(L["mem"], COLS[0:2])
                barrier()
                for dst in (L["mk"], L["mv"]):
                    copies("A", COLS[0:2], [((lambda i, b=b: dst[:, i, 512 * b:512 * b + 512]), 512) for b in range(2)])
                barrier()
                store(O["mem_k"][l].rearrange("(m p) h d -> p m (h d)", p=128), L["mk"])
                store(O["mem_v"][l].rearrange("(m p) h d -> p m (h d)", p=128), L["mv"])
                for g in range(4):
                    tr_copy("A", L["mkT"][:, 2 * g:2 * g + 2, :], view=lambda t: t.rearrange("p (c m) -> p c m", c=2))
                barrier()

                def xp_exps(j, n, s, p):
                    for h in range(H):
                        ins = fn(p[:, h * 256:h * 256 + 256], s[:, h * 256:h * 256 + 256], ACT.Exp, bias=nm2[n % 2][:, h:h + 1],
                                 scale=256 ** -0.5, accum_out=sm2[n % 2][:, h:h + 1])
                    return ins

                def xp_outs(j):
                    for g in range(2):
                        tr_copy("A", PT[:, 4 * g:4 * g + 4, :], view=lambda t: t.rearrange("p (c q) -> p c q", c=4))

                attend(4, xp_exps, xp_outs)

                def xs_prep(j):
                    for b in range(NB):
                        for g in range(4):
                            tr_copy("A" if g % 2 else "D", [L["mkK"], L["mkT"]][b % 2][:, 2 * g:2 * g + 2, :],
                                    view=lambda t: t.rearrange("p (c m) -> p c m", c=2))

                def xs_exps(j, n, s, p):
                    for e in range(2):
                        ins = fn(p[:, e * 256:e * 256 + 256], s[:, e * 512:e * 512 + 256], ACT.Exp, bias=nm2[n % 2][:, e:e + 1],
                                 scale=256 ** -0.5, accum_out=sm2[n % 2][:, e:e + 1])
                    return ins

                def xs_outs(j):
                    tr_copy("A", PT[:, 0:4, :], view=lambda t: t.rearrange("p (c q) -> p c q", c=4))

                attend(1, xs_exps, xs_outs, xs_prep)
                barrier()
                for b in range(2 * NTILE):
                    pj.add("D")
                barrier()

                load(L["frow"][0:16, :], A["state_ffn_conv"][l].rearrange("b w f -> (b w) f"))
                load(L["frow"][16:19, :], A["conv_ffn_w"][l])
                load(L["frow"][19:20, :], A["conv_ffn_b"][l:l + 1])
                normalise(x, COLS)
                for c in range(0, FC, 4):
                    tr("D")
                barrier()
                for j in range(FC // 2):
                    for e in range(5):
                        pj.add("D")
                    for e in range(2):
                        n = 2 * j + e
                        S["silu"] = S.get("silu", 0) + 1
                        act.wait_ge(handoff["gate_done"], S["silu"])
                        if S["silu"] > 2:
                            act.wait_ge(handoff["u_used"], S["silu"] - 2)
                        fn(L["sil"][:, n % 2, :], L["gc"][:, n % 2, :], ACT.Silu).then_inc(handoff["silu_done"], 1)
                barrier()
                for b in range(2 * NTILE):
                    pj.add("D")
                for c in range(0, FC, 4):
                    m = min(4, FC - c)
                    tr_copy("A", L["frow"][0:18, c * 128:(c + m) * 128], view=lambda t: t[0:18, 0:m * 128])
                barrier()
                store(O["conv_p"][l], L["frow"][0:2, :])
                store(O["conv_s"][l].rearrange("b w f -> (b w) f"), L["frow"][2:18, :])

            cross_and_ffn(0)

            normalise(x, COLS)
            load(L["ikn"], A["idx_k_norm"].to_broadcast([128, 64]))
            barrier()
            copies("A", COLS, [((lambda i: L["i_tm"][:, i, 0:512]), 512), ((lambda i: L["i_tm"][:, i, 512:584]), 72)])
            act.wait_ge(proj_act, pj.count("A", len(pj.who)))
            for i, (c0, rows) in enumerate(COLS):
                ins = fn(L["ikj"][0:rows, :], L["i_tm"][0:rows, i, 512:576], ACT.Square, accum_out=ss[0:rows, i:i + 1])
                if i < NTILE - 1:
                    step(ins)
                else:
                    ins.then_inc(squares, 1)
            S["means"] += 1
            act.wait_ge(means, S["means"])
            fn(sd, ms, ACT.Sqrt).then_inc(roots, 1)
            barrier()
            for i, (c0, rows) in enumerate(COLS):
                tr("D")
                tr_copy("A", L["iqT"][0:64, 4:8, c0:c0 + rows],
                        view=lambda t: t[0:64].rearrange("p (h t) -> p h t", h=4)[:, :, 0:rows])
            for i in range(6):
                tr("D")
            store(O["dsa_ik_p"].rearrange("(i p) d -> p i d", p=128), L["i_tm"][:, 0:4, 512:576])
            store(O["dsa_ik_s"].rearrange("b t d -> (b t) d"), L["i_tm"][0:64, 4, 512:576])
            barrier()
            pj.add("D")
            k = 0
            for i in range(1, 4):
                n = (i + 1) * 128
                for h in range(8):
                    for v in banks("A", 1):
                        if k >= 2:
                            act.wait_ge(handoff["relu_used"], k - 1)
                        fn(L["relup"][:, k % 2, 0:n], v[:, 0:n], ACT.Relu).then_inc(proj_act, 1)
                    k += 1
            barrier()
            for b in range(NB):
                if b == 0:
                    tr("D")
                    tr_copy("A", L["IKT"][0:64, 0, 512:1024], view=lambda t: t[0:64])
                act.wait_ge(handoff["isc_done"], b + 1)
                if b >= 2:
                    act.wait_ge(handoff["relu_used"], 24 + b - 1)
                fn(L["relu"][0:64, b % 2, :], sreg(0)[0:64, 0:1088], ACT.Relu).then_inc(handoff["relu_done"], 1)
                if b + 1 < NB:
                    tr("D")
                    tr_copy("A", L["IKT"][0:64, (b + 1) % 2, 512:1024], view=lambda t: t[0:64])
            barrier()
            barrier()
            copies("A", COLS, [((lambda i, b=b: L["c_tm"][:, i, 512 * b:512 * b + 512]), 512) for b in range(2)])
            for i, (c0, rows) in enumerate(COLS):
                for v in banks("A", 1):
                    step(fn(L["c_tm"][0:rows, i, 1024:1280], v[0:rows, 0:256], ACT.Copy))
                    fn(L["v_c"][0:rows, i, :], v[0:rows, 256:512], ACT.Copy).then_inc(proj_act, 1)
            barrier()
            for i, (c0, rows) in enumerate(COLS):
                tr_copy("A", L["qT_c"][:, 0:4, c0:c0 + rows], view=lambda t: t.rearrange("p (h t) -> p h t", h=4)[:, :, 0:rows])
                tr("D")
                tr("D")
            store(O["dsa_k_p"].rearrange("(i p) h d -> p i (h d)", p=128), L["c_tm"][:, 0:4, 1024:1280])
            store(O["dsa_v_p"].rearrange("(i p) h d -> p i (h d)", p=128), L["v_c"][:, 0:4, :])
            store(O["dsa_k_s"].rearrange("b t h d -> (b t) (h d)"), L["c_tm"][0:64, 4, 1024:1280])
            store(O["dsa_v_s"].rearrange("b t h d -> (b t) (h d)"), L["v_c"][0:64, 4, :])
            barrier()

            def cp_outs(j):
                i, hp = JOBS_CP[j]
                for e in range(2):
                    tr_copy("A", PT[:, 4 * e:4 * e + i + 1, :],
                            view=lambda t: t[:, 0:(i + 1) * 128].rearrange("p (c q) -> p c q", c=i + 1))

            attend(16, two_exps(128 ** -0.5, lambda j: (JOBS_CP[j][0] + 1) * 128), cp_outs)

            def cs_prep(p):
                for bb in range(2):
                    for g in range(2):
                        tr("D")
                        tr_copy("A", L["KT_c"][:, 2 * bb + g, 512:1024])

            attend(NB // 2, one_exp(128 ** -0.5), past_outs, cs_prep)
            barrier()
            for b in range(2 * NTILE):
                pj.add("D")
            barrier()
            cross_and_ffn(1)
            load(L["fin"], A["norm_final"].unsqueeze(0).to_broadcast([128, D]))
            norm(x, COLS)
            act.wait_ge(handoff["onorm_done"], KC + 1)
            store(O["y_p"].rearrange("(i p) d -> p i d", p=128), x[:, 0:4, :])
            store(O["y_s"].rearrange("b t d -> (b t) d"), x[0:64, 4, :])
            act.wait_ge(stores, 16 * S["stores"])

        @block.vector
        def _(dve):
            S = {"phase": 0, "job": 0, "norms": 0, "silu": 0}
            pj, tj = Turns(), Turns()
            step = Chain(dve, dve_step)
            v_ = nc.vector

            def barrier():
                S["phase"] += 1
                dve.drain().then_inc(phase["dve"], 1)
                for e in ("pe", "act"):
                    dve.wait_ge(phase[e], S["phase"])

            def banks(who, count):
                for _ in range(count):
                    n = pj.add(who)
                    if who == "D":
                        dve.wait_ge(proj_done, n + 1)
                        yield bank(n)
                    else:
                        yield None

            def tr(who):
                n = tj.add(who)
                if who != "D":
                    return None
                dve.wait_ge(tr_done, n + 1)
                return tbank(n)

            def tr_copy(who, out, view=None):
                t = tr(who)
                if t is not None:
                    v_.tensor_copy(out, t if view is None else view(t)).then_inc(tr_dve, 1)

            def norm(width=D):
                S["norms"] += 1
                dve.wait_ge(squares, S["norms"])
                v_.tensor_scalar(ms, ss, 1.0 / width, EPS, ALU.mult, ALU.add).then_inc(means, 1)
                dve.wait_ge(roots, S["norms"])
                v_.reciprocal(rstd, sd).then_inc(rstds, 1)

            def normalise(tiles, g, dst):
                norm()
                for i, (c0, rows) in enumerate(tiles):
                    for e in range(2):
                        t = tr("D").rearrange("p (c t) -> p c t", c=4)[:, :, 0:rows]
                        gain = gains[:, 4 * e:4 * e + 4, g:g + 1].to_broadcast([128, 4, rows])
                        v_.tensor_tensor(dst[:, 4 * e:4 * e + 4, c0:c0 + rows], t, gain, ALU.mult).then_inc(tr_dve, 1)

            def add_to_x():
                for b in range(2):
                    for i, (c0, rows) in enumerate(COLS):
                        for v in banks("D", 1):
                            xs = x[0:rows, i, 512 * b:512 * b + 512]
                            v_.tensor_tensor(xs, xs, v[0:rows, :], ALU.add).then_inc(proj_dve, 1)

            def rotate(t, table, half, heads, tmp="ropet"):
                rows = t.shape[0]
                a = L[tmp][0:rows, 0, 0:heads * 2 * half].rearrange("p (h d) -> p h d", h=heads)
                b = L[tmp][0:rows, 1, 0:heads * 2 * half].rearrange("p (h d) -> p h d", h=heads)
                bc = lambda s, lo, hi: table[:, s, lo:hi].unsqueeze(1).to_broadcast([rows, heads, hi - lo])
                v_.tensor_tensor(a, t[:, :, 0:2 * half], bc(0, 0, 2 * half), ALU.mult)
                v_.tensor_tensor(b[:, :, 0:half], t[:, :, half:2 * half], bc(1, 0, half), ALU.mult)
                step(v_.tensor_tensor(b[:, :, half:2 * half], t[:, :, 0:half], bc(1, half, 2 * half), ALU.mult))
                step(v_.tensor_tensor(t[:, :, 0:2 * half], a, b, ALU.add))

            def attend(count, rowmax, normal, outs, copy, prep=None):
                def start(j):
                    n = S["job"] + j
                    if prep:
                        prep(j)
                    dve.wait_ge(scores_ready, n + 1)
                    rowmax(j, n, sreg(n))

                start(0)
                for j in range(count):
                    n = S["job"] + j
                    dve.wait_ge(exp_done, n + 1)
                    normal(j, n, P[n % 2])
                    if j + 1 < count:
                        start(j + 1)
                    outs(j)
                    dve.wait_ge(out_ready, n + 1)
                    copy(j, sreg(n))
                S["job"] += count

            def biased(n, out, in_, scale, k):
                step(v_.tensor_reduce(out=mx2[n % 2][:, 0:k], in_=in_, axis=AX.X, op=ALU.max))
                v_.tensor_scalar(nm2[n % 2][:, 0:k], mx2[n % 2][:, 0:k], -scale, None, ALU.mult).then_inc(rowmax_ready, 1)

            def two_max(scale, width):
                def run(j, n, s):
                    biased(n, None, s[:, 0:1024].rearrange("p (e s) -> p e s", e=2)[:, :, 0:width(j)], scale, 2)
                return run

            def one_max(scale):
                return lambda j, n, s: biased(n, None, s[:, 0:1088], scale, 1)

            dve.wait_ge(first_in, FIRST)
            v_.memset(misc[:, :], EPS)
            step(v_.memset(stat[:, :], 1.0))
            v_.tensor_copy(lev[:, :], L["lev_in"])
            v_.tensor_copy(identb[:, :], ident)
            v_.tensor_copy(causalb[:, :], const("causal"))
            v_.tensor_copy(newmaskb[:, :], const("newmask"))
            tr_copy("D", gains[:, :, :], view=lambda t: t[:, 0:64].rearrange("p (c g) -> p c g", c=8))
            t = tr("D")
            v_.tensor_copy(small[:, :], t[:, 0:10]).then_inc(tr_dve, 1)
            lr = L["lrow"]
            step(v_.tensor_tensor(L["lp"], lr[:, 0:4:2, :], lr[:, 1:4:2, :], ALU.mult))
            v_.tensor_reduce(out=L["ls"][:, 0:2], in_=L["lp"], axis=AX.X, op=ALU.add).then_inc(handoff["lam_in"], 1)
            dve.wait_ge(handoff["lam_e"], 1)
            step(v_.tensor_tensor(L["ld"], L["le"][:, 0:1], L["le"][:, 1:2], ALU.subtract))
            step(v_.tensor_scalar(lam, L["ld"], LAM_INIT, None, ALU.add))
            ms_ = const("mapsel")
            step(v_.tensor_scalar(L["ld"], ms_[:, 1:2], lam, -1.0, ALU.mult, ALU.mult))
            step(v_.tensor_tensor(sgn, L["ld"], ms_[:, 0:1], ALU.add))
            dve.wait_ge(tr_dve, 2)
            v_.tensor_scalar(subg, small[:, 0:1], 1.0 - LAM_INIT, None, ALU.mult)
            step(v_.tensor_tensor(L["lbm"], small[:, 2:6], small[:, 6:10], ALU.max))
            v_.tensor_tensor(L["lbd"][:, 0:4], small[:, 2:6], L["lbm"], ALU.subtract)
            v_.tensor_tensor(L["lbd"][:, 4:8], small[:, 6:10], L["lbm"], ALU.subtract).then_inc(handoff["lam_in"], 1)
            dve.wait_ge(handoff["lam_e"], 2)
            step(v_.tensor_tensor(L["lbm"], L["lbe"][:, 0:4], L["lbe"][:, 4:8], ALU.add))
            step(v_.reciprocal(L["lbr"], L["lbm"]))
            step(v_.tensor_tensor(lb, L["lbe"][:, 0:4], L["lbr"], ALU.mult))
            step(v_.tensor_scalar(omlb, lb, -1.0, 1.0, ALU.mult, ALU.add))
            barrier()

            normalise(COLS, 0, hT)
            barrier()
            for b in range(3):
                for i, (c0, rows) in enumerate(COLS):
                    n = pj.add("A")
                    if b == 1:
                        dve.wait_ge(proj_act, pj.count("A", n + 1))
                        rotate(L["a_qk"][0:rows, i, :].rearrange("p (h d) -> p h d", h=16), rope8[0:rows, i], 8, 16)
            barrier()
            for i, (c0, rows) in enumerate(COLS):
                tr_copy("D", L["qT_a"][:, :, c0:c0 + rows], view=lambda t: t.rearrange("p (h t) -> p h t", h=H)[:, :, 0:rows])
                tr("A")
            step(v_.memset(L["qz_a"], 0.0))
            dve.wait_ge(tr_dve, tj.count("D", len(tj.who)))
            for m in range(2):
                r = slice(64 * m, 64 * m + 64)
                for b in range(NB):
                    v_.tensor_copy(L["qz_a"][r, b, :, 8 * m:8 * m + 8], L["qT_a"][r, :, SEQ + 8 * b:SEQ + 8 * b + 8])
            barrier()

            def ap_normal(j, n, p):
                w = (JOBS_AP[j][0] + 1) * 128
                r = rs2[n % 2]
                step(v_.reciprocal(r[:, 0:2], sm2[n % 2][:, 0:2]))
                step(v_.tensor_scalar(r[:, 2:3], r[:, 1:2], lam, -1.0, ALU.mult, ALU.mult))
                step(v_.tensor_scalar(p[:, 0:w], p[:, 0:w], r[:, 0:1], None, ALU.mult))
                v_.scalar_tensor_tensor(out=p[:, 0:w], in0=p[:, 512:512 + w], scalar=r[:, 2:3], in1=p[:, 0:w],
                                        op0=ALU.mult, op1=ALU.add).then_inc(probs_ready, 1)

            def ap_copy(j, s):
                i, h = JOBS_AP[j]
                v_.tensor_copy(oT[:, h, i * 128:i * 128 + 128], s[:, 0:128]).then_inc(out_copied, 1)

            attend(16, two_max(64 ** -0.5, lambda j: (JOBS_AP[j][0] + 1) * 128), ap_normal, lambda j: tr("A"), ap_copy)

            def as_prep(b):
                for half in range(2):
                    for h in range(H):
                        tr_copy("A" if h % 2 else "D", L["KT_a"][:, h, half * 512:half * 512 + 512])

            def as_normal(j, n, p):
                r = rs2[n % 2]
                step(v_.reciprocal(r[:, 0:1], sm2[n % 2][:, 0:1]))
                v_.tensor_scalar(p[:, 0:1088], p[:, 0:1088], r[:, 0:1], sgn, ALU.mult, ALU.mult).then_inc(probs_ready, 1)

            def past_outs(j):
                tr_copy("D", PT[:, 0:4, :], view=lambda t: t.rearrange("p (c q) -> p c q", c=4))
                tr("A")
                t = tr("D")
                v_.tensor_copy(PT[0:64, 8, :], t[0:64, 0:128]).then_inc(tr_dve, 1)

            def as_copy(b, s):
                o = s[:, 0:64].rearrange("p (h m q) -> p h q m", h=H, m=2)
                v_.tensor_reduce(out=oT[:, 0:H, SEQ + 8 * b:SEQ + 8 * b + 8], in_=o, axis=AX.X, op=ALU.add).then_inc(out_copied, 1)

            attend(NB, one_max(64 ** -0.5), as_normal, past_outs, as_copy, as_prep)
            barrier()
            for i in range(20):
                pj.add("A")
            barrier()
            HQ, HK, QK, B, ATT, SS = (L[k] for k in ("HQ", "HK", "QK", "B", "ATT", "SS"))
            for e in range(H):
                ins = v_.tensor_scalar(HK[:, e, :], HK[:, e, :], omlb[:, e:e + 1], lb[:, e:e + 1], ALU.mult, ALU.add)
            step(ins)
            v_.tensor_scalar(B, HK, 1e-19, None, ALU.max).then_inc(handoff["f_ready"], 1)
            v_.tensor_scalar(HK, HK, -1.0, 1.0, ALU.mult, ALU.add)
            v_.tensor_scalar(HQ, HQ, 128 ** -0.5, None, ALU.mult).then_inc(handoff["qk_ready"], 1)
            v_.memset(ATT, 0.0)
            dve.wait_ge(handoff["logf"], 1)
            for e in range(H):
                ins = v_.tensor_tensor_scan(out=B[:, e, :], data0=const("reset"), data1=QK[:, e, :], initial=0.0,
                                            op0=ALU.mult, op1=ALU.add)
            step(ins)

            def attend_level(n, h):
                mask = levels[:, n, :]
                for i, (c0, rows) in enumerate(COLS):
                    if i == 4 and h > 4:
                        continue
                    for v in banks("D", 1):
                        m = mask[0:rows, 0:rows].unsqueeze(1).to_broadcast([rows, H, rows])
                        v_.copy_predicated(ATT[0:rows, i, :, 0:rows], m,
                                           v[0:rows].rearrange("p (h t) -> p h t", h=H)[:, :, 0:rows]).then_inc(proj_dve, 1)

            for n, h in enumerate(LEVELS):
                if h:
                    w = TOK if h <= 4 else SEQ
                    nb = w // (2 * h)
                    cut = lambda t: t[:, :, 0:w].rearrange("p e (n s) -> p e n s", s=2 * h)
                    anchor = cut(B)[:, :, :, h - 1:h].to_broadcast([128, H, nb, h])
                    dve.wait_ge(handoff["qk_used"], n)
                    if n == 1:
                        pass
                    v_.tensor_tensor(cut(QK)[:, :, :, h:2 * h], cut(B)[:, :, :, h:2 * h], anchor, ALU.subtract)
                    v_.tensor_tensor(cut(QK)[:, :, :, 0:h], anchor, cut(B)[:, :, :, 0:h], ALU.subtract)\
                        .then_inc(handoff["decay_d"], 1)
                    attend_level(n - 1, LEVELS[n - 1])
                    dve.wait_ge(handoff["decay_e"], n)
                    v_.tensor_tensor(cut(QK)[:, :, :, h:2 * h], cut(QK)[:, :, :, h:2 * h], cut(HQ)[:, :, :, h:2 * h], ALU.mult)
                    v_.tensor_tensor(cut(QK)[:, :, :, 0:h], cut(QK)[:, :, :, 0:h], cut(HK)[:, :, :, 0:h], ALU.mult)\
                        .then_inc(handoff["qk_ready"], 1)
            attend_level(len(LEVELS) - 1, LEVELS[-1])
            barrier()
            for w, n, a in ((128, 4, 0), (TS, NB, SEQ)):
                cut = lambda t: t[:, :, a:a + w * n].rearrange("p e (n s) -> p e n s", s=w)
                ins = v_.tensor_tensor(cut(QK), cut(B)[:, :, :, w - 1:w].to_broadcast([128, H, n, w]), cut(B), ALU.subtract)
            ins.then_inc(handoff["decay_d"], 1)
            dve.wait_ge(handoff["decay_e"], len(LEVELS))
            v_.tensor_tensor(QK, QK, HK, ALU.mult).then_inc(handoff["qk_ready"], 1)
            for i in range(5):
                tr("A")
            barrier()
            dve.wait_ge(handoff["decay_e"], len(LEVELS) + 1)
            for i in range(4):
                for v in banks("D", 1):
                    new = v.rearrange("p (h v) -> p h v", h=H)
                    if i == 0:
                        ins = v_.tensor_copy(SS[:, 0], new)
                        ins.then_inc(proj_dve, 1)
                        dve.wait_ge(proj_dve, pj.count("D", len(pj.who)))
                    else:
                        dec = QK[:, :, i * 128 + 127:i * 128 + 128].to_broadcast([128, H, 128])
                        step(v_.tensor_tensor(SS[:, i], SS[:, i - 1], dec, ALU.mult))
                        v_.tensor_tensor(SS[:, i], SS[:, i], new, ALU.add).then_inc(proj_dve, 1)
                        dve.wait_ge(proj_dve, pj.count("D", len(pj.who)))
            step(v_.tensor_copy(L["edec"], QK[:, :, SEQ + TS - 1:TOK:TS]))
            step(v_.tensor_tensor(QK, QK, HQ, ALU.mult))
            barrier()
            for i in range(5):
                pj.add("A")
            dve.wait_ge(rows_in, ROWS["hgrn"])
            dve.wait_ge(proj_act, pj.count("A", len(pj.who)))
            for e in range(H):
                if e >= 2:
                    dve.wait_ge(proj_done, len(pj.who))
                v_.tensor_tensor(L["Vz"][0:64, e % 2, :].rearrange("p (b v) -> p b v", b=NB),
                                 L["ib"][0:64, 4, e * 128:e * 128 + 128].unsqueeze(1).to_broadcast([64, NB, 128]),
                                 const("rowmask", 64).unsqueeze(2).to_broadcast([64, NB, 128]), ALU.mult)\
                    .then_inc(handoff["kd_ready"], 1)
                s0 = L["S0"][:, :, e, :]
                step(v_.tensor_tensor(s0, s0, L["edec"][:, e, :].unsqueeze(2).to_broadcast([128, NB, 128]), ALU.mult))
                for c in range(2):
                    for v in banks("D", 1):
                        s = L["S0"][:, 4 * c:4 * c + 4, e, :]
                        v_.tensor_tensor(s, s, v.rearrange("p (b v) -> p b v", b=4), ALU.add).then_inc(proj_dve, 1)
            barrier()
            for c in range(KC):
                dve.wait_ge(handoff["onorm_root"], c + 1)
                r = L["rt"][:, c % 2, :]
                step(v_.reciprocal(r, r))
                if c < 4:
                    v_.scalar_tensor_tensor(out=oT[:, c, :], in0=oT[:, c, :], scalar=subg, in1=r, op0=ALU.mult,
                                            op1=ALU.mult).then_inc(handoff["onorm_done"], 1)
                else:
                    step(v_.scalar_tensor_tensor(out=r, in0=L["OB"][:, c - 4, :], scalar=small[:, 1:2], in1=r,
                                                 op0=ALU.mult, op1=ALU.mult))
                    v_.tensor_tensor(oT[:, c, :], oT[:, c, :], r, ALU.mult).then_inc(handoff["onorm_done"], 1)
            barrier()
            add_to_x()
            barrier()

            def cross_and_ffn(l):
                normalise(COLS, 2 + l, hT)
                barrier()
                for i in range(10):
                    pj.add("A")
                normalise(COLS[0:2], 4 + l, L["memT"])
                barrier()
                for i in range(8):
                    pj.add("A")
                barrier()
                for i in range(4):
                    tr("A")
                step(v_.memset(L["qzx"], 0.0))
                for c in range(KC):
                    v_.tensor_copy(L["qzx"][:, c, :].rearrange("p (b w) -> p b w", w=72)[:, :, 0:8],
                                   L["qxT"][:, c, SEQ:TOK].rearrange("p (b t) -> p b t", b=NB))
                barrier()

                def xp_normal(j, n, p):
                    r = rs2[n % 2]
                    step(v_.reciprocal(r[:, 0:4], sm2[n % 2][:, 0:4]))
                    pv = p[:, 0:1024].rearrange("p (h m) -> p h m", h=4)
                    v_.tensor_tensor(pv, pv, r[:, 0:4].unsqueeze(2).to_broadcast([128, 4, 256]), ALU.mult)\
                        .then_inc(probs_ready, 1)

                def xp_copy(i, s):
                    v_.tensor_copy(oT[:, :, i * 128:i * 128 + 128], s[:, 0:1024].rearrange("p (c q) -> p c q", c=8))\
                        .then_inc(out_copied, 1)

                attend(4, lambda j, n, s: biased(n, None, s[:, 0:1024].rearrange("p (h m) -> p h m", h=4), 256 ** -0.5, 4),
                       xp_normal, lambda j: (tr("A"), tr("A")), xp_copy)

                def xs_prep(j):
                    for b in range(NB):
                        for g in range(4):
                            tr_copy("A" if g % 2 else "D", [L["mkK"], L["mkT"]][b % 2][:, 2 * g:2 * g + 2, :],
                                    view=lambda t: t.rearrange("p (c m) -> p c m", c=2))

                def xs_normal(j, n, p):
                    r = rs2[n % 2]
                    step(v_.reciprocal(r[:, 0:2], sm2[n % 2][:, 0:2]))
                    pv = p[:, 0:512].rearrange("p (h m) -> p h m", h=2)
                    v_.tensor_tensor(pv, pv, r[:, 0:2].unsqueeze(2).to_broadcast([128, 2, 256]), ALU.mult)\
                        .then_inc(probs_ready, 1)

                def xs_copy(i, s):
                    v_.tensor_copy(oT[:, :, SEQ:TOK], s[:, 0:512].rearrange("p (c q) -> p c q", c=8)).then_inc(out_copied, 1)

                attend(1, lambda j, n, s: biased(n, None, s[:, 0:1024].rearrange("p (h m) -> p h m", h=2)[:, :, 0:256],
                                                 256 ** -0.5, 2), xs_normal, lambda j: tr("A"), xs_copy, xs_prep)
                barrier()
                add_to_x()
                barrier()
                normalise(COLS, 6 + l, hT)
                for c in range(0, FC, 4):
                    m = min(4, FC - c)
                    tr_copy("D", L["fcol"][:, c:c + m, :], view=lambda t: t[:, 0:m * 20].rearrange("p (c r) -> p c r", c=m))
                barrier()
                fcol, gc, sil, actT, gs, cst_ = (L[k] for k in ("fcol", "gc", "sil", "act", "gs", "cstate"))
                for j in range(FC // 2):
                    first = len(pj.who)
                    us = [pj.add("D") for _ in range(5)]
                    for e in range(2):
                        n = 2 * j + e
                        dve.wait_ge(proj_done, first + 5)
                        main, samp = bank(us[e]), bank(us[4])[:, e * 64:e * 64 + 64].rearrange("p (b t) -> p b t", b=NB)
                        w = lambda r: fcol[:, n, 16 + r:17 + r]
                        g = gc[:, n % 2, :]
                        gsm = g[:, SEQ:TOK].rearrange("p (b t) -> p b t", b=NB)
                        S["silu"] += 1
                        if S["silu"] > 2:
                            dve.wait_ge(handoff["silu_done"], S["silu"] - 2)
                        if S["silu"] > 1:
                            dve.wait_ge(handoff["gate_done"], S["silu"] - 1)
                        v_.tensor_copy(gs[:, :, 0:2], fcol[:, n, 0:16].rearrange("p (b w) -> p b w", b=NB))
                        v_.tensor_copy(gs[:, :, 2:10], samp)
                        step(v_.tensor_scalar(g[:, 0:SEQ], main, w(2), w(3), ALU.mult, ALU.add))
                        v_.tensor_copy(cst_[:, n, 2:18].rearrange("p (b w) -> p b w", b=NB), gs[:, :, 8:10])
                        v_.tensor_scalar(gsm, gs[:, :, 2:10], w(2), w(3), ALU.mult, ALU.add)
                        step(v_.scalar_tensor_tensor(out=g[:, 1:SEQ], in0=main[:, 0:SEQ - 1], scalar=w(1), in1=g[:, 1:SEQ],
                                                     op0=ALU.mult, op1=ALU.add))
                        v_.tensor_copy(cst_[:, n, 0:2], main[:, SEQ - 2:SEQ])
                        step(v_.scalar_tensor_tensor(out=gsm, in0=gs[:, :, 1:9], scalar=w(1), in1=gsm, op0=ALU.mult, op1=ALU.add))
                        v_.scalar_tensor_tensor(out=g[:, 2:SEQ], in0=main[:, 0:SEQ - 2], scalar=w(0), in1=g[:, 2:SEQ],
                                                op0=ALU.mult, op1=ALU.add)
                        v_.scalar_tensor_tensor(out=gsm, in0=gs[:, :, 0:8], scalar=w(0), in1=gsm, op0=ALU.mult, op1=ALU.add)\
                            .then_inc(handoff["gate_done"], 1)
                    for e in range(2):
                        n = 2 * j + e
                        dve.wait_ge(handoff["silu_done"], S["silu"] - 1 + e)
                        v_.tensor_tensor(actT[:, n, 0:SEQ], sil[:, n % 2, 0:SEQ], bank(us[2 + e]), ALU.mult)
                        v_.tensor_tensor(actT[:, n, SEQ:TOK], sil[:, n % 2, SEQ:TOK], bank(us[4])[:, 128 + e * 64:192 + e * 64],
                                         ALU.mult).then_inc(handoff["u_used"], 1)
                    dve.drain().then_inc(proj_dve, 5)
                barrier()
                add_to_x()
                for c in range(0, FC, 4):
                    tr("A")
                barrier()

            cross_and_ffn(0)

            normalise(COLS, 1, hT)
            barrier()
            for i in range(10):
                pj.add("A")
            dve.wait_ge(rows_in, ROWS["ikn"])
            S["norms"] += 1
            dve.wait_ge(squares, S["norms"])
            v_.tensor_scalar(ms, ss, 1.0 / 64, EPS, ALU.mult, ALU.add).then_inc(means, 1)
            dve.wait_ge(roots, S["norms"])
            v_.reciprocal(rstd, sd).then_inc(rstds, 1)
            dve.wait_ge(rstds, S["norms"])
            for i, (c0, rows) in enumerate(COLS):
                k = L["i_tm"][0:rows, i, 512:576]
                step(v_.scalar_tensor_tensor(out=k, in0=k, scalar=rstd[0:rows, i:i + 1], in1=L["ikn"][0:rows, :],
                                             op0=ALU.mult, op1=ALU.mult))
                rotate(L["i_tm"][0:rows, i, 0:576].rearrange("p (h d) -> p h d", h=9), rope8[0:rows, i], 8, 9)
                iw = L["i_tm"][0:rows, i, 576:584]
                step(v_.tensor_scalar(iw, iw, 512 ** -0.5, None, ALU.mult))
            barrier()
            for i, (c0, rows) in enumerate(COLS):
                tr_copy("D", L["iqT"][0:64, 0:4, c0:c0 + rows],
                        view=lambda t: t[0:64].rearrange("p (h t) -> p h t", h=4)[:, :, 0:rows])
                tr("A")
            for i, (c0, rows) in enumerate(COLS):
                tr_copy("D", L["ikT"][0:64, c0:c0 + rows], view=lambda t: t[0:64, 0:rows])
            tr_copy("D", L["iwT"][0:8, :], view=lambda t: t[0:8, 0:64])
            dve.wait_ge(tr_act, tj.count("A", len(tj.who)))
            dve.wait_ge(tr_dve, tj.count("D", len(tj.who)))
            v_.tensor_copy(L["iqs"][0:64].rearrange("p b (h q) -> p h b q", h=8),
                           L["iqT"][0:64, :, SEQ:TOK].rearrange("p h (b q) -> p h b q", b=NB))
            barrier()
            step(v_.memset(L["wz"], 0.0))
            for v in banks("D", 1):
                v_.tensor_tensor(L["wz"][0:64, :].rearrange("p (b w) -> p b w", w=72)[:, :, 0:8],
                                 v[0:64, 0:64].rearrange("p (b t) -> p b t", b=NB),
                                 const("sameq", 64).rearrange("p (b t) -> p b t", b=NB), ALU.mult).then_inc(proj_dve, 1)
            k = 0
            for i in range(1, 4):
                n = (i + 1) * 128
                isc = L["iscp"][i - 1]
                for h in range(8):
                    pj.add("A")
                    dve.wait_ge(proj_act, pj.count("A", len(pj.who)))
                    w = L["i_tm"][:, i, 576 + h:577 + h]
                    r = L["relup"][:, k % 2, 0:n]
                    if h == 0:
                        ins = v_.tensor_scalar(isc, r, w, None, ALU.mult)
                    else:
                        ins = v_.scalar_tensor_tensor(out=isc, in0=r, scalar=w, in1=isc, op0=ALU.mult, op1=ALU.add)
                    k += 1
                    ins.then_inc(handoff["relu_used"], 1)
                    dve.wait_ge(handoff["relu_used"], k)
                step(v_.tensor_tensor(isc[:, n - 128:n], isc[:, n - 128:n], const("causal"), ALU.add))
            dve.drain().then_inc(handoff["wz_ready"], 1)
            barrier()
            for b in range(NB):
                if b == 0:
                    tr_copy("D", L["IKT"][0:64, 0, 0:512], view=lambda t: t[0:64])
                    tr("A")
                if b + 1 < NB:
                    tr_copy("D", L["IKT"][0:64, (b + 1) % 2, 0:512], view=lambda t: t[0:64])
                    tr("A")
            dve.wait_ge(handoff["relu_used"], 24 + NB)
            s = sreg(1)
            v_.tensor_copy(L["iscs"][0:64, 0:1024], s[0:64, 0:1024])
            v_.tensor_tensor(L["iscs"][0:64, 1024:1088], s[0:64, 1024:1088], const("block64", 64), ALU.add)
            barrier()

            def select(isc, out, rows, n, k):
                work, top, eq, rank = L["work"][0:rows, 0:n], L["top"][0:rows, :], L["eq"][0:rows, 0:n], L["rank"][0:rows, 0:n]
                c = L["cnt"][0:rows, :]
                src = isc
                for it in range(k // 8):
                    step(v_.max(out=top, in_=src))
                    if it < k // 8 - 1:
                        step(v_.match_replace(out=work, in_to_replace=top, in_values=src, imm_value=-3e38))
                        src = work
                t = top[:, 7:8]
                step(v_.tensor_scalar(eq, isc, t, None, ALU.is_gt, ALU.add, accum_out=c[:, 0:1]))
                step(v_.tensor_scalar(c[:, 1:2], c[:, 0:1], -1.0, float(k), ALU.mult, ALU.add))
                step(v_.tensor_scalar(work, isc, t, None, ALU.is_equal))
                step(v_.tensor_tensor_scan(out=rank, data0=work, data1=work, initial=0.0, op0=ALU.add, op1=ALU.bypass))
                step(v_.tensor_scalar(rank, rank, c[:, 1:2], None, ALU.is_le))
                step(v_.tensor_tensor(work, work, rank, ALU.mult))
                step(v_.tensor_tensor(work, work, eq, ALU.add))
                step(v_.tensor_scalar(out, work, -NEG, NEG, ALU.mult, ALU.add))

            for i in range(1, 4):
                select(L["iscp"][i - 1], L["selp"][i - 1], 128, (i + 1) * 128, 128)
            select(L["iscs"][0:64, :], L["sels"][0:64, :], 64, 1088, 256)
            v_.tensor_copy(L["expb"][0:64, :], const("expand", 64))
            barrier()
            for b in range(3):
                for i, (c0, rows) in enumerate(COLS):
                    n = pj.add("A")
                    if b == 2:
                        dve.wait_ge(proj_act, pj.count("A", n + 1))
                        rotate(L["c_tm"][0:rows, i, :].rearrange("p (h d) -> p h d", h=10), rope16[0:rows, i], 16, 10, "ropet_c")
            barrier()
            for i, (c0, rows) in enumerate(COLS):
                tr("A")
                tr_copy("D", L["qT_c"][:, 4:8, c0:c0 + rows], view=lambda t: t.rearrange("p (h t) -> p h t", h=4)[:, :, 0:rows])
                tr_copy("D", L["kT_c"][:, :, c0:c0 + rows],
                        view=lambda t: t[:, 0:256].rearrange("p (h t) -> p h t", h=2)[:, :, 0:rows])
            dve.wait_ge(tr_act, tj.count("A", len(tj.who)))
            dve.wait_ge(tr_dve, tj.count("D", len(tj.who)))
            v_.tensor_copy(L["qs_c"].rearrange("p b g (h q) -> p (g h) b q", h=4),
                           L["qT_c"][:, :, SEQ:TOK].rearrange("p h (b q) -> p h b q", b=NB))
            barrier()

            def cp_normal(j, n, p):
                w = (JOBS_CP[j][0] + 1) * 128
                r = rs2[n % 2]
                step(v_.reciprocal(r[:, 0:2], sm2[n % 2][:, 0:2]))
                for e in range(2):
                    ins = v_.tensor_scalar(p[:, 512 * e:512 * e + w], p[:, 512 * e:512 * e + w], r[:, e:e + 1], None, ALU.mult)
                ins.then_inc(probs_ready, 1)

            def cp_copy(j, s):
                i, hp = JOBS_CP[j]
                v_.tensor_copy(oT[:, 2 * hp:2 * hp + 2, i * 128:i * 128 + 128], s[:, 0:256].rearrange("p (e q) -> p e q", e=2))\
                    .then_inc(out_copied, 1)

            attend(16, two_max(128 ** -0.5, lambda j: (JOBS_CP[j][0] + 1) * 128), cp_normal, lambda j: (tr("A"), tr("A")), cp_copy)

            def cs_prep(p):
                for bb in range(2):
                    for g in range(2):
                        tr_copy("D", L["KT_c"][:, 2 * bb + g, 0:512])
                        tr("A")

            def cs_normal(j, n, p):
                r = rs2[n % 2]
                step(v_.reciprocal(r[:, 0:1], sm2[n % 2][:, 0:1]))
                v_.tensor_scalar(p[:, 0:1088], p[:, 0:1088], r[:, 0:1], None, ALU.mult).then_inc(probs_ready, 1)

            def cs_copy(p, s):
                for bb in range(2):
                    b = 2 * p + bb
                    ins = v_.tensor_copy(oT[:, :, SEQ + 8 * b:SEQ + 8 * b + 8],
                                         s[:, 64 * bb:64 * bb + 64].rearrange("p (h q) -> p h q", h=8))
                ins.then_inc(out_copied, 1)

            attend(NB // 2, one_max(128 ** -0.5), cs_normal, past_outs, cs_copy, cs_prep)
            barrier()
            add_to_x()
            barrier()
            cross_and_ffn(1)
            norm()
            dve.wait_ge(rstds, S["norms"])
            dve.wait_ge(rows_in, ROWS["fin"])
            for i, (c0, rows) in enumerate(COLS):
                xs = x[0:rows, i, :]
                ins = v_.scalar_tensor_tensor(out=xs, in0=xs, scalar=rstd[0:rows, i:i + 1], in1=L["fin"][0:rows, :],
                                              op0=ALU.mult, op1=ALU.mult)
            ins.then_inc(handoff["onorm_done"], 1)


_INS = ["x_prompt", "x_sample", "cache_diff_k", "cache_diff_v", "state_hgrn", "cache_dsa_k", "cache_dsa_v", "cache_dsa_ik",
        "cache_mem_k", "cache_mem_v", "state_ffn_conv", "page_table", "mem_prompt", "norm_mix", "w_in_ab", "diff_lq1",
        "diff_lk1", "diff_lq2", "diff_lk2", "diff_subln", "hgrn_lb_logits", "hgrn_onorm", "w_out_ab", "w_in_c",
        "idx_k_norm", "w_out_c", "norm_x", "norm_mem", "w_xq", "w_xk", "w_xv", "w_xo", "norm_ffn", "w_ffn_in",
        "conv_ffn_w", "conv_ffn_b", "w_ffn_out", "norm_final"]
_OUTS = [("y_p", (1, 512, 1024)), ("y_s", (8, 8, 1024)), ("diff_k_p", (1, 1, 512, 4, 128)), ("diff_v_p", (1, 1, 512, 4, 128)),
         ("hgrn_p", (1, 1, 4, 128, 128)), ("dsa_k_p", (1, 1, 512, 2, 128)), ("dsa_v_p", (1, 1, 512, 2, 128)),
         ("dsa_ik_p", (1, 1, 512, 64)), ("mem_k", (2, 1, 256, 4, 256)), ("mem_v", (2, 1, 256, 4, 256)),
         ("conv_p", (2, 1, 2, 2816)), ("diff_k_s", (1, 8, 8, 4, 128)), ("diff_v_s", (1, 8, 8, 4, 128)),
         ("hgrn_s", (1, 8, 4, 128, 128)), ("dsa_k_s", (1, 8, 8, 2, 128)), ("dsa_v_s", (1, 8, 8, 2, 128)),
         ("dsa_ik_s", (1, 8, 8, 64)), ("conv_s", (2, 8, 2, 2816))]


def kernel(**inputs):
    import concourse.bacc as _bacc
    from concourse.bass_utils import run_bass_kernel_spmd as _run

    nc = _bacc.Bacc("TRN2", target_bir_lowering=False, num_devices=1)
    arrays, A, O = {}, {}, {}
    for name in _INS:
        a = np.ascontiguousarray(inputs[name])
        arrays[f"in_{name}"] = a
        A[name] = nc.dram_tensor(f"in_{name}", a.shape, mybir.dt.from_np(a.dtype), kind="ExternalInput").ap()
    for name, a in zip(("consts", "levels"), constants()):
        arrays[f"in_{name}"] = a
        A[name] = nc.dram_tensor(f"in_{name}", a.shape, mybir.dt.from_np(a.dtype), kind="ExternalInput").ap()
    for name, shape in _OUTS:
        ap = nc.dram_tensor(f"out_{name}", shape, mybir.dt.float32, kind="ExternalOutput").ap()
        if name in ("diff_k_p", "diff_v_p", "hgrn_p", "dsa_k_p", "dsa_v_p", "dsa_ik_p"):
            ap = ap[0, 0]
        elif name in ("y_p", "diff_k_s", "diff_v_s", "hgrn_s", "dsa_k_s", "dsa_v_s", "dsa_ik_s"):
            ap = ap[0]
        elif name in ("mem_k", "mem_v", "conv_p"):
            ap = ap[:, 0]
        O[name] = ap
    build(nc, A, O)
    r = _run(nc, [arrays], core_ids=[0])
    return tuple(r.results[0][f"out_{name}"] for name, _ in _OUTS)
```

```python
import math
import numpy as np
import concourse.bass as bass
from concourse import mybir
from contextlib import ExitStack

D = 1024
SEQ = 512
NB, TS = 8, 8
NSAMP = NB * TS
TOK = SEQ + NSAMP
NTILE = 5
PAST, PAGE = 1024, 128
NPAGE = PAST // PAGE
DEPTH = 2
H = 4
DFF = 2816
KC = D // 128
FC = DFF // 128
NMEM = 256
EPS = 1e-6
NEG = -1e30
LAM_INIT = 0.8 - 0.6 * math.exp(-0.3 * 0)
THETA = 500000.0
COLS = [(i * 128, 128) for i in range(4)] + [(SEQ, NSAMP)]
WC_Q, WC_K, WC_V, WC_IQ, WC_IK, WC_IW, WC_END = 0, 1024, 1280, 1536, 2048, 2112, 2120

CONST = {}
_at = 0
for _name, _n in (("ident", 128), ("ones", 128), ("causal", 128), ("newmask", 120), ("expand", 512),
                  ("rope8", 5 * 2 * 16), ("rope16", 5 * 2 * 32), ("reset", TOK), ("heads", 64), ("sameq", 64),
                  ("block64", 64), ("rowmask", 8), ("mapsel", 2)):
    CONST[_name] = (_at, _n)
    _at += _n
NCONST = _at
LEVELS = [0, 1, 2, 4, 8, 16, 32, 64]


def constants():
    c = np.zeros((128, NCONST), np.float32)

    def put(name, a):
        at, n = CONST[name]
        c[:a.shape[0], at:at + n] = a.reshape(a.shape[0], n)

    r = np.arange(128)
    put("ident", np.eye(128, dtype=np.float32))
    put("ones", np.full((128, 128), 1.0 / 128, np.float32))
    put("causal", np.where(r[None, :] <= r[:, None], 0.0, NEG).astype(np.float32))
    off = np.arange(120)[None, :] - 56
    put("newmask", np.where((off >= 0) & (off <= (r % 8)[:, None]), 0.0, NEG).astype(np.float32))
    e = np.zeros((64, 4, 128), np.float32)
    for p in range(4):
        for row in range(128):
            e[(2 * p + row // 64) * 8 + row % 8, p, row] = 1.0
    put("expand", e)
    pos = np.zeros((128, 5), np.float32)
    pos[:, :4] = np.arange(512).reshape(4, 128).T
    pos[:64, 4] = PAST + np.arange(64) % TS
    for name, half in (("rope8", 8), ("rope16", 16)):
        inv = np.exp(np.arange(half, dtype=np.float32) * np.float32(-math.log(THETA) / half)).astype(np.float32)
        ang = (pos[:, :, None] * inv).astype(np.float32)
        co, si = np.cos(ang), np.sin(ang)
        put(name, np.stack([np.concatenate([co, co], -1), np.concatenate([-si, si], -1)], 2).astype(np.float32))
    reset = np.ones(TOK, np.float32)
    reset[0:SEQ:128] = 0.0
    reset[SEQ::TS] = 0.0
    put("reset", np.tile(reset, (128, 1)))
    hq = np.arange(64)
    put("heads", (hq[None, :] // 8 == np.arange(8)[:, None]).astype(np.float32))
    put("sameq", (hq[None, :] % 8 == hq[:, None] % 8).astype(np.float32))
    put("block64", np.where((hq[None, :] // 8 == hq[:, None] // 8) & (hq[None, :] % 8 <= hq[:, None] % 8),
                            0.0, NEG).astype(np.float32))
    put("rowmask", (hq[:, None] // 8 == np.arange(8)[None, :]).astype(np.float32))
    put("mapsel", np.stack([(r % 16 < 8), (r % 16 >= 8)], 1).astype(np.float32))
    s, t = r[:, None], r[None, :]
    lev = np.zeros((128, len(LEVELS), 128), np.float32)
    for i, h in enumerate(LEVELS):
        if h == 0:
            lev[:, i] = s == t
        else:
            lev[:, i] = (s // (2 * h) == t // (2 * h)) & (s // h % 2 == 0) & (t // h % 2 == 1)
    return c, lev.reshape(128, -1)


class Turns:

    def __init__(self):
        self.who = []

    def add(self, w):
        self.who.append(w)
        return len(self.who) - 1

    def count(self, w, n):
        return sum(1 for x in self.who[:n] if x == w)


class Chain:

    def __init__(self, eng, sem):
        self.eng, self.sem, self.n = eng, sem, 0

    def __call__(self, ins):
        self.n += 1
        ins.then_inc(self.sem, 1)
        self.eng.wait_ge(self.sem, self.n)


def build(nc, A, O):
    f32, bf16, u8, i32, f32r = (mybir.dt.float32, mybir.dt.bfloat16, mybir.dt.uint8, mybir.dt.int32, mybir.dt.float32r)
    ALU, ACT, AX = mybir.AluOpType, mybir.ActivationFunctionType, mybir.AxisListType
    NW, NV, NC_ = 5, 3, 3
    KS = 2
    NBANK = 6
    AW = 16640
    ctx = ExitStack()
    with ctx:
        ctx.enter_context(nc.allow_non_contiguous_dma(reason="narrow rows of small operands"))

        def sb(name, shape, dt=f32):
            return ctx.enter_context(nc.sbuf_tensor(name, shape, dt))

        def sem(name):
            return ctx.enter_context(nc.semaphore(name))

        cst = sb("cst", [128, NCONST])
        lev = sb("lev", [128, len(LEVELS) * 128], u8)
        identb = sb("identb", [128, 128], bf16)
        causalb = sb("causalb", [128, 128], bf16)
        newmaskb = sb("newmaskb", [128, 120], bf16)
        x = sb("x", [128, NTILE, D])

        def two(name, shape):
            with nc.sbuf_tensor(name, shape, f32) as plain:
                pass
            return plain, sb(name + "_r", shape, f32r)

        hT, hH = two("hT", [128, KC, TOK])
        xr, xL = two("xr", [128, KC, TOK])
        oT, oH = two("oT", [128, KC, TOK])
        W, WL = two("W", [128, NW, KS, 512])
        WH = sb("WH", [128, NV, KS, 512], f32r)
        C = sb("C", [128, NC_, 2048])
        arena, arena_r = two("arena", [128, AW])
        gains = sb("gains", [128, 8, 8])
        small = sb("small", [128, 10])
        misc = sb("misc", [128, 64])
        stat = sb("stat", [128, 64])
        pt = sb("pt", [1, 64], i32)
        gs_t = sb("gs_t", [128, 160])
        edec_t = sb("edec_t", [128, 32])
        PS = ctx.enter_context(nc.psum_tensor("PS", [128, 8 * 512], f32))

        def const(name, rows=128):
            at, n = CONST[name]
            return cst[0:rows, at:at + n]

        ident = const("ident")
        rope8 = const("rope8").rearrange("p (i s c) -> p i s c", i=5, s=2)
        rope16 = const("rope16").rearrange("p (i s c) -> p i s c", i=5, s=2)
        levels = lev[:, :].rearrange("p (l t) -> p l t", t=128)

        def region(at, *shape):
            n = int(np.prod(shape))
            assert at + n <= AW, (at, n, AW)
            v = arena[:, at:at + n]
            if len(shape) == 1:
                return v
            if len(shape) == 2:
                return v.rearrange("p (a b) -> p a b", b=shape[1])
            if len(shape) == 3:
                return v.rearrange("p (a b c) -> p a b c", b=shape[1], c=shape[2])
            return v.rearrange("p (a b c d) -> p a b c d", b=shape[1], c=shape[2], d=shape[3])

        def bank(n):
            return PS[:, (n % NBANK) * 512:(n % NBANK) * 512 + 512]

        def tbank(n):
            return PS[:, 3072 + 512 * (n % 2):3584 + 512 * (n % 2)]

        def sreg(j):
            return PS[:, 1536 * (j % 2):1536 * (j % 2) + 1536]

        oflat = oT[:, :, :].rearrange("p c t -> p (c t)")
        hflat = hT[:, :, :].rearrange("p c t -> p (c t)")
        xflat = xr[:, :, :].rearrange("p c t -> p (c t)")

        hX = hH[:, :, :], xL[:, :, :]
        oX = oH[:, :, :], xL[:, :, :]

        def plain(v):
            return v.bitcast(f32)

        junk = oflat[:, 0:1024]
        xn = [oflat[:, 1024 + 1024 * i:2048 + 1024 * i] for i in range(2)]
        ss, ms, sd, rstd = (stat[:, 8 * i:8 * i + 5] for i in range(4))
        lam = misc[:, 0:1]
        sgn = misc[:, 1:2]
        eps_col = misc[:, 2:3]
        lb, omlb = misc[:, 4:8], misc[:, 8:12]
        subg = misc[:, 12:13]
        mx, nm, sm, rs = (stat[:, 32 + 4 * i:36 + 4 * i] for i in range(4))
        mx2, nm2, sm2 = ([v, stat[:, a:a + 4]] for v, a in ((mx, 48), (nm, 52), (sm, 56)))
        rs2 = [rs, stat[:, 60:64]]

        FH = 12
        FA = 2 * FH * TOK
        P = [region(0, 1088), region(1088, 1088)]
        PT = region(2176, 9, 128)
        L = {
            "grow": region(0, 1024), "srow": region(1024, 128), "lrow": region(1280, 4, 64), "lp": region(1536, 2, 64),
            "ls": region(1664, 2), "le": region(1668, 2), "ld": region(1672, 1), "lbm": region(1676, 4),
            "lbd": region(1680, 8), "lbe": region(1688, 8), "lbr": region(1696, 4), "lev_in": region(2048, len(LEVELS) * 128),
            "a_qk": region(3328, 5, 1024), "a_v": region(8448, 5, 512), "qT_a": region(11008, 4, TOK),
            "kT_a": region(13312, 4, TOK), "qz_a": region(15616, 8, 4, 32), "KT_a": region(3328, 4, 1024),
            "ropet": region(0, 2, 256),
            "HQ": region(0, 4, TOK), "HK": region(2304, 4, TOK), "B": region(4608, 4, TOK), "QK": region(6912, 4, TOK),
            "ATT": region(9216, 5, 4, 128), "KD": xflat[:, 0:2560].rearrange("p (i h k) -> p i h k", i=5, h=4), "ib": region(11776, 5, 512),
            "SS": region(2304, 4, 4, 128), "Vz": region(0, 2, 1024), "OB": region(4608, 4, TOK),
            "edec": edec_t[:, :].rearrange("p (h b) -> p h b", h=4), "sq": region(9216, 2, TOK), "rt": region(10368, 2, TOK),
            "S0": hflat[:, 0:4096].rearrange("p (b h v) -> p b h v", b=8, h=4),
            "qxT": region(3328, 8, TOK), "mk": region(7936, 2, 1024), "mkK": region(7936, 8, 256), "mv": region(9984, 2, 1024),
            "mkT": region(12032, 8, 256), "qzx": hT[:, :, :],
            "mem": region(0, 2, 1024),
            "frow": region(0, DFF), "cstate": region(FA, FC, 18), "fcol": region(FA + FC * 18, FC, 20),
            "gc": oflat[:, 0:1024].rearrange("p (e t) -> p e t", e=2), "sil": oflat[:, 1024:2048].rearrange("p (e t) -> p e t", e=2),
            "gcs": oflat[:, 2048:2176].rearrange("p (e t) -> p e t", e=2),
            "sils": oflat[:, 2176:2304].rearrange("p (e t) -> p e t", e=2),
            "gs": gs_t[:, :].rearrange("p (e b w) -> p e b w", e=2, b=8),
            "i_tm": region(0, 5, 584), "iwT": region(2920, 64), "wz": region(2984, TOK), "ikn": region(3560, 64),
            "ikj": region(3624, 64), "ikT": region(3688, TOK), "relup": region(4264, 2, 512), "IKT": region(5288, 2, 1024),
            "relu": region(7336, 2, 1088), "iqs": region(9512, 8, 64), "ropet_i": region(10024, 2, 256), "iqT": oT[:, :, :],
            "iscp": [region(14048, 256), region(14304, 384), region(14688, 512)], "iscs": region(15200, 1088),
            "work": region(0, 1088), "eq": region(1088, 1088), "rank": region(2176, 1088), "top": region(16288, 8),
            "cnt": region(16296, 8),
            "c_tm": region(3328, 5, 1280), "v_c": region(9728, 5, 256), "kT_c": region(11008, 2, TOK), "qT_c": hT[:, :, :],
            "qs_c": region(13536, 8, 2, 32), "KT_c": region(3328, 4, 1024), "ropet_c": region(0, 2, 320),
            "selp": [region(12160 + a, n).bitcast(bf16) for a, n in ((0, 128), (128, 192), (320, 256))],
            "sels": region(12160 + 576, 544).bitcast(bf16), "expb": region(12160 + 1120, 256).bitcast(bf16),
            "fin": region(4096, D),
        }
        aH, aL = (arena_r[:, at:at + FH * TOK].rearrange("p (c t) -> p c t", t=TOK) for at in (0, FH * TOK))
        FIRST = 16 * 15
        ROWS = {"hgrn": 128, "mem0": 144, "ffn0": 192, "ikn": 208, "mem1": 224, "ffn1": 272, "fin": 288}
        JOBS_AP = [(i, h) for i in range(4) for h in range(H)]
        JOBS_CP = [(i, hp) for i in range(4) for hp in range(4)]

        first_in = sem("first_in")
        cast_in = sem("cast_in")
        rows_in = sem("rows_in")
        w_full = [sem(f"w_full{i}") for i in range(NW)]
        hi_done = sem("hi_done")
        lo_done = sem("lo_done")
        w_free = sem("w_free")
        c_full = [sem(f"c_full{i}") for i in range(NC_)]
        c_free = sem("c_free")
        proj_done = sem("proj_done")
        proj_act = sem("proj_act")
        proj_dve = sem("proj_dve")
        tr_done = sem("tr_done")
        tr_act = sem("tr_act")
        tr_dve = sem("tr_dve")
        squares = sem("squares")
        means = sem("means")
        roots = sem("roots")
        rstds = sem("rstds")
        xn_done = sem("xn_done")
        scores_ready = sem("scores_ready")
        rowmax_ready = sem("rowmax_ready")
        exp_done = sem("exp_done")
        probs_ready = sem("probs_ready")
        out_ready = sem("out_ready")
        out_copied = sem("out_copied")
        phase = {e: sem(f"phase_{e}") for e in ("pe", "act", "dve", "pool")}
        dve_step = sem("dve_step")
        act_step = sem("act_step")
        stores = sem("stores")
        handoff = {k: sem(k) for k in ("lam_in", "lam_e", "decay_d", "decay_e", "qk_ready", "qk_used", "f_ready", "logf",
                                       "relu_done", "relu_used", "isc_done", "silu_done", "prod_done", "act_hi", "h_raw", "h_hi", "o_raw", "o_hi", "sq_done", "onorm_mean", "onorm_root",
                                       "onorm_done", "gate_done", "wz_ready", "kd_ready", "pool_rows")}

        def halves(w, cols, nk=KC):
            v = w.rearrange("(k p) n -> p k n", p=128)
            return [(v, k, min(KS, nk - k), cols) for k in range(0, nk, KS)]

        blk = lambda a, b, step=512: [[(i, min(i + step, b))] for i in range(a, b, step)]
        HALF = ((0, FH), (FH, FC))
        ORDER = {}
        stream = []

        def add(name, w, blocks, nk=KC):
            ORDER[name] = [halves(w, cols, nk) for cols in blocks]
            for b in ORDER[name]:
                stream.extend(b)

        add("a_in", A["w_in_ab"][0], blk(0, 1536))
        add("b_gates", A["w_in_ab"][0], blk(1536, 2560) + blk(3072, 3584))
        add("b_values", A["w_in_ab"][0], blk(2560, 3072))
        add("ab_out", A["w_out_ab"][0], blk(0, D))

        def add_rest(l):
            add(f"xq{l}", A["w_xq"][l], blk(0, D))
            add(f"xk{l}", A["w_xk"][l], blk(0, D))
            add(f"xv{l}", A["w_xv"][l], blk(0, D))
            add(f"xo{l}", A["w_xo"][l], blk(0, D))
            for part, (a, z) in enumerate(HALF):
                add(f"up{l}{part}", A["w_ffn_in"][l], [[(256 * j, 256 * j + 256), (DFF + 256 * j, DFF + 256 * j + 256)]
                                                       for j in range(a // 2, z // 2)])
                add(f"down{l}{part}", A["w_ffn_out"][l][a * 128:z * 128, :], blk(0, D), z - a)

        add_rest(0)
        add("c_idx", A["w_in_c"][0], [[(WC_IQ, WC_IK)], [(WC_IK, WC_END)]])
        add("c_qkv", A["w_in_c"][0], blk(0, WC_IQ))
        add("c_out", A["w_out_c"][0], blk(0, D))
        add_rest(1)

        block = ctx.enter_context(nc.Block())

        @block.sync
        def _(sp):
            for n, (v, k0, nk, cols) in enumerate(stream):
                if n >= NW:
                    sp.wait_ge(w_free, n - NW + 1)
                at = 0
                for a, b in cols:
                    sp.dma_start(W[:, n % NW, 0:nk, at:at + b - a], v[:, k0:k0 + nk, a:b]).then_inc(w_full[n % NW], 16)
                    at += b - a

        def w_target(n):
            return 16 * sum(len(stream[m][3]) for m in range(n % NW, n + 1, NW))

        K_A, V_A = A["cache_diff_k"][0], A["cache_diff_v"][0]
        K_C, V_C, IK_C = A["cache_dsa_k"][0], A["cache_dsa_v"][0], A["cache_dsa_ik"][0]
        CL = []

        def diff_slots():
            for b in range(NB + 1):
                if b < NB:
                    CL.extend([("ka", b, 0), ("ka", b, 4)])
                if b > 0:
                    CL.extend([("va", b - 1, 0), ("va", b - 1, 4)])

        def cross_slots(l):
            CL.extend([(f"mk{l}", b, 0) for b in range(NB)])
            CL.extend([(f"mv{l}", b, 0) for b in range(NB)])

        diff_slots()
        cross_slots(0)
        CL.extend([("ik", b, 0) for b in range(NB)])
        CL.extend([("kc", 0, 0), ("kc", 1, 0)])
        for p in range(1, NB // 2 + 1):
            if p < NB // 2:
                CL.extend([("kc", 2 * p, 0), ("kc", 2 * p + 1, 0)])
            CL.extend([("vc", 2 * p - 2, 0), ("vc", 2 * p - 1, 0)])
        cross_slots(1)

        def c_pieces(kind):
            return {"ka": 4, "va": 4, "ik": 8, "kc": 8, "vc": 8}.get(kind, 1)

        def c_target(n):
            return 16 * sum(c_pieces(CL[m][0]) for m in range(n % NC_, n + 1, NC_))

        @block.gpsimd
        def _(pool):
            pool.dma_start(pt[0:1, :], A["page_table"].rearrange("b n -> (b n)").unsqueeze(0)).then_inc(handoff["pool_rows"], 16)
            pool.wait_ge(handoff["pool_rows"], 16)
            for n, (kind, b, first) in enumerate(CL):
                if n >= NC_:
                    pool.wait_ge(c_free, n - NC_ + 1)
                slot = C[:, n % NC_, :]
                if kind[0] == "m":
                    src = A["cache_mem_" + kind[1]][int(kind[2]), b].rearrange("(m p) h d -> p m (h d)", p=128)
                    pool.dma_start(slot.rearrange("p (m d) -> p m d", m=2), src).then_inc(c_full[n % NC_], 16)
                    continue
                pools = {"ka": K_A, "va": V_A, "kc": K_C, "vc": V_C, "ik": IK_C}[kind]
                v = pools.rearrange("g s d -> s g d") if kind == "ik" else pools.rearrange("g s h d -> s g (h d)")
                width = v.shape[2]
                for j in range(c_pieces(kind)):
                    at = b * NPAGE + first + j
                    page = pool.value_load(pt[0:1, at:at + 1], min_val=0, max_val=v.shape[1] - 1)
                    pool.dma_start(slot[:, j * width:(j + 1) * width],
                                   v[:, bass.ds(page, 1), :].rearrange("s g d -> s (g d)")).then_inc(c_full[n % NC_], 16)

        @block.tensor
        def _(pe):
            S = {"w": 0, "c": 0, "job": 0, "phase": 0, "xn": 0, "release": 0}
            pj, tj = Turns(), Turns()
            mm, tp = nc.tensor.matmul, nc.tensor.transpose

            def barrier():
                S["phase"] += 1
                pe.drain().then_inc(phase["pe"], 1)
                for e in ("act", "dve"):
                    pe.wait_ge(phase[e], S["phase"])

            def open_bank(who):
                n = pj.add(who)
                if n >= NBANK:
                    w = pj.who[n - NBANK]
                    pe.wait_ge(proj_act if w == "A" else proj_dve, pj.count(w, n - NBANK + 1))
                return n

            def open_tr(who):
                n = tj.add(who)
                if n >= 2:
                    w = tj.who[n - 2]
                    pe.wait_ge(tr_act if w == "A" else tr_dve, tj.count(w, n - 1))
                return tbank(n)

            def wait_tr(n=None):
                n = len(tj.who) if n is None else n
                for w, s in (("A", tr_act), ("D", tr_dve)):
                    if tj.count(w, n):
                        pe.wait_ge(s, tj.count(w, n))

            def wait_projections():
                for w, s in (("A", proj_act), ("D", proj_dve)):
                    if pj.count(w, len(pj.who)):
                        pe.wait_ge(s, pj.count(w, len(pj.who)))

            def cache():
                n = S["c"]
                S["c"] += 1
                pe.wait_ge(c_full[n % NC_], c_target(n))
                return C[:, n % NC_, :]

            def project(name, src, tiles, who, feature=False):
                xh, xl = src
                for b in ORDER[name]:
                    width = sum(y - x_ for x_, y in b[0][3])
                    count = width // 128 + 1 if feature else len(tiles)
                    units = []
                    for s, (_, k0, nk, _) in enumerate(b):
                        n = S["w"]
                        S["w"] += 1
                        pe.wait_ge(lo_done, n + 1)
                        first, last = s == 0, s == len(b) - 1
                        wh, wl = WH[:, n % NV], WL[:, n % NW]
                        for u in range(count):
                            if first:
                                units.append(open_bank(who))
                            o = bank(units[u])
                            if not feature:
                                c0, rows = tiles[u]
                                work = [(o[0:rows, 0:width], lambda v, k, c0=c0, rows=rows: v[:, k0 + k, c0:c0 + rows],
                                         lambda w, k: w[:, k, 0:width], True)]
                            elif u < count - 1:
                                work = [(o[:, 0:SEQ], lambda w, k, c=u: w[:, k, c * 128:c * 128 + 128],
                                         lambda v, k: v[:, k0 + k, 0:SEQ], False)]
                            else:
                                work = [(o[:, c * 64:c * 64 + 64], lambda w, k, c=c: w[:, k, c * 128:c * 128 + 128],
                                         lambda v, k: v[:, k0 + k, SEQ:TOK], False) for c in range(count - 1)]
                            for g, (out, lhs, rhs, rows_first) in enumerate(work):
                                for k in range(nk):
                                    pairs = ((xh, wh), (xh, wl), (xl, wh)) if rows_first else ((wh, xh), (wh, xl), (wl, xh))
                                    for e, (a, c) in enumerate(pairs):
                                        ins = mm(out, lhs(a, k), rhs(c, k), start=first and k == 0 and e == 0 and g == 0,
                                                 stop=last and k == nk - 1 and e == 2, skip_group_check=True)
                            if last:
                                ins.then_inc(proj_done, 1)
                        if last:
                            pe.drain().then_inc(w_free, 1)
                        else:
                            ins.then_inc(w_free, 1)

            def norm_transposes(tiles):
                for i, (c0, rows) in enumerate(tiles):
                    S["xn"] += 1
                    pe.wait_ge(xn_done, S["xn"])
                    for g in range(2):
                        t = open_tr("D")
                        for c in range(4):
                            ins = tp(t[:, c * 128:c * 128 + rows], xn[i % 2][0:rows, (4 * g + c) * 128:(4 * g + c + 1) * 128],
                                     ident[0:rows, 0:rows])
                        ins.then_inc(tr_done, 1)

            def tr_unit(who, pieces):
                t = open_tr(who)
                for off, src in pieces:
                    rows, cols = src.shape[0], src.shape[1]
                    ins = tp(t[0:cols, off:off + rows], src, ident[0:rows, 0:rows])
                ins.then_inc(tr_done, 1)

            def attend(jobs, prep, scores, prob_units, values):
                def start(j):
                    n = S["job"] + j
                    if prep:
                        prep(j)
                    if n >= 2:
                        pe.wait_ge(out_copied, n - 1)
                    scores(j, sreg(n)).then_inc(scores_ready, 1)

                start(0)
                for j in range(len(jobs)):
                    if j + 1 < len(jobs):
                        start(j + 1)
                    n = S["job"] + j
                    pe.wait_ge(probs_ready, n + 1)
                    for who, pieces in prob_units(j, P[n % 2]):
                        tr_unit(who, pieces)
                    wait_tr()
                    values(j, sreg(n)).then_inc(out_ready, 1)
                    if S["release"]:
                        pe.drain().then_inc(c_free, S["release"])
                        S["release"] = 0
                S["job"] += len(jobs)

            pe.wait_ge(first_in, FIRST)
            tr_unit("D", [(8 * c, L["grow"][0:8, c * 128:c * 128 + 128]) for c in range(8)])
            tr_unit("D", [(0, L["srow"][0:10, 0:128])])
            barrier()

            norm_transposes(COLS)
            barrier()
            project("a_in", hX, COLS, "A")
            barrier()
            for i, (c0, rows) in enumerate(COLS):
                tr_unit("D", [(h * 128, L["a_qk"][0:rows, i, h * 128:h * 128 + 128]) for h in range(H)])
                tr_unit("A", [(h * 128, L["a_qk"][0:rows, i, 512 + h * 128:640 + h * 128]) for h in range(H)])
            barrier()
            qT, kT, qz, KT, a_v = L["qT_a"], L["kT_a"], L["qz_a"], L["KT_a"], L["a_v"]
            jobs = JOBS_AP

            def ap_scores(j, s):
                i, h = jobs[j]
                n = (i + 1) * 128
                for m in range(2):
                    r = slice(64 * m, 64 * m + 64)
                    mm(s[:, 512 * m:512 * m + n], qT[r, h, i * 128:i * 128 + 128], kT[r, h, 0:n], start=True, stop=False,
                       skip_group_check=True)
                    ins = mm(s[:, 512 * m + n - 128:512 * m + n], identb[:, :], causalb[:, :], start=False, stop=True,
                             skip_group_check=True)
                return ins

            def ap_units(j, p):
                i, h = jobs[j]
                return [("A", [(c * 128, p[:, c * 128:c * 128 + 128]) for c in range(i + 1)])]

            def ap_values(j, s):
                i, h = jobs[j]
                for c in range(i + 1):
                    ins = mm(s[:, 0:128], a_v[:, c, h * 128:h * 128 + 128], PT[:, c, :], start=c == 0, stop=c == i)
                return ins

            attend(jobs, None, ap_scores, ap_units, ap_values)

            def as_prep(b):
                for half in range(2):
                    k = cache().rearrange("p (g h d) -> p g h d", g=4, h=H)
                    for h in range(H):
                        t = open_tr("A" if h % 2 else "D")
                        for g in range(4):
                            ins = tp(t[:, g * 128:g * 128 + 128], k[:, g, h, :], ident)
                        ins.then_inc(tr_done, 1)
                    pe.drain().then_inc(c_free, 1)
                wait_tr()

            def as_scores(b, s):
                mm(s[:, 1024:1088], identb[:, :], newmaskb[:, 56 - 8 * b:120 - 8 * b], start=True, stop=False, skip_group_check=True)
                for h in range(H):
                    o = slice(32 * h, 32 * h + 32)
                    for c in range(2):
                        mm(s[o, 512 * c:512 * c + 512], qz[:, b, h, :], KT[:, h, 512 * c:512 * c + 512], start=True, stop=True)
                    ins = mm(s[o, 1024:1088], qz[:, b, h, :], kT[:, h, SEQ:TOK], start=False, stop=True, skip_group_check=True)
                return ins

            def past_units(j, p):
                return [("D", [(c * 128, p[:, c * 128:c * 128 + 128]) for c in range(4)]),
                        ("A", [(c * 128, p[:, (c + 4) * 128:(c + 5) * 128]) for c in range(4)]),
                        ("D", [(0, p[:, 1024:1088])])]

            def as_values(b, s):
                v = [cache().rearrange("p (g h d) -> p g h d", g=4, h=H) for _ in range(2)]
                for h in range(H):
                    o = s[:, 16 * h:16 * h + 16]
                    for c in range(NPAGE):
                        mm(o, v[c // 4][:, c % 4, h, :], PT[:, c, 32 * h:32 * h + 16], start=c == 0, stop=False)
                    ins = mm(o, a_v[0:64, 4, h * 128:h * 128 + 128], PT[0:64, 8, 32 * h:32 * h + 16],
                             start=False, stop=True)
                S["release"] = 2
                return ins

            attend(list(range(NB)), as_prep, as_scores, past_units, as_values)
            barrier()
            project("b_gates", hX, COLS, "A", feature=True)
            project("b_values", hX, COLS, "A")
            barrier()

            HQ, HK, QK, ATT, KD, SS, ib = L["HQ"], L["HK"], L["QK"], L["ATT"], L["KD"], L["SS"], L["ib"]
            for n, h in enumerate(LEVELS):
                pe.wait_ge(handoff["qk_ready"], n + 1)
                for i, (c0, rows) in enumerate(COLS):
                    if i == 4 and h > 4:
                        continue
                    u = open_bank("D")
                    for e in range(H):
                        lhs = (HK if h == 0 else QK)[:, e, c0:c0 + rows]
                        rhs = (HQ if h == 0 else QK)[:, e, c0:c0 + rows]
                        ins = mm(bank(u)[0:rows, e * 128:e * 128 + rows], lhs, rhs, start=True, stop=True)
                    ins.then_inc(proj_done, 1)
                pe.drain().then_inc(handoff["qk_used"], 1)
            barrier()
            pe.wait_ge(handoff["qk_ready"], len(LEVELS) + 1)
            for i, (c0, rows) in enumerate(COLS):
                tr_unit("A", [(e * 128, QK[:, e, c0:c0 + rows]) for e in range(H)])
            barrier()
            for i in range(4):
                u = open_bank("D")
                for e in range(H):
                    ins = mm(bank(u)[:, e * 128:e * 128 + 128], KD[:, i, e, :], ib[:, i, e * 128:e * 128 + 128], start=True, stop=True)
                ins.then_inc(proj_done, 1)
            barrier()
            for i in range(4):
                u = open_bank("A")
                for e in range(H):
                    o = bank(u)[:, e * 128:e * 128 + 128]
                    ins = mm(o, ib[:, i, e * 128:e * 128 + 128], ATT[:, i, e, :], start=True, stop=i == 0)
                    if i > 0:
                        ins = mm(o, SS[:, i - 1, e, :], QK[:, e, i * 128:i * 128 + 128], start=False, stop=True)
                ins.then_inc(proj_done, 1)
            u = open_bank("A")
            pe.wait_ge(rows_in, ROWS["hgrn"])
            for e in range(H):
                o = bank(u)[:, e * 64:e * 64 + 64]
                mm(o, ib[0:64, 4, e * 128:e * 128 + 128], ATT[0:64, 4, e, 0:64], start=True, stop=False, skip_group_check=True)
                for b in range(NB):
                    ins = mm(o[:, 8 * b:8 * b + 8], L["S0"][:, b, e, :], QK[:, e, SEQ + 8 * b:SEQ + 8 * b + 8],
                             start=False, stop=b == NB - 1, skip_group_check=True)
            ins.then_inc(proj_done, 1)
            for e in range(H):
                pe.wait_ge(handoff["kd_ready"], e + 1)
                for c in range(2):
                    u = open_bank("D")
                    mm(bank(u)[:, 0:512], KD[0:64, 4, e, :], L["Vz"][0:64, e % 2, 512 * c:512 * c + 512],
                       start=True, stop=True).then_inc(proj_done, 1)
            barrier()
            for c in range(KC):
                pe.wait_ge(handoff["sq_done"], c + 1)
                if c >= 2:
                    pe.wait_ge(handoff["onorm_root"], c - 1)
                s = sreg(c)
                mm(s[:, 0:512], const("ones"), L["sq"][:, c % 2, 0:512], start=True, stop=True)
                mm(s[:, 512:576], const("ones"), L["sq"][:, c % 2, 512:576], start=True, stop=True).then_inc(handoff["onorm_mean"], 1)
            barrier()
            project("ab_out", oX, COLS, "D")
            barrier()

            def cross_and_ffn(l):
                norm_transposes(COLS)
                barrier()
                project(f"xq{l}", hX, COLS, "A", feature=True)
                wait_projections()
                norm_transposes(COLS[0:2])
                barrier()
                project(f"xk{l}", hX, COLS[0:2], "A")
                project(f"xv{l}", hX, COLS[0:2], "A")
                barrier()
                for g in range(4):
                    tr_unit("A", [((2 * c + m) * 128, L["mk"][:, m, (2 * g + c) * 128:(2 * g + c + 1) * 128])
                                  for c in range(2) for m in range(2)])
                barrier()
                qT, mkT, mv, qz = L["qxT"], L["mkT"], L["mv"], L["qzx"]
                KTs = [L["mkK"], L["mkT"]]

                def xp_scores(i, s):
                    for h in range(H):
                        for c in range(2):
                            ins = mm(s[:, h * 256:h * 256 + 256], qT[:, 2 * h + c, i * 128:i * 128 + 128],
                                     mkT[:, 2 * h + c, :], start=c == 0, stop=c == 1)
                    return ins

                def xp_units(i, p):
                    return [("A", [((2 * e + m) * 128, p[:, (4 * g + 2 * e + m) * 128:(4 * g + 2 * e + m + 1) * 128])
                                   for e in range(2) for m in range(2)]) for g in range(2)]

                def xp_values(i, s):
                    for h in range(H):
                        for dc in range(2):
                            for m in range(2):
                                ins = mm(s[:, (2 * h + dc) * 128:(2 * h + dc + 1) * 128],
                                         mv[:, m, (2 * h + dc) * 128:(2 * h + dc + 1) * 128], PT[:, 2 * h + m, :],
                                         start=m == 0, stop=m == 1)
                    return ins

                attend(list(range(4)), None, xp_scores, xp_units, xp_values)

                def xs_prep(b):
                    k = cache().rearrange("p (m d) -> p m d", m=2)
                    for g in range(4):
                        tr_unit("A" if g % 2 else "D",
                                [((2 * c + m) * 128, k[:, m, (2 * g + c) * 128:(2 * g + c + 1) * 128])
                                 for c in range(2) for m in range(2)])
                    pe.drain().then_inc(c_free, 1)

                def xs_scores(j, s):
                    xs_prep(0)
                    for b in range(NB):
                        done = len(tj.who)
                        if b + 1 < NB:
                            xs_prep(b + 1)
                        wait_tr(done)
                        for h in range(H):
                            for c in range(2):
                                ins = mm(s[64 * (h % 2):64 * (h % 2) + 64, 512 * (h // 2):512 * (h // 2) + 256],
                                         qz[:, 2 * h + c, b * 64:b * 64 + 64], KTs[b % 2][:, 2 * h + c, :],
                                         start=b == 0 and c == 0, stop=b == NB - 1 and c == 1, skip_group_check=True)
                    return ins

                def xs_units(j, p):
                    return [("A", [((2 * g + m) * 128, p[:, (2 * g + m) * 128:(2 * g + m + 1) * 128])
                                   for g in range(2) for m in range(2)])]

                def xs_values(j, s):
                    for b in range(NB):
                        v = cache().rearrange("p (m d) -> p m d", m=2)
                        for h in range(H):
                            for dc in range(2):
                                for m in range(2):
                                    ins = mm(s[:, (2 * h + dc) * 64 + 8 * b:(2 * h + dc) * 64 + 8 * b + 8],
                                             v[:, m, (2 * h + dc) * 128:(2 * h + dc + 1) * 128],
                                             PT[:, 2 * (h // 2) + m, 64 * (h % 2) + 8 * b:64 * (h % 2) + 8 * b + 8],
                                             start=m == 0, stop=m == 1)
                        if b < NB - 1:
                            ins.then_inc(c_free, 1)
                    S["release"] = 1
                    return ins

                attend([0], None, xs_scores, xs_units, xs_values)
                barrier()
                project(f"xo{l}", oX, COLS, "D")
                barrier()

                norm_transposes(COLS)
                pe.wait_ge(rows_in, ROWS[f"ffn{l}"])
                for c in range(0, FC, 4):
                    t = open_tr("D")
                    for e in range(min(4, FC - c)):
                        ins = tp(t[:, e * 20:e * 20 + 20], L["frow"][0:20, (c + e) * 128:(c + e + 1) * 128], ident[0:20, 0:20])
                    ins.then_inc(tr_done, 1)
                barrier()
                for part in range(2):
                    project(f"up{l}{part}", hX, COLS, "D", feature=True)
                    barrier()
                    project(f"down{l}{part}", (aH, aL), COLS, "D")
                    if part == 0:
                        barrier()
                wait_projections()
                for c in range(0, FC, 4):
                    tr_unit2("A", c)
                barrier()

            def tr_unit2(who, c):
                t = open_tr(who)
                for e in range(min(4, FC - c)):
                    ins = tp(t[0:18, e * 128:e * 128 + 128], L["cstate"][:, c + e, :], ident)
                ins.then_inc(tr_done, 1)

            cross_and_ffn(0)

            norm_transposes(COLS)
            barrier()
            project("c_idx", hX, COLS, "A")
            barrier()
            iT, ikT = L["iqT"], L["ikT"]
            for i, (c0, rows) in enumerate(COLS):
                for g in range(2):
                    tr_unit("A" if g else "D", [(e * 128, L["i_tm"][0:rows, i, (4 * g + e) * 64:(4 * g + e + 1) * 64])
                                                for e in range(4)])
            for i, (c0, rows) in enumerate(COLS):
                tr_unit("D", [(0, L["i_tm"][0:rows, i, 512:576])])
            tr_unit("D", [(0, L["i_tm"][0:64, 4, 576:584])])
            barrier()
            u = open_bank("D")
            mm(bank(u)[0:64, 0:64], const("heads", 8), L["iwT"][0:8, :], start=True, stop=True).then_inc(proj_done, 1)
            for i in range(1, 4):
                n = (i + 1) * 128
                for h in range(8):
                    u = open_bank("A")
                    mm(bank(u)[:, 0:n], iT[0:64, h, i * 128:i * 128 + 128], ikT[0:64, 0:n], start=True, stop=True)\
                        .then_inc(proj_done, 1)
            barrier()

            def ik_prep(b):
                k = cache()[:, 0:512].rearrange("p (g d) -> p g d", g=8)
                for g in range(2):
                    tr_unit("A" if g else "D", [(c * 128, k[:, 4 * g + c, :]) for c in range(4)])
                pe.drain().then_inc(c_free, 1)

            ik_prep(0)
            for b in range(NB):
                done = len(tj.who)
                wait_tr(done)
                if b > 0:
                    pe.wait_ge(handoff["relu_done"], b)
                s = sreg(0)
                q = L["iqs"][0:64, b, :]
                for c in range(2):
                    mm(s[0:64, 512 * c:512 * c + 512], q, L["IKT"][0:64, b % 2, 512 * c:512 * c + 512], start=True, stop=True)
                mm(s[0:64, 1024:1088], q, ikT[0:64, SEQ:TOK], start=True, stop=True).then_inc(handoff["isc_done"], 1)
                if b + 1 < NB:
                    ik_prep(b + 1)
                pe.wait_ge(handoff["relu_done"], b + 1)
                if b == 0:
                    pe.wait_ge(handoff["wz_ready"], 1)
                t = sreg(1)
                for c, (a, z) in enumerate(((0, 512), (512, 1024), (1024, 1088))):
                    ins = mm(t[0:64, a:z], L["wz"][0:64, b * 64:b * 64 + 64], L["relu"][0:64, b % 2, a:z],
                             start=b == 0, stop=b == NB - 1, skip_group_check=True)
                ins.then_inc(handoff["relu_used"], 1)
            barrier()
            project("c_qkv", hX, COLS, "A")
            barrier()
            for i, (c0, rows) in enumerate(COLS):
                for g in range(2):
                    tr_unit("D" if g else "A", [(e * 128, L["c_tm"][0:rows, i, (4 * g + e) * 128:(4 * g + e + 1) * 128])
                                                for e in range(4)])
                tr_unit("D", [(e * 128, L["c_tm"][0:rows, i, 1024 + e * 128:1152 + e * 128]) for e in range(2)])
            barrier()
            qT, kT, KT, v_tm = L["qT_c"], L["kT_c"], L["KT_c"], L["v_c"]
            jobs = JOBS_CP

            def cp_scores(j, s):
                i, hp = jobs[j]
                n = (i + 1) * 128
                for e in range(2):
                    h = 2 * hp + e
                    mm(s[:, 512 * e:512 * e + n], qT[:, h, i * 128:i * 128 + 128], kT[:, h // 4, 0:n], start=True, stop=False,
                       skip_group_check=True)
                    if i == 0:
                        ins = mm(s[:, 512 * e:512 * e + n], identb[:, :], causalb[:, :], start=False, stop=True, skip_group_check=True)
                    else:
                        ins = mm(s[:, 512 * e:512 * e + n], identb[:, :], L["selp"][i - 1], start=False, stop=True,
                                 skip_group_check=True)
                return ins

            def cp_units(j, p):
                i, hp = jobs[j]
                return [("A", [(c * 128, p[:, e * 512 + c * 128:e * 512 + c * 128 + 128]) for c in range(i + 1)]) for e in range(2)]

            def cp_values(j, s):
                i, hp = jobs[j]
                for e in range(2):
                    g = (2 * hp + e) // 4
                    for c in range(i + 1):
                        ins = mm(s[:, e * 128:e * 128 + 128], v_tm[:, c, g * 128:g * 128 + 128], PT[:, 4 * e + c, :],
                                 start=c == 0, stop=c == i)
                return ins

            attend(jobs, None, cp_scores, cp_units, cp_values)

            def cs_prep(p):
                for bb in range(2):
                    k = cache().rearrange("p (n g d) -> p n g d", n=8, g=2)
                    for g in range(2):
                        for half in range(2):
                            tr_unit("A" if half else "D", [(c * 128, k[:, 4 * half + c, g, :]) for c in range(4)])
                    pe.drain().then_inc(c_free, 1)
                wait_tr()

            def cs_scores(p, s):
                ex = L["expb"][0:64, p * 128:p * 128 + 128]
                for a, z in ((0, 512), (512, 1024), (1024, 1088)):
                    mm(s[:, a:z], ex, L["sels"][0:64, a:z], start=True, stop=False, skip_group_check=True)
                for bb in range(2):
                    b = 2 * p + bb
                    for g in range(2):
                        r = 2 * bb + g
                        q = L["qs_c"][:, b, g, :]
                        o = slice(32 * r, 32 * r + 32)
                        for c in range(2):
                            mm(s[o, 512 * c:512 * c + 512], q, KT[:, r, 512 * c:512 * c + 512], start=False, stop=True,
                               skip_group_check=True)
                        ins = mm(s[o, 1024:1088], q, kT[:, g, SEQ:TOK], start=False, stop=True, skip_group_check=True)
                return ins

            def cs_values(p, s):
                for bb in range(2):
                    v = cache().rearrange("p (n g d) -> p n g d", n=8, g=2)
                    for g in range(2):
                        r = 2 * bb + g
                        o = s[:, 32 * r:32 * r + 32]
                        for c in range(NPAGE):
                            mm(o, v[:, c, g, :], PT[:, c, 32 * r:32 * r + 32], start=c == 0, stop=False)
                        ins = mm(o, v_tm[0:64, 4, g * 128:g * 128 + 128], PT[0:64, 8, 32 * r:32 * r + 32], start=False, stop=True)
                    if bb == 0:
                        ins.then_inc(c_free, 1)
                S["release"] = 1
                return ins

            attend(list(range(NB // 2)), cs_prep, cs_scores, past_units, cs_values)
            barrier()
            project("c_out", oX, COLS, "D")
            barrier()
            cross_and_ffn(1)

        @block.scalar
        def _(act):
            S = {"phase": 0, "job": 0, "stores": 0, "means": 0, "ffn": 0}
            pj, tj = Turns(), Turns()
            step = Chain(act, act_step)
            fn = nc.scalar.activation
            S["split"], S["slot"], S["hi"], S["o"] = 0, 0, 0, 0

            def ahead(k):
                while S["split"] < min(k, len(stream)):
                    n = S["split"]
                    S["split"] += 1
                    _, _, nk, cols = stream[n]
                    width = sum(z - a for a, z in cols)
                    act.wait_ge(w_full[n % NW], w_target(n))
                    if n >= NV:
                        act.wait_ge(w_free, n - NV + 1)
                    fn(WH[:, n % NV, 0:nk, 0:width], W[:, n % NW, 0:nk, 0:width], ACT.Copy).then_inc(hi_done, 1)

            def blocks(name):
                for b in ORDER[name]:
                    ahead(S["slot"] + len(b) + 2)
                    S["slot"] += len(b)
                    yield b
                ahead(S["slot"] + 3)

            def leading(count):
                for dst, src in count:
                    S["hi"] += 1
                    act.wait_ge(handoff["h_raw"], S["hi"])
                    fn(dst, src, ACT.Copy).then_inc(handoff["h_hi"], 1)

            def barrier():
                if S["stores"]:
                    act.wait_ge(stores, 16 * S["stores"])
                S["phase"] += 1
                act.drain().then_inc(phase["act"], 1)
                for e in ("pe", "dve"):
                    act.wait_ge(phase[e], S["phase"])

            def store(dst, src):
                S["stores"] += 1
                act.dma_start(dst, src).then_inc(stores, 16)

            def load(dst, src):
                act.dma_start(dst, src).then_inc(rows_in, 16)

            def banks(who, count):
                for _ in range(count):
                    n = pj.add(who)
                    if who == "A":
                        act.wait_ge(proj_done, n + 1)
                        yield bank(n)
                    else:
                        yield None

            def tr(who):
                n = tj.add(who)
                if who != "A":
                    return None
                act.wait_ge(tr_done, n + 1)
                return tbank(n)

            def tr_copy(who, out, rows=128, view=None):
                t = tr(who)
                if t is not None:
                    fn(out, t if view is None else view(t), ACT.Copy).then_inc(tr_act, 1)

            def pass_by(name):
                for _ in blocks(name):
                    for i in range(NTILE):
                        pj.add("D")

            def norm(src, tiles):
                for i, (c0, rows) in enumerate(tiles):
                    ins = fn(junk[0:rows, :], src[0:rows, i, :], ACT.Square, accum_out=ss[0:rows, i:i + 1])
                    if i < len(tiles) - 1:
                        step(ins)
                    else:
                        ins.then_inc(squares, 1)
                S["means"] += 1
                act.wait_ge(means, S["means"])
                fn(sd, ms, ACT.Sqrt).then_inc(roots, 1)
                act.wait_ge(rstds, S["means"])

            def normalise(src, tiles):
                norm(src, tiles)
                pending = []
                for i, (c0, rows) in enumerate(tiles):
                    if len(pending) > 1:
                        leading(pending.pop(0))
                    pending.append([(hH[:, 4 * e:4 * e + 4, c0:c0 + rows], xr[:, 4 * e:4 * e + 4, c0:c0 + rows])
                                    for e in range(2)])
                    if i >= 2:
                        act.wait_ge(tr_done, len(tj.who) - 2)
                    fn(xn[i % 2][0:rows, :], src[0:rows, i, :], ACT.Copy, scale=rstd[0:rows, i:i + 1]).then_inc(xn_done, 1)
                    tr("D"), tr("D")
                for p in pending:
                    leading(p)

            def copies(name, tiles, dst):
                who = "A"
                for (a, z), _ in zip(dst, blocks(name), strict=True):
                    for i, (c0, rows) in enumerate(tiles):
                        for v in banks(who, 1):
                            if v is not None:
                                fn(a(i)[0:rows], v[0:rows, 0:z], ACT.Copy).then_inc(proj_act, 1)

            def attend(count, exps, outs, prep=None):
                def start(j):
                    n = S["job"] + j
                    if prep:
                        prep(j)
                    act.wait_ge(rowmax_ready, n + 1)
                    exps(j, n, sreg(n), P[n % 2]).then_inc(exp_done, 1)

                start(0)
                for j in range(count):
                    if j + 1 < count:
                        start(j + 1)
                    outs(j)
                S["job"] += count

            act.dma_start(cst[:, :], A["consts"]).then_inc(first_in, 16)
            act.dma_start(L["lev_in"], A["levels"]).then_inc(first_in, 16)
            for r, name in ((0, "norm_mix"), (2, "norm_x"), (4, "norm_mem"), (6, "norm_ffn")):
                act.dma_start(L["grow"][r:r + 2, :], A[name]).then_inc(first_in, 16)
            act.dma_start(L["srow"][0:1, :], A["diff_subln"]).then_inc(first_in, 16)
            act.dma_start(L["srow"][1:2, :], A["hgrn_onorm"]).then_inc(first_in, 16)
            act.dma_start(L["srow"][2:10, :], A["hgrn_lb_logits"].rearrange("l (h k) -> (l h) k", h=H)).then_inc(first_in, 16)
            for i, name in enumerate(("diff_lq1", "diff_lk1", "diff_lq2", "diff_lk2")):
                act.dma_start(L["lrow"][:, i, :], A[name].to_broadcast([128, 64])).then_inc(first_in, 16)
            act.dma_start(x[:, 0:4, :], A["x_prompt"][0].rearrange("(i p) d -> p i d", p=128)).then_inc(first_in, 16)
            act.dma_start(x[0:64, 4, :], A["x_sample"].rearrange("b t d -> (b t) d")).then_inc(first_in, 16)
            act.wait_ge(first_in, FIRST)
            tr("D"), tr("D")
            act.wait_ge(handoff["lam_in"], 1)
            fn(L["le"][:, 0:2], L["ls"][:, 0:2], ACT.Exp).then_inc(handoff["lam_e"], 1)
            act.wait_ge(handoff["lam_in"], 2)
            fn(L["lbe"][:, 0:8], L["lbd"][:, 0:8], ACT.Exp).then_inc(handoff["lam_e"], 1)
            barrier()

            ahead(3)
            normalise(x, COLS)
            barrier()
            copies("a_in", COLS, [((lambda i, b=b: L["a_qk"][:, i, 512 * b:512 * b + 512]), 512) for b in range(2)]
                   + [((lambda i: L["a_v"][:, i, :]), 512)])
            barrier()
            for i, (c0, rows) in enumerate(COLS):
                tr("D")
                tr_copy("A", L["kT_a"][:, :, c0:c0 + rows], view=lambda t: t.rearrange("p (h t) -> p h t", h=H)[:, :, 0:rows])
            store(O["diff_k_p"].rearrange("(i p) h d -> p i (h d)", p=128), L["a_qk"][:, 0:4, 512:1024])
            store(O["diff_v_p"].rearrange("(i p) h d -> p i (h d)", p=128), L["a_v"][:, 0:4, :])
            store(O["diff_k_s"].rearrange("b t h d -> (b t) (h d)"), L["a_qk"][0:64, 4, 512:1024])
            store(O["diff_v_s"].rearrange("b t h d -> (b t) (h d)"), L["a_v"][0:64, 4, :])
            barrier()

            def two_exps(scale, width):
                def run(j, n, s, p):
                    m = width(j)
                    for e in range(2):
                        ins = fn(p[:, 512 * e:512 * e + m], s[:, 512 * e:512 * e + m], ACT.Exp, bias=nm2[n % 2][:, e:e + 1],
                                 scale=scale, accum_out=sm2[n % 2][:, e:e + 1])
                    return ins
                return run

            def ap_outs(j):
                i, h = JOBS_AP[j]
                tr_copy("A", PT[:, 0:i + 1, :], view=lambda t: t[:, 0:(i + 1) * 128].rearrange("p (c q) -> p c q", c=i + 1))

            attend(16, two_exps(64 ** -0.5, lambda j: (JOBS_AP[j][0] + 1) * 128), ap_outs)

            def as_prep(b):
                for half in range(2):
                    for h in range(H):
                        tr_copy("A" if h % 2 else "D", L["KT_a"][:, h, half * 512:half * 512 + 512])

            def one_exp(scale):
                return lambda j, n, s, p: fn(p[:, 0:1088], s[:, 0:1088], ACT.Exp, bias=nm2[n % 2][:, 0:1], scale=scale,
                                             accum_out=sm2[n % 2][:, 0:1])

            def past_outs(j):
                tr("D")
                tr_copy("A", PT[:, 4:8, :], view=lambda t: t.rearrange("p (c q) -> p c q", c=4))
                tr("D")

            attend(NB, one_exp(64 ** -0.5), past_outs, as_prep)
            barrier()
            HQ, HK = L["HQ"], L["HK"]
            for (dst, f), _ in zip(((HQ, ACT.Silu), (HK, ACT.Sigmoid), (oT[:, 4:8, :], ACT.Silu)), blocks("b_gates"), strict=True):
                for c in range(4):
                    for v in banks("A", 1):
                        fn(dst[:, c, 0:SEQ], v, f).then_inc(proj_act, 1)
                for v in banks("A", 1):
                    fn(dst[:, :, SEQ:TOK], v[:, 0:256].rearrange("p (c t) -> p c t", c=4), f).then_inc(proj_act, 1)
            copies("b_values", COLS, [((lambda i: L["ib"][:, i, :]), 512)])
            barrier()
            for g in range(8):
                load(L["S0"][:, g], A["state_hgrn"][0, g].rearrange("h k v -> k h v"))
            act.wait_ge(handoff["f_ready"], 1)
            fn(L["QK"], L["B"], ACT.Ln).then_inc(handoff["logf"], 1)
            for n, h in enumerate(LEVELS):
                if h:
                    act.wait_ge(handoff["decay_d"], n)
                    e = L["QK"] if h <= 4 else L["QK"][:, :, 0:SEQ]
                    fn(e, e, ACT.Exp).then_inc(handoff["decay_e"], 1)
                for i in range(5 if h <= 4 else 4):
                    pj.add("D")
            barrier()
            act.wait_ge(handoff["decay_d"], len(LEVELS))
            fn(L["QK"], L["QK"], ACT.Exp).then_inc(handoff["decay_e"], 1)
            for i, (c0, rows) in enumerate(COLS):
                tr_copy("A", L["KD"][0:rows, i, :, :], view=lambda t: t[0:rows].rearrange("p (h k) -> p h k", h=H))
            barrier()
            for i in range(4):
                pj.add("D")
            fn(L["QK"], L["B"], ACT.Exp).then_inc(handoff["decay_e"], 1)
            barrier()
            for i in range(4):
                for v in banks("A", 1):
                    fn(L["OB"][:, :, i * 128:i * 128 + 128], v.rearrange("p (h t) -> p h t", h=H), ACT.Copy).then_inc(proj_act, 1)
            for v in banks("A", 1):
                fn(L["OB"][:, :, SEQ:TOK], v[:, 0:256].rearrange("p (h t) -> p h t", h=H), ACT.Copy).then_inc(proj_act, 1)
            for i in range(8):
                pj.add("D")
            barrier()
            store(O["hgrn_p"].rearrange("h k v -> k h v"), L["SS"][:, 3, :, :])
            for g in range(8):
                store(O["hgrn_s"][g].rearrange("h k v -> k h v"), L["S0"][:, g])
            for c in range(KC):
                src = oT[:, c, :] if c < 4 else L["OB"][:, c - 4, :]
                if c >= 2:
                    act.wait_ge(handoff["onorm_mean"], c - 1)
                fn(L["sq"][:, c % 2, :], src, ACT.Square).then_inc(handoff["sq_done"], 1)
                act.wait_ge(handoff["onorm_mean"], c + 1)
                if c >= 2:
                    act.wait_ge(handoff["onorm_done"], c - 1)
                fn(L["rt"][:, c % 2, :], sreg(c)[:, 0:TOK], ACT.Sqrt, bias=eps_col).then_inc(handoff["onorm_root"], 1)
                if c > 0:
                    act.wait_ge(handoff["o_raw"], c)
                    fn(oH[:, c - 1, :], L["rt"][:, (c - 1) % 2, :], ACT.Copy).then_inc(handoff["o_hi"], 1)
            act.wait_ge(handoff["o_raw"], KC)
            fn(oH[:, KC - 1, :], L["rt"][:, (KC - 1) % 2, :], ACT.Copy).then_inc(handoff["o_hi"], 1)
            barrier()
            pass_by("ab_out")
            barrier()

            def cross_and_ffn(l):
                load(L["mem"], A["mem_prompt"][0].rearrange("(m p) d -> p m d", p=128))
                normalise(x, COLS)
                barrier()
                for g, _ in enumerate(blocks(f"xq{l}")):
                    for c in range(4):
                        for v in banks("A", 1):
                            fn(L["qxT"][:, 4 * g + c, 0:SEQ], v, ACT.Copy).then_inc(proj_act, 1)
                    for v in banks("A", 1):
                        fn(L["qxT"][:, 4 * g:4 * g + 4, SEQ:TOK], v[:, 0:256].rearrange("p (c t) -> p c t", c=4),
                           ACT.Copy).then_inc(proj_act, 1)
                act.wait_ge(rows_in, ROWS[f"mem{l}"])
                normalise(L["mem"], COLS[0:2])
                barrier()
                for name, dst in ((f"xk{l}", L["mk"]), (f"xv{l}", L["mv"])):
                    copies(name, COLS[0:2], [((lambda i, b=b: dst[:, i, 512 * b:512 * b + 512]), 512) for b in range(2)])
                barrier()
                store(O["mem_k"][l].rearrange("(m p) h d -> p m (h d)", p=128), L["mk"])
                store(O["mem_v"][l].rearrange("(m p) h d -> p m (h d)", p=128), L["mv"])
                for g in range(4):
                    tr_copy("A", L["mkT"][:, 2 * g:2 * g + 2, :], view=lambda t: t.rearrange("p (c m) -> p c m", c=2))
                barrier()

                def xp_exps(j, n, s, p):
                    for h in range(H):
                        ins = fn(p[:, h * 256:h * 256 + 256], s[:, h * 256:h * 256 + 256], ACT.Exp, bias=nm2[n % 2][:, h:h + 1],
                                 scale=256 ** -0.5, accum_out=sm2[n % 2][:, h:h + 1])
                    return ins

                def xp_outs(j):
                    for g in range(2):
                        tr_copy("A", PT[:, 4 * g:4 * g + 4, :], view=lambda t: t.rearrange("p (c q) -> p c q", c=4))

                attend(4, xp_exps, xp_outs)

                def xs_prep(j):
                    for b in range(NB):
                        for g in range(4):
                            tr_copy("A" if g % 2 else "D", [L["mkK"], L["mkT"]][b % 2][:, 2 * g:2 * g + 2, :],
                                    view=lambda t: t.rearrange("p (c m) -> p c m", c=2))

                def xs_exps(j, n, s, p):
                    for e in range(2):
                        ins = fn(p[:, e * 256:e * 256 + 256], s[:, e * 512:e * 512 + 256], ACT.Exp, bias=nm2[n % 2][:, e:e + 1],
                                 scale=256 ** -0.5, accum_out=sm2[n % 2][:, e:e + 1])
                    return ins

                def xs_outs(j):
                    tr_copy("A", PT[:, 0:4, :], view=lambda t: t.rearrange("p (c q) -> p c q", c=4))

                attend(1, xs_exps, xs_outs, xs_prep)
                barrier()
                pass_by(f"xo{l}")
                barrier()

                load(L["frow"][0:16, :], A["state_ffn_conv"][l].rearrange("b w f -> (b w) f"))
                load(L["frow"][16:19, :], A["conv_ffn_w"][l])
                load(L["frow"][19:20, :], A["conv_ffn_b"][l:l + 1])
                normalise(x, COLS)
                for c in range(0, FC, 4):
                    tr("D")
                barrier()
                gc, sil, gcs, sils = (L[k] for k in ("gc", "sil", "gcs", "sils"))
                for part, (a, z) in enumerate(HALF):
                    for j, _ in enumerate(blocks(f"up{l}{part}")):
                        for e in range(5):
                            pj.add("D")
                        k = S["ffn"]
                        S["ffn"] += 1
                        for e, (dst, src) in enumerate(((sil[:, 0], gc[:, 0]), (sil[:, 1], gc[:, 1]), (sils, gcs))):
                            act.wait_ge(handoff["gate_done"], 3 * k + e + 1)
                            if k > 0:
                                act.wait_ge(handoff["prod_done"], 6 * k - 3 + e + 1)
                            fn(dst, src, ACT.Silu).then_inc(handoff["silu_done"], 1)
                        ahead(S["slot"] + 3)
                        for e, (dst, src) in enumerate(((aH[:, 2 * j, 0:SEQ], sil[:, 0]), (aH[:, 2 * j + 1, 0:SEQ], sil[:, 1]),
                                                        (aH[:, 2 * j:2 * j + 2, SEQ:TOK], sils))):
                            act.wait_ge(handoff["prod_done"], 6 * k + e + 1)
                            fn(dst, src, ACT.Copy).then_inc(handoff["act_hi"], 1)
                    barrier()
                    pass_by(f"down{l}{part}")
                    if part == 0:
                        barrier()
                for c in range(0, FC, 4):
                    m = min(4, FC - c)
                    tr_copy("A", L["frow"][0:18, c * 128:(c + m) * 128], view=lambda t: t[0:18, 0:m * 128])
                barrier()
                store(O["conv_p"][l], L["frow"][0:2, :])
                store(O["conv_s"][l].rearrange("b w f -> (b w) f"), L["frow"][2:18, :])

            cross_and_ffn(0)

            normalise(x, COLS)
            load(L["ikn"], A["idx_k_norm"].to_broadcast([128, 64]))
            barrier()
            copies("c_idx", COLS, [((lambda i: L["i_tm"][:, i, 0:512]), 512), ((lambda i: L["i_tm"][:, i, 512:584]), 72)])
            act.wait_ge(proj_act, pj.count("A", len(pj.who)))
            for i, (c0, rows) in enumerate(COLS):
                ins = fn(L["ikj"][0:rows, :], L["i_tm"][0:rows, i, 512:576], ACT.Square, accum_out=ss[0:rows, i:i + 1])
                if i < NTILE - 1:
                    step(ins)
                else:
                    ins.then_inc(squares, 1)
            S["means"] += 1
            act.wait_ge(means, S["means"])
            fn(sd, ms, ACT.Sqrt).then_inc(roots, 1)
            barrier()
            for i, (c0, rows) in enumerate(COLS):
                tr("D")
                tr_copy("A", L["iqT"][0:64, 4:8, c0:c0 + rows],
                        view=lambda t: t[0:64].rearrange("p (h t) -> p h t", h=4)[:, :, 0:rows])
            for i in range(6):
                tr("D")
            store(O["dsa_ik_p"].rearrange("(i p) d -> p i d", p=128), L["i_tm"][:, 0:4, 512:576])
            store(O["dsa_ik_s"].rearrange("b t d -> (b t) d"), L["i_tm"][0:64, 4, 512:576])
            barrier()
            pj.add("D")
            k = 0
            for i in range(1, 4):
                n = (i + 1) * 128
                for h in range(8):
                    for v in banks("A", 1):
                        if k >= 2:
                            act.wait_ge(handoff["relu_used"], k - 1)
                        fn(L["relup"][:, k % 2, 0:n], v[:, 0:n], ACT.Relu).then_inc(proj_act, 1)
                    k += 1
            barrier()
            for b in range(NB):
                if b == 0:
                    tr("D")
                    tr_copy("A", L["IKT"][0:64, 0, 512:1024], view=lambda t: t[0:64])
                act.wait_ge(handoff["isc_done"], b + 1)
                if b >= 2:
                    act.wait_ge(handoff["relu_used"], 24 + b - 1)
                fn(L["relu"][0:64, b % 2, :], sreg(0)[0:64, 0:1088], ACT.Relu).then_inc(handoff["relu_done"], 1)
                if b + 1 < NB:
                    tr("D")
                    tr_copy("A", L["IKT"][0:64, (b + 1) % 2, 512:1024], view=lambda t: t[0:64])
            barrier()
            for b, _ in enumerate(blocks("c_qkv")):
                for i, (c0, rows) in enumerate(COLS):
                    for v in banks("A", 1):
                        if b < 2:
                            fn(L["c_tm"][0:rows, i, 512 * b:512 * b + 512], v[0:rows], ACT.Copy).then_inc(proj_act, 1)
                        else:
                            step(fn(L["c_tm"][0:rows, i, 1024:1280], v[0:rows, 0:256], ACT.Copy))
                            fn(L["v_c"][0:rows, i, :], v[0:rows, 256:512], ACT.Copy).then_inc(proj_act, 1)
            barrier()
            for i, (c0, rows) in enumerate(COLS):
                tr_copy("A", L["qT_c"][:, 0:4, c0:c0 + rows], view=lambda t: t.rearrange("p (h t) -> p h t", h=4)[:, :, 0:rows])
                tr("D")
                tr("D")
            store(O["dsa_k_p"].rearrange("(i p) h d -> p i (h d)", p=128), L["c_tm"][:, 0:4, 1024:1280])
            store(O["dsa_v_p"].rearrange("(i p) h d -> p i (h d)", p=128), L["v_c"][:, 0:4, :])
            store(O["dsa_k_s"].rearrange("b t h d -> (b t) (h d)"), L["c_tm"][0:64, 4, 1024:1280])
            store(O["dsa_v_s"].rearrange("b t h d -> (b t) (h d)"), L["v_c"][0:64, 4, :])
            barrier()

            def cp_outs(j):
                i, hp = JOBS_CP[j]
                for e in range(2):
                    tr_copy("A", PT[:, 4 * e:4 * e + i + 1, :],
                            view=lambda t: t[:, 0:(i + 1) * 128].rearrange("p (c q) -> p c q", c=i + 1))

            attend(16, two_exps(128 ** -0.5, lambda j: (JOBS_CP[j][0] + 1) * 128), cp_outs)

            def cs_prep(p):
                for bb in range(2):
                    for g in range(2):
                        tr("D")
                        tr_copy("A", L["KT_c"][:, 2 * bb + g, 512:1024])

            attend(NB // 2, one_exp(128 ** -0.5), past_outs, cs_prep)
            barrier()
            pass_by("c_out")
            barrier()
            cross_and_ffn(1)
            load(L["fin"], A["norm_final"].unsqueeze(0).to_broadcast([128, D]))
            norm(x, COLS)
            act.wait_ge(handoff["onorm_done"], KC + 1)
            store(O["y_p"].rearrange("(i p) d -> p i d", p=128), x[:, 0:4, :])
            store(O["y_s"].rearrange("b t d -> (b t) d"), x[0:64, 4, :])
            act.wait_ge(stores, 16 * S["stores"])

        @block.vector
        def _(dve):
            S = {"phase": 0, "job": 0, "norms": 0}
            pj, tj = Turns(), Turns()
            step = Chain(dve, dve_step)
            v_ = nc.vector
            S["split"], S["slot"], S["hi"], S["ffn"] = 0, 0, 0, 0

            def ahead(k):
                while S["split"] < min(k, len(stream)):
                    n = S["split"]
                    S["split"] += 1
                    _, _, nk, cols = stream[n]
                    width = sum(z - a for a, z in cols)
                    dve.wait_ge(hi_done, n + 1)
                    at = (slice(None), n % NW, slice(0, nk), slice(0, width))
                    v_.tensor_tensor(WL[at], W[at], plain(WH[:, n % NV, 0:nk, 0:width]), ALU.subtract).then_inc(lo_done, 1)

            def blocks(name):
                for b in ORDER[name]:
                    ahead(S["slot"] + len(b) + 2)
                    S["slot"] += len(b)
                    yield b
                ahead(S["slot"] + 3)

            def pass_by(name, units):
                for _ in blocks(name):
                    for i in range(units):
                        pj.add("A")

            def barrier():
                S["phase"] += 1
                dve.drain().then_inc(phase["dve"], 1)
                for e in ("pe", "act"):
                    dve.wait_ge(phase[e], S["phase"])

            def banks(who, count):
                for _ in range(count):
                    n = pj.add(who)
                    if who == "D":
                        dve.wait_ge(proj_done, n + 1)
                        yield bank(n)
                    else:
                        yield None

            def tr(who):
                n = tj.add(who)
                if who != "D":
                    return None
                dve.wait_ge(tr_done, n + 1)
                return tbank(n)

            def tr_copy(who, out, view=None):
                t = tr(who)
                if t is not None:
                    v_.tensor_copy(out, t if view is None else view(t)).then_inc(tr_dve, 1)

            def norm(width=D):
                S["norms"] += 1
                dve.wait_ge(squares, S["norms"])
                v_.tensor_scalar(ms, ss, 1.0 / width, EPS, ALU.mult, ALU.add).then_inc(means, 1)
                dve.wait_ge(roots, S["norms"])
                v_.reciprocal(rstd, sd).then_inc(rstds, 1)

            def normalise(tiles, g):
                norm()
                pending = []

                def rest():
                    v = pending.pop(0)
                    S["hi"] += 1
                    dve.wait_ge(handoff["h_hi"], S["hi"])
                    v_.tensor_tensor(xL[v], xr[v], plain(hH[v]), ALU.subtract)

                for i, (c0, rows) in enumerate(tiles):
                    for e in range(2):
                        if len(pending) > 3:
                            rest()
                        pending.append((slice(None), slice(4 * e, 4 * e + 4), slice(c0, c0 + rows)))
                        t = tr("D").rearrange("p (c t) -> p c t", c=4)[:, :, 0:rows]
                        gain = gains[:, 4 * e:4 * e + 4, g:g + 1].to_broadcast([128, 4, rows])
                        v_.tensor_tensor(xr[pending[-1]], t, gain, ALU.mult).then_inc(tr_dve, 1)
                        dve.drain().then_inc(handoff["h_raw"], 1)
                while pending:
                    rest()

            def add_to_x(name):
                for b, _ in enumerate(blocks(name)):
                    for i, (c0, rows) in enumerate(COLS):
                        for v in banks("D", 1):
                            xs = x[0:rows, i, 512 * b:512 * b + 512]
                            v_.tensor_tensor(xs, xs, v[0:rows, :], ALU.add).then_inc(proj_dve, 1)

            def rotate(t, table, half, heads, tmp="ropet"):
                rows = t.shape[0]
                a = L[tmp][0:rows, 0, 0:heads * 2 * half].rearrange("p (h d) -> p h d", h=heads)
                b = L[tmp][0:rows, 1, 0:heads * 2 * half].rearrange("p (h d) -> p h d", h=heads)
                bc = lambda s, lo, hi: table[:, s, lo:hi].unsqueeze(1).to_broadcast([rows, heads, hi - lo])
                v_.tensor_tensor(a, t[:, :, 0:2 * half], bc(0, 0, 2 * half), ALU.mult)
                v_.tensor_tensor(b[:, :, 0:half], t[:, :, half:2 * half], bc(1, 0, half), ALU.mult)
                step(v_.tensor_tensor(b[:, :, half:2 * half], t[:, :, 0:half], bc(1, half, 2 * half), ALU.mult))
                step(v_.tensor_tensor(t[:, :, 0:2 * half], a, b, ALU.add))

            def attend(count, rowmax, normal, outs, copy, prep=None):
                def start(j):
                    n = S["job"] + j
                    if prep:
                        prep(j)
                    dve.wait_ge(scores_ready, n + 1)
                    rowmax(j, n, sreg(n))

                start(0)
                for j in range(count):
                    n = S["job"] + j
                    dve.wait_ge(exp_done, n + 1)
                    normal(j, n, P[n % 2])
                    if j + 1 < count:
                        start(j + 1)
                    outs(j)
                    dve.wait_ge(out_ready, n + 1)
                    copy(j, sreg(n))
                S["job"] += count

            def split_out(at, s):
                step(v_.tensor_copy(oH[at], s))
                v_.tensor_tensor(xL[at], s, plain(oH[at]), ALU.subtract).then_inc(out_copied, 1)

            def biased(n, out, in_, scale, k):
                step(v_.tensor_reduce(out=mx2[n % 2][:, 0:k], in_=in_, axis=AX.X, op=ALU.max))
                v_.tensor_scalar(nm2[n % 2][:, 0:k], mx2[n % 2][:, 0:k], -scale, None, ALU.mult).then_inc(rowmax_ready, 1)

            def two_max(scale, width):
                def run(j, n, s):
                    biased(n, None, s[:, 0:1024].rearrange("p (e s) -> p e s", e=2)[:, :, 0:width(j)], scale, 2)
                return run

            def one_max(scale):
                return lambda j, n, s: biased(n, None, s[:, 0:1088], scale, 1)

            dve.wait_ge(first_in, FIRST)
            v_.memset(misc[:, :], EPS)
            step(v_.memset(stat[:, :], 1.0))
            v_.tensor_copy(lev[:, :], L["lev_in"])
            v_.tensor_copy(identb[:, :], ident)
            v_.tensor_copy(causalb[:, :], const("causal"))
            v_.tensor_copy(newmaskb[:, :], const("newmask"))
            tr_copy("D", gains[:, :, :], view=lambda t: t[:, 0:64].rearrange("p (c g) -> p c g", c=8))
            t = tr("D")
            v_.tensor_copy(small[:, :], t[:, 0:10]).then_inc(tr_dve, 1)
            lr = L["lrow"]
            step(v_.tensor_tensor(L["lp"], lr[:, 0:4:2, :], lr[:, 1:4:2, :], ALU.mult))
            v_.tensor_reduce(out=L["ls"][:, 0:2], in_=L["lp"], axis=AX.X, op=ALU.add).then_inc(handoff["lam_in"], 1)
            dve.wait_ge(handoff["lam_e"], 1)
            step(v_.tensor_tensor(L["ld"], L["le"][:, 0:1], L["le"][:, 1:2], ALU.subtract))
            step(v_.tensor_scalar(lam, L["ld"], LAM_INIT, None, ALU.add))
            ms_ = const("mapsel")
            step(v_.tensor_scalar(L["ld"], ms_[:, 1:2], lam, -1.0, ALU.mult, ALU.mult))
            step(v_.tensor_tensor(sgn, L["ld"], ms_[:, 0:1], ALU.add))
            dve.wait_ge(tr_dve, 2)
            v_.tensor_scalar(subg, small[:, 0:1], 1.0 - LAM_INIT, None, ALU.mult)
            step(v_.tensor_tensor(L["lbm"], small[:, 2:6], small[:, 6:10], ALU.max))
            v_.tensor_tensor(L["lbd"][:, 0:4], small[:, 2:6], L["lbm"], ALU.subtract)
            v_.tensor_tensor(L["lbd"][:, 4:8], small[:, 6:10], L["lbm"], ALU.subtract).then_inc(handoff["lam_in"], 1)
            dve.wait_ge(handoff["lam_e"], 2)
            step(v_.tensor_tensor(L["lbm"], L["lbe"][:, 0:4], L["lbe"][:, 4:8], ALU.add))
            step(v_.reciprocal(L["lbr"], L["lbm"]))
            step(v_.tensor_tensor(lb, L["lbe"][:, 0:4], L["lbr"], ALU.mult))
            step(v_.tensor_scalar(omlb, lb, -1.0, 1.0, ALU.mult, ALU.add))
            barrier()

            ahead(3)
            normalise(COLS, 0)
            barrier()
            for b, _ in enumerate(blocks("a_in")):
                for i, (c0, rows) in enumerate(COLS):
                    n = pj.add("A")
                    if b == 1:
                        dve.wait_ge(proj_act, pj.count("A", n + 1))
                        rotate(L["a_qk"][0:rows, i, :].rearrange("p (h d) -> p h d", h=16), rope8[0:rows, i], 8, 16)
            barrier()
            for i, (c0, rows) in enumerate(COLS):
                tr_copy("D", L["qT_a"][:, :, c0:c0 + rows], view=lambda t: t.rearrange("p (h t) -> p h t", h=H)[:, :, 0:rows])
                tr("A")
            step(v_.memset(L["qz_a"], 0.0))
            dve.wait_ge(tr_dve, tj.count("D", len(tj.who)))
            for m in range(2):
                r = slice(64 * m, 64 * m + 64)
                for b in range(NB):
                    v_.tensor_copy(L["qz_a"][r, b, :, 8 * m:8 * m + 8], L["qT_a"][r, :, SEQ + 8 * b:SEQ + 8 * b + 8])
            barrier()

            def ap_normal(j, n, p):
                w = (JOBS_AP[j][0] + 1) * 128
                r = rs2[n % 2]
                step(v_.reciprocal(r[:, 0:2], sm2[n % 2][:, 0:2]))
                step(v_.tensor_scalar(r[:, 2:3], r[:, 1:2], lam, -1.0, ALU.mult, ALU.mult))
                step(v_.tensor_scalar(p[:, 0:w], p[:, 0:w], r[:, 0:1], None, ALU.mult))
                v_.scalar_tensor_tensor(out=p[:, 0:w], in0=p[:, 512:512 + w], scalar=r[:, 2:3], in1=p[:, 0:w],
                                        op0=ALU.mult, op1=ALU.add).then_inc(probs_ready, 1)

            def ap_copy(j, s):
                i, h = JOBS_AP[j]
                v_.tensor_copy(oT[:, h, i * 128:i * 128 + 128], s[:, 0:128]).then_inc(out_copied, 1)

            attend(16, two_max(64 ** -0.5, lambda j: (JOBS_AP[j][0] + 1) * 128), ap_normal, lambda j: tr("A"), ap_copy)

            def as_prep(b):
                for half in range(2):
                    for h in range(H):
                        tr_copy("A" if h % 2 else "D", L["KT_a"][:, h, half * 512:half * 512 + 512])

            def as_normal(j, n, p):
                r = rs2[n % 2]
                step(v_.reciprocal(r[:, 0:1], sm2[n % 2][:, 0:1]))
                v_.tensor_scalar(p[:, 0:1088], p[:, 0:1088], r[:, 0:1], sgn, ALU.mult, ALU.mult).then_inc(probs_ready, 1)

            def past_outs(j):
                tr_copy("D", PT[:, 0:4, :], view=lambda t: t.rearrange("p (c q) -> p c q", c=4))
                tr("A")
                t = tr("D")
                v_.tensor_copy(PT[0:64, 8, :], t[0:64, 0:128]).then_inc(tr_dve, 1)

            def as_copy(b, s):
                o = s[:, 0:64].rearrange("p (h m q) -> p h q m", h=H, m=2)
                v_.tensor_reduce(out=oT[:, 0:H, SEQ + 8 * b:SEQ + 8 * b + 8], in_=o, axis=AX.X, op=ALU.add).then_inc(out_copied, 1)

            attend(NB, one_max(64 ** -0.5), as_normal, past_outs, as_copy, as_prep)
            barrier()
            pass_by("b_gates", 5)
            pass_by("b_values", 5)
            barrier()
            HQ, HK, QK, B, ATT, SS = (L[k] for k in ("HQ", "HK", "QK", "B", "ATT", "SS"))
            for e in range(H):
                ins = v_.tensor_scalar(HK[:, e, :], HK[:, e, :], omlb[:, e:e + 1], lb[:, e:e + 1], ALU.mult, ALU.add)
            step(ins)
            v_.tensor_scalar(B, HK, 1e-19, None, ALU.max).then_inc(handoff["f_ready"], 1)
            v_.tensor_scalar(HK, HK, -1.0, 1.0, ALU.mult, ALU.add)
            v_.tensor_scalar(HQ, HQ, 128 ** -0.5, None, ALU.mult).then_inc(handoff["qk_ready"], 1)
            v_.memset(ATT, 0.0)
            dve.wait_ge(handoff["logf"], 1)
            for e in range(H):
                ins = v_.tensor_tensor_scan(out=B[:, e, :], data0=const("reset"), data1=QK[:, e, :], initial=0.0,
                                            op0=ALU.mult, op1=ALU.add)
            step(ins)

            def attend_level(n, h):
                mask = levels[:, n, :]
                for i, (c0, rows) in enumerate(COLS):
                    if i == 4 and h > 4:
                        continue
                    for v in banks("D", 1):
                        m = mask[0:rows, 0:rows].unsqueeze(1).to_broadcast([rows, H, rows])
                        v_.copy_predicated(ATT[0:rows, i, :, 0:rows], m,
                                           v[0:rows].rearrange("p (h t) -> p h t", h=H)[:, :, 0:rows]).then_inc(proj_dve, 1)

            for n, h in enumerate(LEVELS):
                if h:
                    w = TOK if h <= 4 else SEQ
                    nb = w // (2 * h)
                    cut = lambda t: t[:, :, 0:w].rearrange("p e (n s) -> p e n s", s=2 * h)
                    anchor = cut(B)[:, :, :, h - 1:h].to_broadcast([128, H, nb, h])
                    dve.wait_ge(handoff["qk_used"], n)
                    v_.tensor_tensor(cut(QK)[:, :, :, h:2 * h], cut(B)[:, :, :, h:2 * h], anchor, ALU.subtract)
                    v_.tensor_tensor(cut(QK)[:, :, :, 0:h], anchor, cut(B)[:, :, :, 0:h], ALU.subtract)\
                        .then_inc(handoff["decay_d"], 1)
                    attend_level(n - 1, LEVELS[n - 1])
                    dve.wait_ge(handoff["decay_e"], n)
                    v_.tensor_tensor(cut(QK)[:, :, :, h:2 * h], cut(QK)[:, :, :, h:2 * h], cut(HQ)[:, :, :, h:2 * h], ALU.mult)
                    v_.tensor_tensor(cut(QK)[:, :, :, 0:h], cut(QK)[:, :, :, 0:h], cut(HK)[:, :, :, 0:h], ALU.mult)\
                        .then_inc(handoff["qk_ready"], 1)
            attend_level(len(LEVELS) - 1, LEVELS[-1])
            barrier()
            for w, n, a in ((128, 4, 0), (TS, NB, SEQ)):
                cut = lambda t: t[:, :, a:a + w * n].rearrange("p e (n s) -> p e n s", s=w)
                ins = v_.tensor_tensor(cut(QK), cut(B)[:, :, :, w - 1:w].to_broadcast([128, H, n, w]), cut(B), ALU.subtract)
            ins.then_inc(handoff["decay_d"], 1)
            dve.wait_ge(handoff["decay_e"], len(LEVELS))
            v_.tensor_tensor(QK, QK, HK, ALU.mult).then_inc(handoff["qk_ready"], 1)
            for i in range(5):
                tr("A")
            barrier()
            dve.wait_ge(handoff["decay_e"], len(LEVELS) + 1)
            for i in range(4):
                for v in banks("D", 1):
                    new = v.rearrange("p (h v) -> p h v", h=H)
                    if i == 0:
                        ins = v_.tensor_copy(SS[:, 0], new)
                        ins.then_inc(proj_dve, 1)
                        dve.wait_ge(proj_dve, pj.count("D", len(pj.who)))
                    else:
                        dec = QK[:, :, i * 128 + 127:i * 128 + 128].to_broadcast([128, H, 128])
                        step(v_.tensor_tensor(SS[:, i], SS[:, i - 1], dec, ALU.mult))
                        v_.tensor_tensor(SS[:, i], SS[:, i], new, ALU.add).then_inc(proj_dve, 1)
                        dve.wait_ge(proj_dve, pj.count("D", len(pj.who)))
            step(v_.tensor_copy(L["edec"], QK[:, :, SEQ + TS - 1:TOK:TS]))
            step(v_.tensor_tensor(QK, QK, HQ, ALU.mult))
            barrier()
            for i in range(5):
                pj.add("A")
            dve.wait_ge(rows_in, ROWS["hgrn"])
            dve.wait_ge(proj_act, pj.count("A", len(pj.who)))
            for e in range(H):
                if e >= 2:
                    dve.wait_ge(proj_done, len(pj.who))
                v_.tensor_tensor(L["Vz"][0:64, e % 2, :].rearrange("p (b v) -> p b v", b=NB),
                                 L["ib"][0:64, 4, e * 128:e * 128 + 128].unsqueeze(1).to_broadcast([64, NB, 128]),
                                 const("rowmask", 64).unsqueeze(2).to_broadcast([64, NB, 128]), ALU.mult)\
                    .then_inc(handoff["kd_ready"], 1)
                s0 = L["S0"][:, :, e, :]
                step(v_.tensor_tensor(s0, s0, L["edec"][:, e, :].unsqueeze(2).to_broadcast([128, NB, 128]), ALU.mult))
                for c in range(2):
                    for v in banks("D", 1):
                        s = L["S0"][:, 4 * c:4 * c + 4, e, :]
                        v_.tensor_tensor(s, s, v.rearrange("p (b v) -> p b v", b=4), ALU.add).then_inc(proj_dve, 1)
            barrier()
            def o_rest(c):
                dve.wait_ge(handoff["o_hi"], c + 1)
                v_.tensor_tensor(xL[:, c, :], L["rt"][:, c % 2, :], plain(oH[:, c, :]), ALU.subtract).then_inc(handoff["onorm_done"], 1)

            for c in range(KC):
                dve.wait_ge(handoff["onorm_root"], c + 1)
                r = L["rt"][:, c % 2, :]
                step(v_.reciprocal(r, r))
                if c < 4:
                    v_.scalar_tensor_tensor(out=r, in0=oT[:, c, :], scalar=subg, in1=r, op0=ALU.mult,
                                            op1=ALU.mult).then_inc(handoff["o_raw"], 1)
                else:
                    step(v_.scalar_tensor_tensor(out=r, in0=L["OB"][:, c - 4, :], scalar=small[:, 1:2], in1=r,
                                                 op0=ALU.mult, op1=ALU.mult))
                    v_.tensor_tensor(r, oT[:, c, :], r, ALU.mult).then_inc(handoff["o_raw"], 1)
                if c > 0:
                    o_rest(c - 1)
            o_rest(KC - 1)
            barrier()
            add_to_x("ab_out")
            barrier()

            def cross_and_ffn(l):
                normalise(COLS, 2 + l)
                barrier()
                pass_by(f"xq{l}", 5)
                normalise(COLS[0:2], 4 + l)
                barrier()
                pass_by(f"xk{l}", 2)
                pass_by(f"xv{l}", 2)
                barrier()
                for i in range(4):
                    tr("A")
                step(v_.memset(L["qzx"], 0.0))
                for c in range(KC):
                    v_.tensor_copy(L["qzx"][:, c, :].rearrange("p (b w) -> p b w", w=72)[:, :, 0:8],
                                   L["qxT"][:, c, SEQ:TOK].rearrange("p (b t) -> p b t", b=NB))
                barrier()

                def xp_normal(j, n, p):
                    r = rs2[n % 2]
                    step(v_.reciprocal(r[:, 0:4], sm2[n % 2][:, 0:4]))
                    pv = p[:, 0:1024].rearrange("p (h m) -> p h m", h=4)
                    v_.tensor_tensor(pv, pv, r[:, 0:4].unsqueeze(2).to_broadcast([128, 4, 256]), ALU.mult)\
                        .then_inc(probs_ready, 1)

                def xp_copy(i, s):
                    split_out((slice(None), slice(None), slice(i * 128, i * 128 + 128)),
                              s[:, 0:1024].rearrange("p (c q) -> p c q", c=8))

                attend(4, lambda j, n, s: biased(n, None, s[:, 0:1024].rearrange("p (h m) -> p h m", h=4), 256 ** -0.5, 4),
                       xp_normal, lambda j: (tr("A"), tr("A")), xp_copy)

                def xs_prep(j):
                    for b in range(NB):
                        for g in range(4):
                            tr_copy("A" if g % 2 else "D", [L["mkK"], L["mkT"]][b % 2][:, 2 * g:2 * g + 2, :],
                                    view=lambda t: t.rearrange("p (c m) -> p c m", c=2))

                def xs_normal(j, n, p):
                    r = rs2[n % 2]
                    step(v_.reciprocal(r[:, 0:2], sm2[n % 2][:, 0:2]))
                    pv = p[:, 0:512].rearrange("p (h m) -> p h m", h=2)
                    v_.tensor_tensor(pv, pv, r[:, 0:2].unsqueeze(2).to_broadcast([128, 2, 256]), ALU.mult)\
                        .then_inc(probs_ready, 1)

                def xs_copy(i, s):
                    split_out((slice(None), slice(None), slice(SEQ, TOK)), s[:, 0:512].rearrange("p (c q) -> p c q", c=8))

                attend(1, lambda j, n, s: biased(n, None, s[:, 0:1024].rearrange("p (h m) -> p h m", h=2)[:, :, 0:256],
                                                 256 ** -0.5, 2), xs_normal, lambda j: tr("A"), xs_copy, xs_prep)
                barrier()
                add_to_x(f"xo{l}")
                barrier()
                normalise(COLS, 6 + l)
                for c in range(0, FC, 4):
                    m = min(4, FC - c)
                    tr_copy("D", L["fcol"][:, c:c + m, :], view=lambda t: t[:, 0:m * 20].rearrange("p (c r) -> p c r", c=m))
                barrier()
                fcol, gc, sil, gcs, sils, gs, cst_ = (L[k] for k in ("fcol", "gc", "sil", "gcs", "sils", "gs", "cstate"))
                for part, (first_chunk, _) in enumerate(HALF):
                    for j, _ in enumerate(blocks(f"up{l}{part}")):
                        first = len(pj.who)
                        us = [pj.add("D") for _ in range(5)]
                        k = S["ffn"]
                        S["ffn"] += 1
                        c = first_chunk + 2 * j
                        for e in range(2):
                            w = lambda r: fcol[:, c + e, 16 + r:17 + r]
                            g, main = gc[:, e], bank(us[e])
                            dve.wait_ge(proj_done, first + e + 1)
                            if k > 0:
                                dve.wait_ge(handoff["silu_done"], 3 * k - 2 + e)
                            step(v_.tensor_scalar(g, main, w(2), w(3), ALU.mult, ALU.add))
                            step(v_.scalar_tensor_tensor(out=g[:, 1:SEQ], in0=main[:, 0:SEQ - 1], scalar=w(1), in1=g[:, 1:SEQ],
                                                         op0=ALU.mult, op1=ALU.add))
                            v_.scalar_tensor_tensor(out=g[:, 2:SEQ], in0=main[:, 0:SEQ - 2], scalar=w(0), in1=g[:, 2:SEQ],
                                                    op0=ALU.mult, op1=ALU.add).then_inc(handoff["gate_done"], 1)
                            v_.tensor_copy(cst_[:, c + e, 0:2], main[:, SEQ - 2:SEQ]).then_inc(proj_dve, 1)
                        dve.wait_ge(proj_done, first + 5)
                        samp = bank(us[4])
                        if k > 0:
                            dve.wait_ge(handoff["silu_done"], 3 * k)
                        v_.tensor_copy(gs[:, :, :, 0:2], fcol[:, c:c + 2, 0:16].rearrange("p e (b w) -> p e b w", b=NB))
                        step(v_.tensor_copy(gs[:, :, :, 2:10], samp[:, 0:128].rearrange("p (e b t) -> p e b t", e=2, b=NB)))
                        v_.tensor_copy(cst_[:, c:c + 2, 2:18].rearrange("p e (b w) -> p e b w", b=NB), gs[:, :, :, 8:10])
                        for r in (2, 1, 0):
                            for e in range(2):
                                w = lambda r: fcol[:, c + e, 16 + r:17 + r]
                                g = gcs[:, e].rearrange("p (b t) -> p b t", b=NB)
                                if r == 2:
                                    ins = v_.tensor_scalar(g, gs[:, e, :, 2:10], w(2), w(3), ALU.mult, ALU.add)
                                else:
                                    ins = v_.scalar_tensor_tensor(out=g, in0=gs[:, e, :, r:r + 8], scalar=w(r), in1=g,
                                                                  op0=ALU.mult, op1=ALU.add)
                            if r > 0:
                                step(ins)
                            else:
                                ins.then_inc(handoff["gate_done"], 1)
                                dve.wait_ge(handoff["gate_done"], 3 * k + 3)
                        ahead(S["slot"] + 3)
                        for e, (s_, u) in enumerate(((sil[:, 0], bank(us[2])), (sil[:, 1], bank(us[3])),
                                                     (sils, samp[:, 128:256].rearrange("p (e t) -> p e t", e=2)))):
                            dve.wait_ge(handoff["silu_done"], 3 * k + e + 1)
                            v_.tensor_tensor(s_, s_, u, ALU.mult).then_inc(handoff["prod_done"], 1)
                        dve.drain().then_inc(proj_dve, 3)
                        for e, (at, src) in enumerate((((slice(None), 2 * j, slice(0, SEQ)), sil[:, 0]),
                                                       ((slice(None), 2 * j + 1, slice(0, SEQ)), sil[:, 1]),
                                                       ((slice(None), slice(2 * j, 2 * j + 2), slice(SEQ, TOK)), sils))):
                            dve.wait_ge(handoff["act_hi"], 3 * k + e + 1)
                            v_.tensor_tensor(aL[at], src, plain(aH[at]), ALU.subtract).then_inc(handoff["prod_done"], 1)
                    barrier()
                    add_to_x(f"down{l}{part}")
                    if part == 0:
                        barrier()
                for c in range(0, FC, 4):
                    tr("A")
                barrier()

            cross_and_ffn(0)

            normalise(COLS, 1)
            barrier()
            pass_by("c_idx", 5)
            dve.wait_ge(rows_in, ROWS["ikn"])
            S["norms"] += 1
            dve.wait_ge(squares, S["norms"])
            v_.tensor_scalar(ms, ss, 1.0 / 64, EPS, ALU.mult, ALU.add).then_inc(means, 1)
            dve.wait_ge(roots, S["norms"])
            v_.reciprocal(rstd, sd).then_inc(rstds, 1)
            dve.wait_ge(rstds, S["norms"])
            for i, (c0, rows) in enumerate(COLS):
                k = L["i_tm"][0:rows, i, 512:576]
                step(v_.scalar_tensor_tensor(out=k, in0=k, scalar=rstd[0:rows, i:i + 1], in1=L["ikn"][0:rows, :],
                                             op0=ALU.mult, op1=ALU.mult))
                rotate(L["i_tm"][0:rows, i, 0:576].rearrange("p (h d) -> p h d", h=9), rope8[0:rows, i], 8, 9, "ropet_i")
                iw = L["i_tm"][0:rows, i, 576:584]
                step(v_.tensor_scalar(iw, iw, 512 ** -0.5, None, ALU.mult))
            barrier()
            for i, (c0, rows) in enumerate(COLS):
                tr_copy("D", L["iqT"][0:64, 0:4, c0:c0 + rows],
                        view=lambda t: t[0:64].rearrange("p (h t) -> p h t", h=4)[:, :, 0:rows])
                tr("A")
            for i, (c0, rows) in enumerate(COLS):
                tr_copy("D", L["ikT"][0:64, c0:c0 + rows], view=lambda t: t[0:64, 0:rows])
            tr_copy("D", L["iwT"][0:8, :], view=lambda t: t[0:8, 0:64])
            dve.wait_ge(tr_act, tj.count("A", len(tj.who)))
            dve.wait_ge(tr_dve, tj.count("D", len(tj.who)))
            v_.tensor_copy(L["iqs"][0:64].rearrange("p b (h q) -> p h b q", h=8),
                           L["iqT"][0:64, :, SEQ:TOK].rearrange("p h (b q) -> p h b q", b=NB))
            barrier()
            step(v_.memset(L["wz"], 0.0))
            for v in banks("D", 1):
                v_.tensor_tensor(L["wz"][0:64, :].rearrange("p (b w) -> p b w", w=72)[:, :, 0:8],
                                 v[0:64, 0:64].rearrange("p (b t) -> p b t", b=NB),
                                 const("sameq", 64).rearrange("p (b t) -> p b t", b=NB), ALU.mult).then_inc(proj_dve, 1)
            k = 0
            for i in range(1, 4):
                n = (i + 1) * 128
                isc = L["iscp"][i - 1]
                for h in range(8):
                    pj.add("A")
                    dve.wait_ge(proj_act, pj.count("A", len(pj.who)))
                    w = L["i_tm"][:, i, 576 + h:577 + h]
                    r = L["relup"][:, k % 2, 0:n]
                    if h == 0:
                        ins = v_.tensor_scalar(isc, r, w, None, ALU.mult)
                    else:
                        ins = v_.scalar_tensor_tensor(out=isc, in0=r, scalar=w, in1=isc, op0=ALU.mult, op1=ALU.add)
                    k += 1
                    ins.then_inc(handoff["relu_used"], 1)
                    dve.wait_ge(handoff["relu_used"], k)
                step(v_.tensor_tensor(isc[:, n - 128:n], isc[:, n - 128:n], const("causal"), ALU.add))
            dve.drain().then_inc(handoff["wz_ready"], 1)
            barrier()
            for b in range(NB):
                if b == 0:
                    tr_copy("D", L["IKT"][0:64, 0, 0:512], view=lambda t: t[0:64])
                    tr("A")
                if b + 1 < NB:
                    tr_copy("D", L["IKT"][0:64, (b + 1) % 2, 0:512], view=lambda t: t[0:64])
                    tr("A")
            dve.wait_ge(handoff["relu_used"], 24 + NB)
            s = sreg(1)
            v_.tensor_copy(L["iscs"][0:64, 0:1024], s[0:64, 0:1024])
            v_.tensor_tensor(L["iscs"][0:64, 1024:1088], s[0:64, 1024:1088], const("block64", 64), ALU.add)
            barrier()

            def select(isc, out, rows, n, k):
                work, top, eq, rank = L["work"][0:rows, 0:n], L["top"][0:rows, :], L["eq"][0:rows, 0:n], L["rank"][0:rows, 0:n]
                c = L["cnt"][0:rows, :]
                src = isc
                for it in range(k // 8):
                    if it % 4 == 3:
                        ahead(min(S["split"] + 1, last_split))
                    step(v_.max(out=top, in_=src))
                    if it < k // 8 - 1:
                        step(v_.match_replace(out=work, in_to_replace=top, in_values=src, imm_value=-3e38))
                        src = work
                t = top[:, 7:8]
                step(v_.tensor_scalar(eq, isc, t, None, ALU.is_gt, ALU.add, accum_out=c[:, 0:1]))
                step(v_.tensor_scalar(c[:, 1:2], c[:, 0:1], -1.0, float(k), ALU.mult, ALU.add))
                step(v_.tensor_scalar(work, isc, t, None, ALU.is_equal))
                step(v_.tensor_tensor_scan(out=rank, data0=work, data1=work, initial=0.0, op0=ALU.add, op1=ALU.bypass))
                step(v_.tensor_scalar(rank, rank, c[:, 1:2], None, ALU.is_le))
                step(v_.tensor_tensor(work, work, rank, ALU.mult))
                step(v_.tensor_tensor(work, work, eq, ALU.add))
                step(v_.tensor_scalar(out, work, -NEG, NEG, ALU.mult, ALU.add))

            last_split = S["slot"] + 12 + 3
            assert len(ORDER["c_qkv"]) * len(ORDER["c_qkv"][0]) == 12
            for i in range(1, 4):
                select(L["iscp"][i - 1], L["selp"][i - 1], 128, (i + 1) * 128, 128)
            select(L["iscs"][0:64, :], L["sels"][0:64, :], 64, 1088, 256)
            v_.tensor_copy(L["expb"][0:64, :], const("expand", 64))
            for b, _ in enumerate(blocks("c_qkv")):
                for i, (c0, rows) in enumerate(COLS):
                    n = pj.add("A")
                    if b == 2:
                        dve.wait_ge(proj_act, pj.count("A", n + 1))
                        rotate(L["c_tm"][0:rows, i, :].rearrange("p (h d) -> p h d", h=10), rope16[0:rows, i], 16, 10, "ropet_c")
            barrier()
            for i, (c0, rows) in enumerate(COLS):
                tr("A")
                tr_copy("D", L["qT_c"][:, 4:8, c0:c0 + rows], view=lambda t: t.rearrange("p (h t) -> p h t", h=4)[:, :, 0:rows])
                tr_copy("D", L["kT_c"][:, :, c0:c0 + rows],
                        view=lambda t: t[:, 0:256].rearrange("p (h t) -> p h t", h=2)[:, :, 0:rows])
            dve.wait_ge(tr_act, tj.count("A", len(tj.who)))
            dve.wait_ge(tr_dve, tj.count("D", len(tj.who)))
            v_.tensor_copy(L["qs_c"].rearrange("p b g (h q) -> p (g h) b q", h=4),
                           L["qT_c"][:, :, SEQ:TOK].rearrange("p h (b q) -> p h b q", b=NB))
            barrier()

            def cp_normal(j, n, p):
                w = (JOBS_CP[j][0] + 1) * 128
                r = rs2[n % 2]
                step(v_.reciprocal(r[:, 0:2], sm2[n % 2][:, 0:2]))
                for e in range(2):
                    ins = v_.tensor_scalar(p[:, 512 * e:512 * e + w], p[:, 512 * e:512 * e + w], r[:, e:e + 1], None, ALU.mult)
                ins.then_inc(probs_ready, 1)

            def cp_copy(j, s):
                i, hp = JOBS_CP[j]
                split_out((slice(None), slice(2 * hp, 2 * hp + 2), slice(i * 128, i * 128 + 128)),
                          s[:, 0:256].rearrange("p (e q) -> p e q", e=2))

            attend(16, two_max(128 ** -0.5, lambda j: (JOBS_CP[j][0] + 1) * 128), cp_normal, lambda j: (tr("A"), tr("A")), cp_copy)

            def cs_prep(p):
                for bb in range(2):
                    for g in range(2):
                        tr_copy("D", L["KT_c"][:, 2 * bb + g, 0:512])
                        tr("A")

            def cs_normal(j, n, p):
                r = rs2[n % 2]
                step(v_.reciprocal(r[:, 0:1], sm2[n % 2][:, 0:1]))
                v_.tensor_scalar(p[:, 0:1088], p[:, 0:1088], r[:, 0:1], None, ALU.mult).then_inc(probs_ready, 1)

            def cs_copy(p, s):
                at = (slice(None), slice(None), slice(SEQ + 16 * p, SEQ + 16 * p + 16))
                v = lambda t: t[at].rearrange("p h (b q) -> p b h q", b=2)
                s = s[:, 0:128].rearrange("p (b h q) -> p b h q", b=2, h=8)
                for bb in range(2):
                    ins = v_.tensor_copy(v(oH)[:, bb], s[:, bb])
                step(ins)
                for bb in range(2):
                    ins = v_.tensor_tensor(v(xL)[:, bb], s[:, bb], plain(v(oH)[:, bb]), ALU.subtract)
                ins.then_inc(out_copied, 1)

            attend(NB // 2, one_max(128 ** -0.5), cs_normal, past_outs, cs_copy, cs_prep)
            barrier()
            add_to_x("c_out")
            barrier()
            cross_and_ffn(1)
            norm()
            dve.wait_ge(rstds, S["norms"])
            dve.wait_ge(rows_in, ROWS["fin"])
            for i, (c0, rows) in enumerate(COLS):
                xs = x[0:rows, i, :]
                ins = v_.scalar_tensor_tensor(out=xs, in0=xs, scalar=rstd[0:rows, i:i + 1], in1=L["fin"][0:rows, :],
                                              op0=ALU.mult, op1=ALU.mult)
            ins.then_inc(handoff["onorm_done"], 1)


_INS = ["x_prompt", "x_sample", "cache_diff_k", "cache_diff_v", "state_hgrn", "cache_dsa_k", "cache_dsa_v", "cache_dsa_ik",
        "cache_mem_k", "cache_mem_v", "state_ffn_conv", "page_table", "mem_prompt", "norm_mix", "w_in_ab", "diff_lq1",
        "diff_lk1", "diff_lq2", "diff_lk2", "diff_subln", "hgrn_lb_logits", "hgrn_onorm", "w_out_ab", "w_in_c",
        "idx_k_norm", "w_out_c", "norm_x", "norm_mem", "w_xq", "w_xk", "w_xv", "w_xo", "norm_ffn", "w_ffn_in",
        "conv_ffn_w", "conv_ffn_b", "w_ffn_out", "norm_final"]
_OUTS = [("y_p", (1, 512, 1024)), ("y_s", (8, 8, 1024)), ("diff_k_p", (1, 1, 512, 4, 128)), ("diff_v_p", (1, 1, 512, 4, 128)),
         ("hgrn_p", (1, 1, 4, 128, 128)), ("dsa_k_p", (1, 1, 512, 2, 128)), ("dsa_v_p", (1, 1, 512, 2, 128)),
         ("dsa_ik_p", (1, 1, 512, 64)), ("mem_k", (2, 1, 256, 4, 256)), ("mem_v", (2, 1, 256, 4, 256)),
         ("conv_p", (2, 1, 2, 2816)), ("diff_k_s", (1, 8, 8, 4, 128)), ("diff_v_s", (1, 8, 8, 4, 128)),
         ("hgrn_s", (1, 8, 4, 128, 128)), ("dsa_k_s", (1, 8, 8, 2, 128)), ("dsa_v_s", (1, 8, 8, 2, 128)),
         ("dsa_ik_s", (1, 8, 8, 64)), ("conv_s", (2, 8, 2, 2816))]


def kernel(**inputs):
    import concourse.bacc as _bacc
    from concourse.bass_utils import run_bass_kernel_spmd as _run

    nc = _bacc.Bacc("TRN2", target_bir_lowering=False, num_devices=1)
    arrays, A, O = {}, {}, {}
    for name in _INS:
        a = np.ascontiguousarray(inputs[name])
        arrays[f"in_{name}"] = a
        A[name] = nc.dram_tensor(f"in_{name}", a.shape, mybir.dt.from_np(a.dtype), kind="ExternalInput").ap()
    for name, a in zip(("consts", "levels"), constants()):
        arrays[f"in_{name}"] = a
        A[name] = nc.dram_tensor(f"in_{name}", a.shape, mybir.dt.from_np(a.dtype), kind="ExternalInput").ap()
    for name, shape in _OUTS:
        ap = nc.dram_tensor(f"out_{name}", shape, mybir.dt.float32, kind="ExternalOutput").ap()
        if name in ("diff_k_p", "diff_v_p", "hgrn_p", "dsa_k_p", "dsa_v_p", "dsa_ik_p"):
            ap = ap[0, 0]
        elif name in ("y_p", "diff_k_s", "diff_v_s", "hgrn_s", "dsa_k_s", "dsa_v_s", "dsa_ik_s"):
            ap = ap[0]
        elif name in ("mem_k", "mem_v", "conv_p"):
            ap = ap[:, 0]
        O[name] = ap
    build(nc, A, O)
    r = _run(nc, [arrays], core_ids=[0])
    return tuple(r.results[0][f"out_{name}"] for name, _ in _OUTS)
```

```python
import math
import numpy as np
import concourse.bass as bass
from concourse import mybir
from contextlib import ExitStack

D = 1024
SEQ = 512
NB, TS = 8, 8
NSAMP = NB * TS
TOK = SEQ + NSAMP
NTILE = 5
PAST, PAGE = 1024, 128
NPAGE = PAST // PAGE
DEPTH = 2
H = 4
DFF = 2816
KC = D // 128
FC = DFF // 128
NMEM = 256
EPS = 1e-6
NEG = -1e30
LAM_INIT = 0.8 - 0.6 * math.exp(-0.3 * 0)
THETA = 500000.0
COLS = [(i * 128, 128) for i in range(4)] + [(SEQ, NSAMP)]
WC_Q, WC_K, WC_V, WC_IQ, WC_IK, WC_IW, WC_END = 0, 1024, 1280, 1536, 2048, 2112, 2120

CONST = {}
_at = 0
for _name, _n in (("ident", 128), ("ones", 128), ("causal", 128), ("newmask", 120), ("expand", 512),
                  ("rope8", 5 * 2 * 16), ("rope16", 5 * 2 * 32), ("reset", TOK), ("heads", 64), ("sameq", 64),
                  ("block64", 64), ("rowmask", 8), ("mapsel", 2)):
    CONST[_name] = (_at, _n)
    _at += _n
NCONST = _at
LEVELS = [0, 1, 2, 4, 8, 16, 32, 64]


def constants():
    c = np.zeros((128, NCONST), np.float32)

    def put(name, a):
        at, n = CONST[name]
        c[:a.shape[0], at:at + n] = a.reshape(a.shape[0], n)

    r = np.arange(128)
    put("ident", np.eye(128, dtype=np.float32))
    put("ones", np.full((128, 128), 1.0 / 128, np.float32))
    put("causal", np.where(r[None, :] <= r[:, None], 0.0, NEG).astype(np.float32))
    off = np.arange(120)[None, :] - 56
    put("newmask", np.where((off >= 0) & (off <= (r % 8)[:, None]), 0.0, NEG).astype(np.float32))
    e = np.zeros((64, 4, 128), np.float32)
    for p in range(4):
        for row in range(128):
            e[(2 * p + row // 64) * 8 + row % 8, p, row] = 1.0
    put("expand", e)
    pos = np.zeros((128, 5), np.float32)
    pos[:, :4] = np.arange(512).reshape(4, 128).T
    pos[:64, 4] = PAST + np.arange(64) % TS
    for name, half in (("rope8", 8), ("rope16", 16)):
        inv = np.exp(np.arange(half, dtype=np.float32) * np.float32(-math.log(THETA) / half)).astype(np.float32)
        ang = (pos[:, :, None] * inv).astype(np.float32)
        co, si = np.cos(ang), np.sin(ang)
        put(name, np.stack([np.concatenate([co, co], -1), np.concatenate([-si, si], -1)], 2).astype(np.float32))
    reset = np.ones(TOK, np.float32)
    reset[0:SEQ:128] = 0.0
    reset[SEQ::TS] = 0.0
    put("reset", np.tile(reset, (128, 1)))
    hq = np.arange(64)
    put("heads", (hq[None, :] // 8 == np.arange(8)[:, None]).astype(np.float32))
    put("sameq", (hq[None, :] % 8 == hq[:, None] % 8).astype(np.float32))
    put("block64", np.where((hq[None, :] // 8 == hq[:, None] // 8) & (hq[None, :] % 8 <= hq[:, None] % 8),
                            0.0, NEG).astype(np.float32))
    put("rowmask", (hq[:, None] // 8 == np.arange(8)[None, :]).astype(np.float32))
    put("mapsel", np.stack([(r % 16 < 8), (r % 16 >= 8)], 1).astype(np.float32))
    s, t = r[:, None], r[None, :]
    lev = np.zeros((128, len(LEVELS), 128), np.float32)
    for i, h in enumerate(LEVELS):
        if h == 0:
            lev[:, i] = s == t
        else:
            lev[:, i] = (s // (2 * h) == t // (2 * h)) & (s // h % 2 == 0) & (t // h % 2 == 1)
    return c, lev.reshape(128, -1)


class Turns:

    def __init__(self):
        self.who = []

    def add(self, w):
        self.who.append(w)
        return len(self.who) - 1

    def align(self, n):
        while len(self.who) % n:
            self.who.append(None)

    def last_use(self, n, banks):
        n -= banks
        while n >= 0 and not self.who[n]:
            n -= banks
        return n if n >= 0 else None

    def uses(self, n):
        return sum(1 for x in self.who[:n] if x)

    def count(self, w, n):
        return sum(1 for x in self.who[:n] if x == w)


class Chain:

    def __init__(self, eng, sem):
        self.eng, self.sem, self.n = eng, sem, 0

    def __call__(self, ins):
        self.n += 1
        ins.then_inc(self.sem, 1)
        self.eng.wait_ge(self.sem, self.n)


def build(nc, A, O):
    f32, bf16, u8, i32, f32r = (mybir.dt.float32, mybir.dt.bfloat16, mybir.dt.uint8, mybir.dt.int32, mybir.dt.float32r)
    ALU, ACT, AX = mybir.AluOpType, mybir.ActivationFunctionType, mybir.AxisListType
    NW, NV, NC_ = 5, 3, 3
    NBANK = 6
    AW = 16640
    ctx = ExitStack()
    with ctx:
        ctx.enter_context(nc.allow_non_contiguous_dma(reason="narrow rows of small operands"))

        def sb(name, shape, dt=f32):
            return ctx.enter_context(nc.sbuf_tensor(name, shape, dt))

        def sem(name):
            return ctx.enter_context(nc.semaphore(name))

        cst = sb("cst", [128, NCONST])
        lev = sb("lev", [128, len(LEVELS) * 128], u8)
        identb = sb("identb", [128, 128], bf16)
        causalb = sb("causalb", [128, 128], bf16)
        newmaskb = sb("newmaskb", [128, 120], bf16)
        x = sb("x", [128, NTILE, D])

        def two(name, shape):
            with nc.sbuf_tensor(name, shape, f32) as plain:
                pass
            return plain, sb(name + "_r", shape, f32r)

        hT, hH = two("hT", [128, KC, TOK])
        xr, xL = two("xr", [128, KC, TOK])
        oT, oH = two("oT", [128, KC, TOK])
        W, WL = two("W", [128, NW, 1024])
        WH = sb("WH", [128, NV, 1024], f32r)
        C = sb("C", [128, NC_, 2048])
        arena, arena_r = two("arena", [128, AW])
        gains = sb("gains", [128, 8, 8])
        small = sb("small", [128, 10])
        misc = sb("misc", [128, 64])
        stat = sb("stat", [128, 80])
        pt = sb("pt", [1, 64], i32)
        gs_t = sb("gs_t", [128, 80])
        edec_t = sb("edec_t", [128, 32])
        PS = ctx.enter_context(nc.psum_tensor("PS", [128, 8 * 512], f32))

        def const(name, rows=128):
            at, n = CONST[name]
            return cst[0:rows, at:at + n]

        ident = const("ident")
        rope8 = const("rope8").rearrange("p (i s c) -> p i s c", i=5, s=2)
        rope16 = const("rope16").rearrange("p (i s c) -> p i s c", i=5, s=2)
        levels = lev[:, :].rearrange("p (l t) -> p l t", t=128)

        def region(at, *shape):
            n = int(np.prod(shape))
            assert at + n <= AW, (at, n, AW)
            v = arena[:, at:at + n]
            if len(shape) == 1:
                return v
            if len(shape) == 2:
                return v.rearrange("p (a b) -> p a b", b=shape[1])
            if len(shape) == 3:
                return v.rearrange("p (a b c) -> p a b c", b=shape[1], c=shape[2])
            return v.rearrange("p (a b c d) -> p a b c d", b=shape[1], c=shape[2], d=shape[3])

        def bank(n):
            return PS[:, (n % NBANK) * 512:(n % NBANK) * 512 + 512]

        FAT = 224
        FPIECES = ((0, 0, 288, FAT, True), (0, 288, TOK, 512, True), (1, 0, 224, 800, False), (1, 224, TOK, 1024, True))

        def fset(n):
            assert n % 3 == 0
            return PS[:, (n % NBANK) * 512:(n % NBANK) * 512 + 1536]

        def fchunks(n):
            return fset(n)[:, FAT:FAT + 2 * TOK].rearrange("p (c t) -> p c t", c=2)

        def tbank(n):
            return PS[:, 3072 + 512 * (n % 2):3584 + 512 * (n % 2)]

        def sreg(j):
            return PS[:, 1536 * (j % 2):1536 * (j % 2) + 1536]

        def job_bank(j, depth):
            return sreg(j) if depth == 2 else PS[:, 1024 * (j % 3):1024 * (j % 3) + 1024]

        oflat = oT[:, :, :].rearrange("p c t -> p (c t)")
        hflat = hT[:, :, :].rearrange("p c t -> p (c t)")
        xflat = xr[:, :, :].rearrange("p c t -> p (c t)")

        hX = hH[:, :, :], xL[:, :, :]
        oX = oH[:, :, :], xL[:, :, :]

        def plain(v):
            return v.bitcast(f32)

        junk = oflat[:, 0:1024]
        xn = [oflat[:, 1024 + 1024 * i:2048 + 1024 * i] for i in range(2)]
        ss, ms, sd, rstd = (stat[:, 8 * i:8 * i + 5] for i in range(4))
        lam = misc[:, 0:1]
        sgn = misc[:, 1:2]
        eps_col = misc[:, 2:3]
        lb, omlb = misc[:, 4:8], misc[:, 8:12]
        subg = misc[:, 12:13]
        mxs, nms, sms, rss = ([stat[:, 32 + 16 * i + 4 * e:36 + 16 * i + 4 * e] for i in range(3)] for e in range(4))

        FH = 12
        FA = 2 * FH * TOK
        P = [region(0, 1088), region(1088, 1088)]
        OS, OSx = region(7424, 128), region(3328, 1024)
        P3, P3x = region(3328, 1024), region(7936, 1024)
        PT = region(2176, 9, 128)
        L = {
            "grow": region(0, 1024), "srow": region(1024, 128), "lrow": region(1280, 4, 64), "lp": region(1536, 2, 64),
            "ls": region(1664, 2), "le": region(1668, 2), "ld": region(1672, 1), "lbm": region(1676, 4),
            "lbd": region(1680, 8), "lbe": region(1688, 8), "lbr": region(1696, 4), "lev_in": region(2048, len(LEVELS) * 128),
            "a_qk": region(3328, 5, 1024), "a_v": region(8448, 5, 512), "qT_a": region(11008, 4, TOK),
            "kT_a": region(13312, 4, TOK), "qz_a": region(15616, 8, 4, 32), "KT_a": region(3328, 4, 1024),
            "ropet": region(0, 2, 256),
            "HQ": region(0, 4, TOK), "HK": region(2304, 4, TOK), "B": region(4608, 4, TOK), "QK": region(6912, 4, TOK), "QK2": xflat[:, 0:4 * TOK].rearrange("p (h t) -> p h t", h=4),
            "ATT": region(9216, 5, 4, 128), "KD": xflat[:, 0:2560].rearrange("p (i h k) -> p i h k", i=5, h=4), "ib": region(11776, 5, 512),
            "SS": region(2304, 4, 4, 128), "Vz": region(0, 2, 1024), "OB": region(4608, 4, TOK),
            "edec": edec_t[:, :].rearrange("p (h b) -> p h b", h=4), "sq": region(9216, 2, TOK), "rt": region(10368, 2, TOK),
            "S0": hflat[:, 0:4096].rearrange("p (b h v) -> p b h v", b=8, h=4),
            "qxT": region(3328, 8, TOK), "mk": region(7936, 2, 1024), "mkK": region(7936, 8, 256), "mv": region(9984, 2, 1024),
            "mkT": region(12032, 8, 256), "qzx": hT[:, :, :],
            "mem": region(0, 2, 1024),
            "frow": region(0, DFF), "cstate": region(FA, FC, 18), "fcol": region(FA + FC * 18, FC, 20),
            "gc": oflat[:, 0:2 * TOK].rearrange("p (e t) -> p e t", e=2),
            "sil": oflat[:, 2 * TOK:4 * TOK].rearrange("p (e t) -> p e t", e=2),
            "gs": gs_t[:, :].rearrange("p (b w) -> p b w", b=8),
            "i_tm": region(0, 5, 584), "iwT": region(2920, 64), "wz": region(2984, TOK), "ikn": region(3560, 64),
            "ikj": region(3624, 64), "ikT": region(3688, TOK), "relup": region(4264, 2, 512), "IKT": region(5288, 2, 1024),
            "relu": region(7336, 2, 1088), "iqs": region(9512, 8, 64), "ropet_i": region(10024, 2, 256), "iqT": oT[:, :, :],
            "iscp": [region(14048, 256), region(14304, 384), region(14688, 512)], "iscs": region(15200, 1088),
            "work": region(0, 1088), "eq": region(1088, 1088), "rank": region(2176, 1088), "top": region(16288, 8),
            "cnt": region(16296, 8),
            "c_tm": region(3328, 5, 1280), "v_c": region(9728, 5, 256), "kT_c": region(11008, 2, TOK), "qT_c": hT[:, :, :],
            "qs_c": region(13536, 8, 2, 32), "KT_c": region(3328, 4, 1024), "ropet_c": region(0, 2, 320),
            "selp": [region(12160 + a, n).bitcast(bf16) for a, n in ((0, 128), (128, 192), (320, 256))],
            "sels": region(12160 + 576, 544).bitcast(bf16), "expb": region(12160 + 1120, 256).bitcast(bf16),
            "fin": C[:, 0, 0:D],
        }
        aH, aL = (arena_r[:, at:at + FH * TOK].rearrange("p (c t) -> p c t", t=TOK) for at in (0, FH * TOK))
        mH, mR = (v[:, at:at + KC * NMEM].rearrange("p (c t) -> p c t", t=NMEM)
                  for v, at in ((arena_r, 12032), (arena, 12032 + KC * NMEM)))
        mX = mH, arena_r[:, 12032 + KC * NMEM:12032 + 2 * KC * NMEM].rearrange("p (c t) -> p c t", t=NMEM)
        FIRST = 16 * 13
        ROWS = {"hgrn": 128, "mem0": 144, "ffn0": 192, "ikn": 208, "mem1": 224, "ffn1": 272}
        JOBS_AP = [(i, h) for i in range(4) for h in range(H)]
        JOBS_CP = [(i, hp) for i in range(4) for hp in range(4)]

        first_in = sem("first_in")
        fin_in = sem("fin_in")
        x_in = sem("x_in")
        pages_in = sem("pages_in")
        rows_in = sem("rows_in")
        w_full = [sem(f"w_full{i}") for i in range(NW)]
        hi_done = sem("hi_done")
        lo_pool = sem("lo_pool")
        lo_done = sem("lo_done")
        w_free = sem("w_free")
        c_full = [sem(f"c_full{i}") for i in range(NC_)]
        c_pool = [sem(f"c_pool{i}") for i in range(NC_)]
        c_free = sem("c_free")
        proj_done = sem("proj_done")
        proj_act = sem("proj_act")
        proj_dve = sem("proj_dve")
        tr_done = sem("tr_done")
        tr_act = sem("tr_act")
        tr_dve = sem("tr_dve")
        squares = sem("squares")
        means = sem("means")
        roots = sem("roots")
        rstds = sem("rstds")
        xn_done = sem("xn_done")
        scores_ready = sem("scores_ready")
        rowmax_ready = sem("rowmax_ready")
        exp_done = sem("exp_done")
        probs_ready = sem("probs_ready")
        out_ready = sem("out_ready")
        out_copied = sem("out_copied")
        phase = {e: sem(f"phase_{e}") for e in ("pe", "act", "dve")}
        dve_step = sem("dve_step")
        act_step = sem("act_step")
        stores = sem("stores")
        handoff = {k: sem(k) for k in ("lam_in", "lam_e", "decay_d", "decay_e", "qk_ready", "qk_used", "f_ready", "logf",
                                       "relu_done", "relu_used", "isc_done", "silu_done", "prod_done", "act_hi", "rest_done", "h_hi", "o_raw", "o_hi",
                                       "sq_done", "onorm_mean", "onorm_root", "onorm_rs",
                                       "onorm_done", "gate_done", "wz_ready", "kd_ready")}

        def halves(w, cols, nk=KC):
            v = w.rearrange("(k p) n -> p k n", p=128)
            ks = 4 if sum(z - a for a, z in cols) <= 256 else 2
            return [(v, k, min(ks, nk - k), cols) for k in range(0, nk, ks)]

        def slot_view(t, ring, n):
            _, _, nk, cols = stream[n]
            width = sum(z - a for a, z in cols)
            return t[:, n % ring, 0:nk * width].rearrange("p (k c) -> p k c", c=width)

        blk = lambda a, b, step=512: [[(i, min(i + step, b))] for i in range(a, b, step)]
        HALF = ((0, FH), (FH, FC))
        ORDER = {}
        stream = []

        def add(name, w, blocks, nk=KC):
            ORDER[name] = [halves(w, cols, nk) for cols in blocks]
            for b in ORDER[name]:
                stream.extend(b)

        add("a_in", A["w_in_ab"][0], blk(0, 1536))
        add("b_gates", A["w_in_ab"][0], blk(1536, 2560, 256) + blk(3072, 3584, 256))
        add("b_values", A["w_in_ab"][0], blk(2560, 3072))
        add("ab_out", A["w_out_ab"][0], blk(0, D))

        def add_rest(l):
            add(f"xq{l}", A["w_xq"][l], blk(0, D, 256))
            add(f"xk{l}", A["w_xk"][l], blk(0, D))
            add(f"xv{l}", A["w_xv"][l], blk(0, D))
            add(f"xo{l}", A["w_xo"][l], blk(0, D))
            for part, (a, z) in enumerate(HALF):
                add(f"up{l}{part}", A["w_ffn_in"][l], [[(128 * j, 128 * j + 128), (DFF + 128 * j, DFF + 128 * j + 128)]
                                                       for j in range(a, z)])
                add(f"down{l}{part}", A["w_ffn_out"][l][a * 128:z * 128, :], blk(0, D), z - a)

        add_rest(0)
        add("c_idx", A["w_in_c"][0], [[(WC_IQ, WC_IK)], [(WC_IK, WC_END)]])
        add("c_qkv", A["w_in_c"][0], blk(0, WC_IQ))
        add("c_out", A["w_out_c"][0], blk(0, D))
        add_rest(1)

        block = ctx.enter_context(nc.Block())

        K_A, V_A = A["cache_diff_k"][0], A["cache_diff_v"][0]
        K_C, V_C, IK_C = A["cache_dsa_k"][0], A["cache_dsa_v"][0], A["cache_dsa_ik"][0]
        CL = []

        def diff_slots():
            for b in range(NB + 1):
                if b < NB:
                    CL.extend([("ka", b, 0), ("ka", b, 4)])
                if b > 0:
                    CL.extend([("va", b - 1, 0), ("va", b - 1, 4)])

        def cross_slots(l):
            CL.extend([(f"mk{l}", b, 0) for b in range(NB)])
            CL.extend([(f"mv{l}", b, 0) for b in range(NB)])

        def dsa_slots():
            CL.extend([("kc", 0, 0), ("kc", 1, 0)])
            for p in range(1, NB // 2 + 1):
                if p < NB // 2:
                    CL.extend([("kc", 2 * p, 0), ("kc", 2 * p + 1, 0)])
                CL.extend([("vc", 2 * p - 2, 0), ("vc", 2 * p - 1, 0)])

        def c_pieces(kind, part):
            pages = {"ka": 4, "va": 4, "ik": 8, "kc": 8, "vc": 8}.get(kind, 0)
            return pages // 2 if pages else 1 - part

        LOADS, at = [], 0

        def weights(*names):
            nonlocal at
            for name in names:
                count = sum(len(b) for b in ORDER[name])
                LOADS.extend([("w", n) for n in range(at, at + count)])
                at += count

        def caches(slots, *args):
            nonlocal at
            first = len(CL)
            slots(*args)
            run = [("c", n) for n in range(first, len(CL))]
            early = [("w", n) for n in range(at, at + NW)]
            at += NW
            LOADS.extend(run[:NC_] + early + run[NC_:])

        def rest(name, *names):
            nonlocal at
            at -= NW
            mark = len(LOADS)
            weights(name, *names)
            del LOADS[mark:mark + NW]

        def ffn(l):
            return [f"up{l}0", f"down{l}0", f"up{l}1", f"down{l}1"]

        weights("a_in")
        caches(diff_slots)
        rest("b_gates", "b_values", "ab_out", "xq0", "xk0", "xv0")
        caches(cross_slots, 0)
        rest("xo0", *ffn(0), "c_idx")
        caches(lambda: CL.extend([("ik", b, 0) for b in range(NB)]))
        rest("c_qkv")
        caches(dsa_slots)
        rest("c_out", "xq1", "xk1", "xv1")
        caches(cross_slots, 1)
        rest("xo1", *ffn(1))
        assert sorted(n for kind, n in LOADS if kind == "w") == list(range(len(stream)))

        def w_target(n):
            return 16 * sum(len(stream[m][3]) for m in range(n % NW, n + 1, NW))

        def c_target(n, part):
            return 16 * sum(c_pieces(CL[m][0], part) for m in range(n % NC_, n + 1, NC_))

        def load_cache(eng, n, part):
            kind, b, first = CL[n]
            if n >= NC_:
                eng.wait_ge(c_free, n - NC_ + 1)
            slot = C[:, n % NC_, :]
            if kind[0] == "m":
                src = A["cache_mem_" + kind[1]][int(kind[2]), b].rearrange("(m p) h d -> p m (h d)", p=128)
                eng.dma_start(slot.rearrange("p (m d) -> p m d", m=2), src).then_inc((c_pool if part else c_full)[n % NC_], 16)
                return
            pools = {"ka": K_A, "va": V_A, "kc": K_C, "vc": V_C, "ik": IK_C}[kind]
            v = pools.rearrange("g s d -> s g d") if kind == "ik" else pools.rearrange("g s h d -> s g (h d)")
            width = v.shape[2]
            for j in range(part, 2 * c_pieces(kind, part), 2):
                at = b * NPAGE + first + j
                page = eng.value_load(pt[0:1, at:at + 1], min_val=0, max_val=v.shape[1] - 1)
                eng.dma_start(slot[:, j * width:(j + 1) * width],
                              v[:, bass.ds(page, 1), :].rearrange("s g d -> s (g d)")).then_inc((c_pool if part else c_full)[n % NC_], 16)

        @block.sync
        def _(sp):
            def load_weights(n):
                v, k0, nk, cols = stream[n]
                if n >= NW:
                    sp.wait_ge(w_free, n - NW + 1)
                at = 0
                for a, b in cols:
                    sp.dma_start(slot_view(W, NW, n)[:, :, at:at + b - a], v[:, k0:k0 + nk, a:b]).then_inc(w_full[n % NW], 16)
                    at += b - a

            sp.dma_start(pt[0:1, :], A["page_table"].rearrange("b n -> (b n)").unsqueeze(0)).then_inc(pages_in, 16)
            for kind, n in LOADS:
                if kind == "w":
                    load_weights(n)
                    continue
                if n == 0:
                    sp.wait_ge(pages_in, 16)
                load_cache(sp, n, 0)

        POOL0 = next(n for n, e in enumerate(stream) if e is ORDER["c_qkv"][0][0]) + NV
        POOL1 = POOL0 + sum(len(b) for b in ORDER["c_qkv"]) - NV

        def split_ready(eng, n):
            if POOL0 <= n < POOL1:
                eng.wait_ge(lo_pool, n - POOL0 + 1)
            else:
                eng.wait_ge(lo_done, n + 1 - (POOL1 - POOL0 if n >= POOL1 else 0))

        @block.gpsimd
        def _(pool):
            def rests():
                for n in range(POOL0, POOL1):
                    pool.wait_ge(hi_done, n + 1)
                    nc.gpsimd.tensor_tensor(slot_view(WL, NW, n), slot_view(W, NW, n), plain(slot_view(WH, NV, n)),
                                            ALU.subtract).then_inc(lo_pool, 1)

            pool.wait_ge(pages_in, 16)
            first_kc = next(n for n, (kind, _, _) in enumerate(CL) if kind == "kc")
            for n, (kind, _, _) in enumerate(CL):
                if n == first_kc + NC_:
                    rests()
                if kind[0] != "m":
                    load_cache(pool, n, 1)

        @block.tensor
        def _(pe):
            S = {"w": 0, "c": 0, "job": 0, "phase": 0, "xn": 0, "release": 0}
            pj, tj = Turns(), Turns()
            mm, tp = nc.tensor.matmul, nc.tensor.transpose

            def barrier():
                S["phase"] += 1
                pe.drain().then_inc(phase["pe"], 1)
                for e in ("act", "dve"):
                    pe.wait_ge(phase[e], S["phase"])

            def open_bank(who):
                n = pj.add(who)
                last = pj.last_use(n, NBANK)
                if last is not None:
                    w = pj.who[last]
                    pe.wait_ge(proj_act if w == "A" else proj_dve, pj.count(w, last + 1))
                return n

            def open_tr(who):
                n = tj.add(who)
                if n >= 2:
                    w = tj.who[n - 2]
                    pe.wait_ge(tr_act if w == "A" else tr_dve, tj.count(w, n - 1))
                return tbank(n)

            def wait_tr(n=None):
                n = len(tj.who) if n is None else n
                for w, s in (("A", tr_act), ("D", tr_dve)):
                    if tj.count(w, n):
                        pe.wait_ge(s, tj.count(w, n))

            def wait_projections():
                for w, s in (("A", proj_act), ("D", proj_dve)):
                    if pj.count(w, len(pj.who)):
                        pe.wait_ge(s, pj.count(w, len(pj.who)))

            def cache():
                n = S["c"]
                S["c"] += 1
                pe.wait_ge(c_full[n % NC_], c_target(n, 0))
                if c_target(n, 1):
                    pe.wait_ge(c_pool[n % NC_], c_target(n, 1))
                return C[:, n % NC_, :]


            def slots_of(b):
                for s, (_, k0, nk, _) in enumerate(b):
                    n = S["w"]
                    S["w"] += 1
                    split_ready(pe, n)
                    yield slot_view(WH, NV, n), slot_view(WL, NW, n), k0, nk, s == 0, s == len(b) - 1

            def project(name, src, tiles, who, ready=None):
                xh, xl = src
                for b in ORDER[name]:
                    units = []
                    for wh, wl, k0, nk, first, last in slots_of(b):
                        width = wh.shape[2]
                        if ready:
                            ready(k0 + nk)
                        for u, (c0, rows) in enumerate(tiles):
                            if first:
                                units.append(open_bank(who))
                            o = bank(units[u])[0:rows, 0:width]
                            for k in range(nk):
                                for e, (v, w) in enumerate(((xh, wh), (xh, wl), (xl, wh))):
                                    ins = mm(o, v[:, k0 + k, c0:c0 + rows], w[:, k, :], start=first and k == 0 and e == 0,
                                             stop=last and k == nk - 1 and e == 2)
                            if last:
                                ins.then_inc(proj_done, 1)
                        if last:
                            pe.drain().then_inc(w_free, 1)
                        else:
                            ins.then_inc(w_free, 1)

            def project_features(name, who, between=None):
                pj.align(3)
                xh, xl = hX
                for at, b in enumerate(ORDER[name]):
                    if at == 1 and between:
                        between()
                    u = [open_bank(who) for _ in range(3)][0]
                    for wh, wl, k0, nk, first, last in slots_of(b):
                        for c, t0, t1, at, opens in FPIECES:
                            o = fset(u)[:, at:at + t1 - t0]
                            for k in range(nk):
                                for e, (v, w) in enumerate(((xh, wh), (xh, wl), (xl, wh))):
                                    ins = mm(o, w[:, k, c * 128:c * 128 + 128], v[:, k0 + k, t0:t1],
                                             start=opens and first and k == 0 and e == 0,
                                             stop=last and k == nk - 1 and e == 2, skip_group_check=True)
                        if last:
                            ins.then_inc(proj_done, 3)
                            pe.drain().then_inc(w_free, 1)
                        else:
                            ins.then_inc(w_free, 1)

            def norm_transposes(tiles):
                for i, (c0, rows) in enumerate(tiles):
                    S["xn"] += 1
                    pe.wait_ge(xn_done, S["xn"])
                    for g in range(2):
                        t = open_tr("D")
                        for c in range(4):
                            ins = tp(t[:, c * 128:c * 128 + rows], xn[i % 2][0:rows, (4 * g + c) * 128:(4 * g + c + 1) * 128],
                                     ident[0:rows, 0:rows])
                        ins.then_inc(tr_done, 1)

            def tr_unit(who, pieces):
                t = open_tr(who)
                for off, src in pieces:
                    rows, cols = src.shape[0], src.shape[1]
                    ins = tp(t[0:cols, off:off + rows], src, ident[0:rows, 0:rows])
                ins.then_inc(tr_done, 1)

            def attend(jobs, prep, scores, prob_units, values, p=P, turned=None):
                depth = len(p)
                if S["job"]:
                    pe.wait_ge(out_copied, S["job"])

                def start(j):
                    n = S["job"] + j
                    if prep:
                        prep(j)
                    if j >= depth:
                        pe.wait_ge(out_copied, n - depth + 1)
                    scores(j, job_bank(j, depth)).then_inc(scores_ready, 1)

                def turn(j):
                    pe.wait_ge(out_copied, S["job"] + j + 1)
                    for pieces in turned:
                        tr_unit("D", pieces)

                for j in range(min(depth - 1, len(jobs))):
                    start(j)
                for j in range(len(jobs)):
                    n = S["job"] + j
                    pe.wait_ge(probs_ready, n + 1)
                    for who, pieces in prob_units(j, p[j % depth]):
                        tr_unit(who, pieces)
                    done = len(tj.who)
                    if turned and j > 0:
                        turn(j - 1)
                    if j + depth - 1 < len(jobs):
                        start(j + depth - 1)
                    wait_tr(done)
                    values(j, job_bank(j, depth)).then_inc(out_ready, 1)
                    if S["release"]:
                        pe.drain().then_inc(c_free, S["release"])
                        S["release"] = 0
                if turned:
                    turn(len(jobs) - 1)
                S["job"] += len(jobs)

            pe.wait_ge(first_in, FIRST)
            tr_unit("D", [(8 * c, L["grow"][0:8, c * 128:c * 128 + 128]) for c in range(8)])
            tr_unit("D", [(0, L["srow"][0:10, 0:128])])
            barrier()

            norm_transposes(COLS)
            barrier()
            project("a_in", hX, COLS, "A")
            barrier()
            for i, (c0, rows) in enumerate(COLS):
                tr_unit("D", [(h * 128, L["a_qk"][0:rows, i, h * 128:h * 128 + 128]) for h in range(H)])
                tr_unit("A", [(h * 128, L["a_qk"][0:rows, i, 512 + h * 128:640 + h * 128]) for h in range(H)])
            barrier()
            qT, kT, qz, KT, a_v = L["qT_a"], L["kT_a"], L["qz_a"], L["KT_a"], L["a_v"]
            jobs = JOBS_AP

            def ap_scores(j, s):
                i, h = jobs[j]
                n = (i + 1) * 128
                for m in range(2):
                    r = slice(64 * m, 64 * m + 64)
                    mm(s[:, 512 * m:512 * m + n], qT[r, h, i * 128:i * 128 + 128], kT[r, h, 0:n], start=True, stop=False,
                       skip_group_check=True)
                    ins = mm(s[:, 512 * m + n - 128:512 * m + n], identb[:, :], causalb[:, :], start=False, stop=True,
                             skip_group_check=True)
                return ins

            def ap_units(j, p):
                i, h = jobs[j]
                return [("A", [(c * 128, p[:, c * 128:c * 128 + 128]) for c in range(i + 1)])]

            def ap_values(j, s):
                i, h = jobs[j]
                for c in range(i + 1):
                    ins = mm(s[:, 0:128], a_v[:, c, h * 128:h * 128 + 128], PT[:, c, :], start=c == 0, stop=c == i)
                return ins

            attend(jobs, None, ap_scores, ap_units, ap_values, P + [P3])

            def as_prep(b):
                for half in range(2):
                    k = cache().rearrange("p (g h d) -> p g h d", g=4, h=H)
                    for h in range(H):
                        t = open_tr("A" if h % 2 else "D")
                        for g in range(4):
                            ins = tp(t[:, g * 128:g * 128 + 128], k[:, g, h, :], ident)
                        ins.then_inc(tr_done, 1)
                    pe.drain().then_inc(c_free, 1)
                wait_tr()

            def as_scores(b, s):
                mm(s[:, 1024:1088], identb[:, :], newmaskb[:, 56 - 8 * b:120 - 8 * b], start=True, stop=False, skip_group_check=True)
                for h in range(H):
                    o = slice(32 * h, 32 * h + 32)
                    for c in range(2):
                        mm(s[o, 512 * c:512 * c + 512], qz[:, b, h, :], KT[:, h, 512 * c:512 * c + 512], start=True, stop=True)
                    ins = mm(s[o, 1024:1088], qz[:, b, h, :], kT[:, h, SEQ:TOK], start=False, stop=True, skip_group_check=True)
                return ins

            def past_units(j, p):
                return [("D", [(c * 128, p[:, c * 128:c * 128 + 128]) for c in range(4)]),
                        ("A", [(c * 128, p[:, (c + 4) * 128:(c + 5) * 128]) for c in range(4)]),
                        ("D", [(0, p[:, 1024:1088])])]

            def as_values(b, s):
                for half in range(2):
                    v = cache().rearrange("p (g h d) -> p g h d", g=4, h=H)
                    for c in range(4 * half, 4 * half + 4):
                        for h in range(H):
                            o = slice(32 * h, 32 * h + 32)
                            ins = mm(s[o, 0:128], PT[:, c, o], v[:, c % 4, h, :], start=c == 0, stop=False, skip_group_check=True)
                    if half == 0:
                        pe.drain().then_inc(c_free, 1)
                for h in range(H):
                    o = slice(32 * h, 32 * h + 32)
                    ins = mm(s[o, 0:128], PT[0:64, 8, o], a_v[0:64, 4, h * 128:h * 128 + 128], start=False, stop=True,
                             skip_group_check=True)
                S["release"] = 1
                return ins

            attend(list(range(NB)), as_prep, as_scores, past_units, as_values, turned=[[(0, OS)]])
            barrier()
            project_features("b_gates", "A")
            project("b_values", hX, COLS, "A")
            barrier()

            QKs = [L["QK"], L["QK2"]]
            HQ, HK, QK, ATT, KD, SS, ib = L["HQ"], L["HK"], L["QK"], L["ATT"], L["KD"], L["SS"], L["ib"]
            for n, h in enumerate(LEVELS):
                pe.wait_ge(handoff["qk_ready"], n + 1)
                for i, (c0, rows) in enumerate(COLS):
                    if i == 4 and h > 4:
                        continue
                    u = open_bank("D")
                    for e in range(H):
                        lhs = (HK if h == 0 else QKs[n % 2])[:, e, c0:c0 + rows]
                        rhs = (HQ if h == 0 else QKs[n % 2])[:, e, c0:c0 + rows]
                        ins = mm(bank(u)[0:rows, e * 128:e * 128 + rows], lhs, rhs, start=True, stop=True)
                    ins.then_inc(proj_done, 1)
                pe.drain().then_inc(handoff["qk_used"], 1)
            barrier()
            pe.wait_ge(handoff["qk_ready"], len(LEVELS) + 1)
            for i, (c0, rows) in enumerate(COLS):
                tr_unit("A", [(e * 128, QK[:, e, c0:c0 + rows]) for e in range(H)])
            barrier()
            for i in range(4):
                u = open_bank("D")
                for e in range(H):
                    ins = mm(bank(u)[:, e * 128:e * 128 + 128], KD[:, i, e, :], ib[:, i, e * 128:e * 128 + 128], start=True, stop=True)
                ins.then_inc(proj_done, 1)
            barrier()
            for i in range(4):
                u = open_bank("A")
                for e in range(H):
                    o = bank(u)[:, e * 128:e * 128 + 128]
                    ins = mm(o, ib[:, i, e * 128:e * 128 + 128], ATT[:, i, e, :], start=True, stop=i == 0)
                    if i > 0:
                        ins = mm(o, SS[:, i - 1, e, :], QK[:, e, i * 128:i * 128 + 128], start=False, stop=True)
                ins.then_inc(proj_done, 1)
            u = open_bank("A")
            pe.wait_ge(rows_in, ROWS["hgrn"])
            for e in range(H):
                o = bank(u)[:, e * 64:e * 64 + 64]
                mm(o, ib[0:64, 4, e * 128:e * 128 + 128], ATT[0:64, 4, e, 0:64], start=True, stop=False, skip_group_check=True)
                for b in range(NB):
                    ins = mm(o[:, 8 * b:8 * b + 8], L["S0"][:, b, e, :], QK[:, e, SEQ + 8 * b:SEQ + 8 * b + 8],
                             start=False, stop=b == NB - 1, skip_group_check=True)
            ins.then_inc(proj_done, 1)
            for e in range(H):
                pe.wait_ge(handoff["kd_ready"], e + 1)
                for c in range(2):
                    u = open_bank("D")
                    mm(bank(u)[:, 0:512], KD[0:64, 4, e, :], L["Vz"][0:64, e % 2, 512 * c:512 * c + 512],
                       start=True, stop=True).then_inc(proj_done, 1)
            barrier()
            for c in range(KC):
                pe.wait_ge(handoff["sq_done"], c + 1)
                if c >= 2:
                    pe.wait_ge(handoff["onorm_root"], c - 1)
                s = sreg(c)
                mm(s[:, 0:512], const("ones"), L["sq"][:, c % 2, 0:512], start=True, stop=True)
                mm(s[:, 512:576], const("ones"), L["sq"][:, c % 2, 512:576], start=True, stop=True).then_inc(handoff["onorm_mean"], 1)
            barrier()
            project("ab_out", oX, COLS, "D")
            barrier()

            def cross_and_ffn(l):
                norm_transposes(COLS)
                barrier()
                project_features(f"xq{l}", "A", lambda: norm_transposes(COLS[0:2]))
                barrier()
                project(f"xk{l}", mX, COLS[0:2], "A")
                project(f"xv{l}", mX, COLS[0:2], "A")
                barrier()
                for g in range(4):
                    tr_unit("A", [((2 * c + m) * 128, L["mk"][:, m, (2 * g + c) * 128:(2 * g + c + 1) * 128])
                                  for c in range(2) for m in range(2)])
                barrier()
                qT, mkT, mv, qz = L["qxT"], L["mkT"], L["mv"], L["qzx"]
                KTs = [L["mkK"], L["mkT"]]

                def xp_scores(i, s):
                    for h in range(H):
                        for c in range(2):
                            ins = mm(s[:, h * 256:h * 256 + 256], qT[:, 2 * h + c, i * 128:i * 128 + 128],
                                     mkT[:, 2 * h + c, :], start=c == 0, stop=c == 1)
                    return ins

                def xp_units(i, p):
                    return [("A", [((2 * e + m) * 128, p[:, (4 * g + 2 * e + m) * 128:(4 * g + 2 * e + m + 1) * 128])
                                   for e in range(2) for m in range(2)]) for g in range(2)]

                def xp_values(i, s):
                    for h in range(H):
                        for dc in range(2):
                            for m in range(2):
                                ins = mm(s[:, (2 * h + dc) * 128:(2 * h + dc + 1) * 128],
                                         mv[:, m, (2 * h + dc) * 128:(2 * h + dc + 1) * 128], PT[:, 2 * h + m, :],
                                         start=m == 0, stop=m == 1)
                    return ins

                attend(list(range(4)), None, xp_scores, xp_units, xp_values, P + [P3x])

                def xs_keys(k, g):
                    tr_unit("A" if g % 2 else "D",
                            [((2 * c + m) * 128, k[:, m, (2 * g + c) * 128:(2 * g + c + 1) * 128])
                             for c in range(2) for m in range(2)])

                def xs_scores(j, s):
                    for b in range(-1, NB):
                        done = len(tj.who)
                        if b + 1 < NB:
                            k = cache().rearrange("p (m d) -> p m d", m=2)
                        for h in range(H):
                            if b + 1 < NB:
                                xs_keys(k, h)
                            if b < 0:
                                continue
                            wait_tr(done - 3 + h)
                            for c in range(2):
                                ins = mm(s[64 * (h % 2):64 * (h % 2) + 64, 512 * (h // 2):512 * (h // 2) + 256],
                                         qz[:, 2 * h + c, b * 64:b * 64 + 64], KTs[b % 2][:, 2 * h + c, :],
                                         start=b == 0 and c == 0, stop=b == NB - 1 and c == 1, skip_group_check=True)
                        if b + 1 < NB:
                            pe.drain().then_inc(c_free, 1)
                    return ins

                def xs_units(j, p):
                    return [("A", [((2 * g + m) * 128, p[:, (2 * g + m) * 128:(2 * g + m + 1) * 128])
                                   for g in range(2) for m in range(2)])]

                def xs_values(j, s):
                    for b in range(NB):
                        v = cache().rearrange("p (m d) -> p m d", m=2)
                        for h in range(H):
                            for m in range(2):
                                ins = mm(s[0:64, 256 * h:256 * h + 256], qz[:, 2 * h + m, b * 64:b * 64 + 64],
                                         v[:, m, 256 * h:256 * h + 256], start=b == 0 and m == 0 and h % 2 == 0,
                                         stop=b == NB - 1 and m == 1, skip_group_check=True)
                        if b < NB - 1:
                            ins.then_inc(c_free, 1)
                    S["release"] = 1
                    return ins

                attend([0], None, xs_scores, xs_units, xs_values,
                       turned=[[(64 * e, OSx[0:64, (4 * g + e) * 128:(4 * g + e + 1) * 128]) for e in range(4)] for g in range(2)])
                barrier()
                project(f"xo{l}", oX, COLS, "D")
                barrier()

                pe.wait_ge(rows_in, ROWS[f"ffn{l}"])
                for c in range(0, FC, 4):
                    t = open_tr("D")
                    for e in range(min(4, FC - c)):
                        ins = tp(t[:, e * 20:e * 20 + 20], L["frow"][0:20, (c + e) * 128:(c + e + 1) * 128], ident[0:20, 0:20])
                    ins.then_inc(tr_done, 1)
                norm_transposes(COLS)
                barrier()
                for part in range(2):
                    project_features(f"up{l}{part}", "D")
                    chunks = l * FC + HALF[part][0]
                    project(f"down{l}{part}", (aH, aL), COLS, "D",
                            lambda n: pe.wait_ge(handoff["rest_done"], chunks + n))
                wait_projections()
                for c in range(0, FC, 4):
                    tr_unit2("A", c)
                barrier()

            def tr_unit2(who, c):
                t = open_tr(who)
                for e in range(min(4, FC - c)):
                    ins = tp(t[0:18, e * 128:e * 128 + 128], L["cstate"][:, c + e, :], ident)
                ins.then_inc(tr_done, 1)

            cross_and_ffn(0)

            norm_transposes(COLS)
            barrier()
            project("c_idx", hX, COLS, "A")
            barrier()
            iT, ikT = L["iqT"], L["ikT"]
            for i, (c0, rows) in enumerate(COLS):
                for g in range(2):
                    tr_unit("A" if g else "D", [(e * 128, L["i_tm"][0:rows, i, (4 * g + e) * 64:(4 * g + e + 1) * 64])
                                                for e in range(4)])
            for i, (c0, rows) in enumerate(COLS):
                tr_unit("D", [(0, L["i_tm"][0:rows, i, 512:576])])
            tr_unit("D", [(0, L["i_tm"][0:64, 4, 576:584])])
            barrier()
            u = open_bank("D")
            mm(bank(u)[0:64, 0:64], const("heads", 8), L["iwT"][0:8, :], start=True, stop=True).then_inc(proj_done, 1)
            for i in range(1, 4):
                n = (i + 1) * 128
                for h in range(8):
                    u = open_bank("A")
                    mm(bank(u)[:, 0:n], iT[0:64, h, i * 128:i * 128 + 128], ikT[0:64, 0:n], start=True, stop=True)\
                        .then_inc(proj_done, 1)
            barrier()

            def ik_prep(b):
                k = cache()[:, 0:512].rearrange("p (g d) -> p g d", g=8)
                for g in range(2):
                    tr_unit("A", [(c * 128, k[:, 4 * g + c, :]) for c in range(4)])
                pe.drain().then_inc(c_free, 1)

            ik_prep(0)
            for b in range(NB):
                done = len(tj.who)
                wait_tr(done)
                if b > 0:
                    pe.wait_ge(handoff["relu_done"], b)
                s = sreg(0)
                q = L["iqs"][0:64, b, :]
                for c in range(2):
                    mm(s[0:64, 512 * c:512 * c + 512], q, L["IKT"][0:64, b % 2, 512 * c:512 * c + 512], start=True, stop=True)
                mm(s[0:64, 1024:1088], q, ikT[0:64, SEQ:TOK], start=True, stop=True).then_inc(handoff["isc_done"], 1)
                if b + 1 < NB:
                    ik_prep(b + 1)
                pe.wait_ge(handoff["relu_done"], b + 1)
                if b == 0:
                    pe.wait_ge(handoff["wz_ready"], 1)
                t = sreg(1)
                for c, (a, z) in enumerate(((0, 512), (512, 1024), (1024, 1088))):
                    ins = mm(t[0:64, a:z], L["wz"][0:64, b * 64:b * 64 + 64], L["relu"][0:64, b % 2, a:z],
                             start=b == 0, stop=b == NB - 1, skip_group_check=True)
                ins.then_inc(handoff["relu_used"], 1)
            barrier()
            project("c_qkv", hX, COLS, "A")
            barrier()
            for i, (c0, rows) in enumerate(COLS):
                for g in range(2):
                    tr_unit("D" if g else "A", [(e * 128, L["c_tm"][0:rows, i, (4 * g + e) * 128:(4 * g + e + 1) * 128])
                                                for e in range(4)])
                tr_unit("D", [(e * 128, L["c_tm"][0:rows, i, 1024 + e * 128:1152 + e * 128]) for e in range(2)])
            barrier()
            qT, kT, KT, v_tm = L["qT_c"], L["kT_c"], L["KT_c"], L["v_c"]
            jobs = JOBS_CP

            def cp_scores(j, s):
                i, hp = jobs[j]
                n = (i + 1) * 128
                for e in range(2):
                    h = 2 * hp + e
                    mm(s[:, 512 * e:512 * e + n], qT[:, h, i * 128:i * 128 + 128], kT[:, h // 4, 0:n], start=True, stop=False,
                       skip_group_check=True)
                    if i == 0:
                        ins = mm(s[:, 512 * e:512 * e + n], identb[:, :], causalb[:, :], start=False, stop=True, skip_group_check=True)
                    else:
                        ins = mm(s[:, 512 * e:512 * e + n], identb[:, :], L["selp"][i - 1], start=False, stop=True,
                                 skip_group_check=True)
                return ins

            def cp_units(j, p):
                i, hp = jobs[j]
                return [("A", [(c * 128, p[:, e * 512 + c * 128:e * 512 + c * 128 + 128]) for c in range(i + 1)]) for e in range(2)]

            def cp_values(j, s):
                i, hp = jobs[j]
                for e in range(2):
                    g = (2 * hp + e) // 4
                    for c in range(i + 1):
                        ins = mm(s[:, e * 128:e * 128 + 128], v_tm[:, c, g * 128:g * 128 + 128], PT[:, 4 * e + c, :],
                                 start=c == 0, stop=c == i)
                return ins

            attend(jobs, None, cp_scores, cp_units, cp_values, P + [P3])

            def cs_prep(p):
                for bb in range(2):
                    k = cache().rearrange("p (n g d) -> p n g d", n=8, g=2)
                    for g in range(2):
                        for half in range(2):
                            tr_unit("A" if half else "D", [(c * 128, k[:, 4 * half + c, g, :]) for c in range(4)])
                    pe.drain().then_inc(c_free, 1)
                wait_tr()

            def cs_scores(p, s):
                ex = L["expb"][0:64, p * 128:p * 128 + 128]
                for a, z in ((0, 512), (512, 1024), (1024, 1088)):
                    mm(s[:, a:z], ex, L["sels"][0:64, a:z], start=True, stop=False, skip_group_check=True)
                for bb in range(2):
                    b = 2 * p + bb
                    for g in range(2):
                        r = 2 * bb + g
                        q = L["qs_c"][:, b, g, :]
                        o = slice(32 * r, 32 * r + 32)
                        for c in range(2):
                            mm(s[o, 512 * c:512 * c + 512], q, KT[:, r, 512 * c:512 * c + 512], start=False, stop=True,
                               skip_group_check=True)
                        ins = mm(s[o, 1024:1088], q, kT[:, g, SEQ:TOK], start=False, stop=True, skip_group_check=True)
                return ins

            def cs_values(p, s):
                for bb in range(2):
                    v = cache().rearrange("p (n g d) -> p n g d", n=8, g=2)
                    rows = [slice(64 * bb + 32 * g, 64 * bb + 32 * g + 32) for g in range(2)]
                    for c in range(NPAGE):
                        for g, r in enumerate(rows):
                            mm(s[r, 0:128], PT[:, c, r], v[:, c, g, :], start=c == 0, stop=False, skip_group_check=True)
                    for g, r in enumerate(rows):
                        ins = mm(s[r, 0:128], PT[0:64, 8, r], v_tm[0:64, 4, g * 128:g * 128 + 128], start=False, stop=True,
                                 skip_group_check=True)
                    if bb == 0:
                        pe.drain().then_inc(c_free, 1)
                S["release"] = 1
                return ins

            attend(list(range(NB // 2)), cs_prep, cs_scores, past_units, cs_values, turned=[[(0, OS)]])
            barrier()
            project("c_out", oX, COLS, "D")
            barrier()
            cross_and_ffn(1)

        @block.scalar
        def _(act):
            S = {"phase": 0, "job": 0, "stores": 0, "means": 0, "ffn": 0}
            pj, tj = Turns(), Turns()
            step = Chain(act, act_step)
            fn = nc.scalar.activation
            S["split"], S["slot"], S["hi"], S["o"] = 0, 0, 0, 0

            def ahead(k):
                while S["split"] < min(k, len(stream)):
                    n = S["split"]
                    S["split"] += 1
                    act.wait_ge(w_full[n % NW], w_target(n))
                    if n >= NV:
                        act.wait_ge(w_free, n - NV + 1)
                    fn(slot_view(WH, NV, n), slot_view(W, NW, n), ACT.Copy).then_inc(hi_done, 1)

            def blocks(name):
                for b in ORDER[name]:
                    ahead(S["slot"] + len(b) + 2)
                    S["slot"] += len(b)
                    yield b
                ahead(S["slot"] + 3)

            def leading(count):
                for dst, src, n in count:
                    act.wait_ge(tr_dve, n)
                    fn(dst, src, ACT.Copy).then_inc(handoff["h_hi"], 1)

            def barrier(stored=True):
                if S["stores"] and stored:
                    act.wait_ge(stores, 16 * S["stores"])
                S["phase"] += 1
                act.drain().then_inc(phase["act"], 1)
                for e in ("pe", "dve"):
                    act.wait_ge(phase[e], S["phase"])

            def store(dst, src):
                S["stores"] += 1
                act.dma_start(dst, src).then_inc(stores, 16)

            def load(dst, src):
                act.dma_start(dst, src).then_inc(rows_in, 16)

            def banks(who, count):
                for _ in range(count):
                    n = pj.add(who)
                    if who == "A":
                        act.wait_ge(proj_done, pj.uses(n + 1))
                        yield bank(n)
                    else:
                        yield None

            def feature_block():
                n = [pj.add("A") for _ in range(3)][0]
                act.wait_ge(proj_done, pj.uses(n + 3))
                return fchunks(n)

            def tr(who):
                n = tj.add(who)
                if who != "A":
                    return None
                act.wait_ge(tr_done, n + 1)
                return tbank(n)

            def tr_copy(who, out, rows=128, view=None):
                t = tr(who)
                if t is not None:
                    fn(out, t if view is None else view(t), ACT.Copy).then_inc(tr_act, 1)

            def pass_by(name, scratch=None):
                for b, _ in enumerate(blocks(name)):
                    first = len(pj.who)
                    for i in range(NTILE):
                        pj.add("D")
                    if scratch is not None and b == len(ORDER[name]) - 1:
                        squares_of(x, COLS, scratch, lambda i: act.wait_ge(proj_dve, pj.count("D", first + i + 1)))
                        take_roots()

            def squares_of(src, tiles, scratch, ready=None):
                for i, (c0, rows) in enumerate(tiles):
                    if ready:
                        ready(i)
                    ins = fn(scratch[0:rows, :], src[0:rows, i, :], ACT.Square, accum_out=ss[0:rows, i:i + 1])
                    if i < len(tiles) - 1:
                        step(ins)
                    else:
                        ins.then_inc(squares, 1)

            def take_roots():
                S["means"] += 1
                act.wait_ge(means, S["means"])
                fn(sd, ms, ACT.Sqrt).then_inc(roots, 1)

            def rows_out(src, tiles, hi=hH, raw=xr):
                pending = []
                for i, (c0, rows) in enumerate(tiles):
                    if len(pending) > 1:
                        leading(pending.pop(0))
                    n = tj.count("D", len(tj.who))
                    pending.append([(hi[:, 4 * e:4 * e + 4, c0:c0 + rows], raw[:, 4 * e:4 * e + 4, c0:c0 + rows], n + e + 1)
                                    for e in range(2)])
                    if i >= 2:
                        act.wait_ge(tr_done, len(tj.who) - 2)
                    fn(xn[i % 2][0:rows, :], src[0:rows, i, :], ACT.Copy, scale=rstd[0:rows, i:i + 1]).then_inc(xn_done, 1)
                    tr("D"), tr("D")
                return pending

            def normalise():
                act.wait_ge(rstds, S["means"])
                for p in rows_out(x, COLS):
                    leading(p)

            def copies(name, tiles, dst):
                who = "A"
                for (a, z), _ in zip(dst, blocks(name), strict=True):
                    for i, (c0, rows) in enumerate(tiles):
                        for v in banks(who, 1):
                            if v is not None:
                                fn(a(i)[0:rows], v[0:rows, 0:z], ACT.Copy).then_inc(proj_act, 1)

            def attend(count, exps, outs, prep=None, p=P, turned=0):
                depth = len(p)

                def start(j):
                    n = S["job"] + j
                    if prep:
                        prep(j)
                    act.wait_ge(rowmax_ready, n + 1)
                    exps(j, j % depth, job_bank(j, depth), p[j % depth]).then_inc(exp_done, 1)

                for j in range(min(depth - 1, count)):
                    start(j)
                for j in range(count):
                    outs(j)
                    for _ in range(turned if j else 0):
                        tr("D")
                    if j + depth - 1 < count:
                        start(j + depth - 1)
                for _ in range(turned):
                    tr("D")
                S["job"] += count

            act.dma_start(x[:, 0:4, :], A["x_prompt"][0].rearrange("(i p) d -> p i d", p=128)).then_inc(x_in, 16)
            act.dma_start(x[0:64, 4, :], A["x_sample"].rearrange("b t d -> (b t) d")).then_inc(x_in, 16)
            act.dma_start(cst[:, :], A["consts"]).then_inc(first_in, 16)
            act.dma_start(L["lev_in"], A["levels"]).then_inc(first_in, 16)
            for r, name in ((0, "norm_mix"), (2, "norm_x"), (4, "norm_mem"), (6, "norm_ffn")):
                act.dma_start(L["grow"][r:r + 2, :], A[name]).then_inc(first_in, 16)
            act.dma_start(L["srow"][0:1, :], A["diff_subln"]).then_inc(first_in, 16)
            act.dma_start(L["srow"][1:2, :], A["hgrn_onorm"]).then_inc(first_in, 16)
            act.dma_start(L["srow"][2:10, :], A["hgrn_lb_logits"].rearrange("l (h k) -> (l h) k", h=H)).then_inc(first_in, 16)
            for i, name in enumerate(("diff_lq1", "diff_lk1", "diff_lq2", "diff_lk2")):
                act.dma_start(L["lrow"][:, i, :], A[name].to_broadcast([128, 64])).then_inc(first_in, 16)
            act.wait_ge(x_in, 32)
            act.wait_ge(dve_step, 1)
            squares_of(x, COLS, junk)
            act.wait_ge(first_in, FIRST)
            tr("D"), tr("D")
            act.wait_ge(handoff["lam_in"], 1)
            fn(L["le"][:, 0:2], L["ls"][:, 0:2], ACT.Exp).then_inc(handoff["lam_e"], 1)
            act.wait_ge(handoff["lam_in"], 2)
            fn(L["lbe"][:, 0:8], L["lbd"][:, 0:8], ACT.Exp).then_inc(handoff["lam_e"], 1)
            barrier()

            take_roots()
            ahead(3)
            normalise()
            barrier()
            copies("a_in", COLS, [((lambda i, b=b: L["a_qk"][:, i, 512 * b:512 * b + 512]), 512) for b in range(2)]
                   + [((lambda i: L["a_v"][:, i, :]), 512)])
            barrier()
            for i, (c0, rows) in enumerate(COLS):
                tr("D")
                tr_copy("A", L["kT_a"][:, :, c0:c0 + rows], view=lambda t: t.rearrange("p (h t) -> p h t", h=H)[:, :, 0:rows])
            store(O["diff_k_p"].rearrange("(i p) h d -> p i (h d)", p=128), L["a_qk"][:, 0:4, 512:1024])
            store(O["diff_v_p"].rearrange("(i p) h d -> p i (h d)", p=128), L["a_v"][:, 0:4, :])
            store(O["diff_k_s"].rearrange("b t h d -> (b t) (h d)"), L["a_qk"][0:64, 4, 512:1024])
            store(O["diff_v_s"].rearrange("b t h d -> (b t) (h d)"), L["a_v"][0:64, 4, :])
            barrier()

            def two_exps(scale, width):
                def run(j, n, s, p):
                    m = width(j)
                    for e in range(2):
                        ins = fn(p[:, 512 * e:512 * e + m], s[:, 512 * e:512 * e + m], ACT.Exp, bias=nms[n][:, e:e + 1],
                                 scale=scale, accum_out=sms[n][:, e:e + 1])
                    return ins
                return run

            def ap_outs(j):
                i, h = JOBS_AP[j]
                tr_copy("A", PT[:, 0:i + 1, :], view=lambda t: t[:, 0:(i + 1) * 128].rearrange("p (c q) -> p c q", c=i + 1))

            attend(16, two_exps(64 ** -0.5, lambda j: (JOBS_AP[j][0] + 1) * 128), ap_outs, p=P + [P3])

            def as_prep(b):
                for half in range(2):
                    for h in range(H):
                        tr_copy("A" if h % 2 else "D", L["KT_a"][:, h, half * 512:half * 512 + 512])

            def one_exp(scale):
                return lambda j, n, s, p: fn(p[:, 0:1088], s[:, 0:1088], ACT.Exp, bias=nms[n][:, 0:1], scale=scale,
                                             accum_out=sms[n][:, 0:1])

            def past_outs(j):
                tr("D")
                tr_copy("A", PT[:, 4:8, :], view=lambda t: t.rearrange("p (c q) -> p c q", c=4))
                tr("D")

            attend(NB, one_exp(64 ** -0.5), past_outs, as_prep, turned=1)
            barrier()
            HQ, HK = L["HQ"], L["HK"]
            pj.align(3)
            dsts = [(dst[:, 2 * g:2 * g + 2], f) for dst, f in ((HQ, ACT.Silu), (HK, ACT.Sigmoid), (oT[:, 4:8, :], ACT.Silu))
                    for g in range(2)]
            for (dst, f), _ in zip(dsts, blocks("b_gates"), strict=True):
                fn(dst, feature_block(), f).then_inc(proj_act, 3)
            copies("b_values", COLS, [((lambda i: L["ib"][:, i, :]), 512)])
            barrier()
            for g in range(8):
                load(L["S0"][:, g], A["state_hgrn"][0, g].rearrange("h k v -> k h v"))
            QKs = [L["QK"], L["QK2"]]
            act.wait_ge(handoff["f_ready"], 1)
            fn(L["QK"], L["B"], ACT.Ln).then_inc(handoff["logf"], 1)
            for n, h in enumerate(LEVELS):
                if h:
                    act.wait_ge(handoff["decay_d"], n)
                    e = QKs[n % 2] if h <= 4 else QKs[n % 2][:, :, 0:SEQ]
                    fn(e, e, ACT.Exp).then_inc(handoff["decay_e"], 1)
                for i in range(5 if h <= 4 else 4):
                    pj.add("D")
            barrier()
            act.wait_ge(handoff["decay_d"], len(LEVELS))
            fn(L["QK"], L["QK"], ACT.Exp).then_inc(handoff["decay_e"], 1)
            for i, (c0, rows) in enumerate(COLS):
                tr_copy("A", L["KD"][0:rows, i, :, :], view=lambda t: t[0:rows].rearrange("p (h k) -> p h k", h=H))
            barrier()
            for i in range(4):
                pj.add("D")
            fn(L["QK"], L["B"], ACT.Exp).then_inc(handoff["decay_e"], 1)
            barrier()
            for i in range(4):
                for v in banks("A", 1):
                    fn(L["OB"][:, :, i * 128:i * 128 + 128], v.rearrange("p (h t) -> p h t", h=H), ACT.Copy).then_inc(proj_act, 1)
            for v in banks("A", 1):
                fn(L["OB"][:, :, SEQ:TOK], v[:, 0:256].rearrange("p (h t) -> p h t", h=H), ACT.Copy).then_inc(proj_act, 1)
            for i in range(8):
                pj.add("D")
            barrier()
            store(O["hgrn_p"].rearrange("h k v -> k h v"), L["SS"][:, 3, :, :])
            for g in range(8):
                store(O["hgrn_s"][g].rearrange("h k v -> k h v"), L["S0"][:, g])

            def square(c):
                if c >= 2:
                    act.wait_ge(handoff["onorm_mean"], c - 1)
                fn(L["sq"][:, c % 2, :], oT[:, c, :] if c < 4 else L["OB"][:, c - 4, :], ACT.Square).then_inc(handoff["sq_done"], 1)

            def high(c):
                act.wait_ge(handoff["o_raw"], c + 1)
                fn(oH[:, c, :], xr[:, c, :], ACT.Copy).then_inc(handoff["o_hi"], 1)

            square(0)
            square(1)
            for c in range(KC):
                act.wait_ge(handoff["onorm_mean"], c + 1)
                fn(xr[:, c, :], sreg(c)[:, 0:TOK], ACT.Ln, bias=eps_col).then_inc(handoff["onorm_root"], 1)
                if c + 2 < KC:
                    square(c + 2)
                if c % 4 == 3:
                    act.wait_ge(handoff["onorm_root"], c + 1)
                    four = xr[:, c - 3:c + 1, :]
                    fn(four, four, ACT.Exp, scale=-0.5).then_inc(handoff["onorm_rs"], 1)
            for c in range(KC):
                high(c)
            barrier()
            pass_by("ab_out", region(0, D))
            barrier()

            def cross_and_ffn(l):
                load(L["mem"], A["mem_prompt"][0].rearrange("(m p) d -> p m d", p=128))
                normalise()
                barrier()
                act.wait_ge(rows_in, ROWS[f"mem{l}"])
                squares_of(L["mem"], COLS[0:2], junk)
                take_roots()
                act.wait_ge(rstds, S["means"])
                memory = rows_out(L["mem"], COLS[0:2], mH, mR)
                pj.align(3)
                for g, _ in enumerate(blocks(f"xq{l}")):
                    fn(L["qxT"][:, 2 * g:2 * g + 2, :], feature_block(), ACT.Copy).then_inc(proj_act, 3)
                    if g == 0:
                        for p in memory:
                            leading(p)
                barrier()
                for name, dst in ((f"xk{l}", L["mk"]), (f"xv{l}", L["mv"])):
                    copies(name, COLS[0:2], [((lambda i, b=b: dst[:, i, 512 * b:512 * b + 512]), 512) for b in range(2)])
                barrier()
                store(O["mem_k"][l].rearrange("(m p) h d -> p m (h d)", p=128), L["mk"])
                store(O["mem_v"][l].rearrange("(m p) h d -> p m (h d)", p=128), L["mv"])
                for g in range(4):
                    tr_copy("A", L["mkT"][:, 2 * g:2 * g + 2, :], view=lambda t: t.rearrange("p (c m) -> p c m", c=2))
                barrier(stored=False)

                def xp_exps(j, n, s, p):
                    if j == 2:
                        act.wait_ge(stores, 16 * S["stores"])
                    for h in range(H):
                        ins = fn(p[:, h * 256:h * 256 + 256], s[:, h * 256:h * 256 + 256], ACT.Exp, bias=nms[n][:, h:h + 1],
                                 scale=256 ** -0.5, accum_out=sms[n][:, h:h + 1])
                    return ins

                def xp_outs(j):
                    for g in range(2):
                        tr_copy("A", PT[:, 4 * g:4 * g + 4, :], view=lambda t: t.rearrange("p (c q) -> p c q", c=4))

                attend(4, xp_exps, xp_outs, p=P + [P3x])

                def xs_prep(j):
                    for b in range(NB):
                        for g in range(4):
                            tr_copy("A" if g % 2 else "D", [L["mkK"], L["mkT"]][b % 2][:, 2 * g:2 * g + 2, :],
                                    view=lambda t: t.rearrange("p (c m) -> p c m", c=2))

                def xs_exps(j, n, s, p):
                    for e in range(2):
                        ins = fn(p[:, e * 256:e * 256 + 256], s[:, e * 512:e * 512 + 256], ACT.Exp, bias=nms[n][:, e:e + 1],
                                 scale=256 ** -0.5, accum_out=sms[n][:, e:e + 1])
                    return ins

                def xs_outs(j):
                    t = tr("A")
                    q = L["qzx"].rearrange("p (h m) (b w) -> p h m b w", m=2, w=72)[:, :, :, :, 0:8]
                    for g in range(2):
                        for m in range(2):
                            ins = fn(q[:, 2 * g:2 * g + 2, m], t[:, (2 * g + m) * 128:(2 * g + m + 1) * 128]
                                     .rearrange("p (e b t) -> p e b t", e=2, b=NB), ACT.Copy)
                    ins.then_inc(tr_act, 1)

                attend(1, xs_exps, xs_outs, xs_prep, turned=2)
                barrier()
                load(L["frow"][0:16, :], A["state_ffn_conv"][l].rearrange("b w f -> (b w) f"))
                load(L["frow"][16:19, :], A["conv_ffn_w"][l])
                load(L["frow"][19:20, :], A["conv_ffn_b"][l:l + 1])
                if l == DEPTH - 1:
                    act.dma_start(L["fin"], A["norm_final"].unsqueeze(0).to_broadcast([128, D])).then_inc(fin_in, 16)
                pass_by(f"xo{l}", region(3328, D))
                barrier()

                for c in range(0, FC, 4):
                    tr("D")
                normalise()
                barrier()
                gc, sil = L["gc"], L["sil"]
                for part, (a, z) in enumerate(HALF):
                    pj.align(3)
                    up_from = S["slot"]
                    for j, _ in enumerate(blocks(f"up{l}{part}")):
                        for e in range(3):
                            pj.add("D")
                        k = S["ffn"]
                        S["ffn"] += 1
                        act.wait_ge(handoff["gate_done"], k + 1)
                        if k >= 2:
                            act.wait_ge(handoff["rest_done"], k - 1)
                        fn(sil[:, k % 2], gc[:, k % 2], ACT.Silu).then_inc(handoff["silu_done"], 1)
                        act.wait_ge(handoff["prod_done"], k + 1)
                        if j == 0 and part == 1:
                            act.wait_ge(w_free, up_from)
                        fn(aH[:, j, :], sil[:, k % 2], ACT.Copy).then_inc(handoff["act_hi"], 1)
                    pass_by(f"down{l}{part}", junk if part else None)
                for c in range(0, FC, 4):
                    m = min(4, FC - c)
                    tr_copy("A", L["frow"][0:18, c * 128:(c + m) * 128], view=lambda t: t[0:18, 0:m * 128])
                barrier()
                store(O["conv_p"][l], L["frow"][0:2, :])
                store(O["conv_s"][l].rearrange("b w f -> (b w) f"), L["frow"][2:18, :])

            cross_and_ffn(0)

            normalise()
            load(L["ikn"], A["idx_k_norm"].to_broadcast([128, 64]))
            barrier()
            copies("c_idx", COLS, [((lambda i: L["i_tm"][:, i, 0:512]), 512), ((lambda i: L["i_tm"][:, i, 512:584]), 72)])
            act.wait_ge(proj_act, pj.count("A", len(pj.who)))
            for i, (c0, rows) in enumerate(COLS):
                ins = fn(L["ikj"][0:rows, :], L["i_tm"][0:rows, i, 512:576], ACT.Square, accum_out=ss[0:rows, i:i + 1])
                if i < NTILE - 1:
                    step(ins)
                else:
                    ins.then_inc(squares, 1)
            S["means"] += 1
            act.wait_ge(means, S["means"])
            fn(sd, ms, ACT.Sqrt).then_inc(roots, 1)
            barrier()
            for i, (c0, rows) in enumerate(COLS):
                tr("D")
                tr_copy("A", L["iqT"][0:64, 4:8, c0:c0 + rows],
                        view=lambda t: t[0:64].rearrange("p (h t) -> p h t", h=4)[:, :, 0:rows])
            for i in range(6):
                tr("D")
            store(O["dsa_ik_p"].rearrange("(i p) d -> p i d", p=128), L["i_tm"][:, 0:4, 512:576])
            store(O["dsa_ik_s"].rearrange("b t d -> (b t) d"), L["i_tm"][0:64, 4, 512:576])
            barrier()
            pj.add("D")
            k = 0
            for i in range(1, 4):
                n = (i + 1) * 128
                for h in range(8):
                    for v in banks("A", 1):
                        if k >= 2:
                            act.wait_ge(handoff["relu_used"], k - 1)
                        fn(L["relup"][:, k % 2, 0:n], v[:, 0:n], ACT.Relu).then_inc(proj_act, 1)
                    k += 1
            barrier()
            for g in range(2):
                tr_copy("A", L["IKT"][0:64, 0, 512 * g:512 * g + 512], view=lambda t: t[0:64])
            for b in range(NB):
                act.wait_ge(handoff["isc_done"], b + 1)
                if b >= 2:
                    act.wait_ge(handoff["relu_used"], 24 + b - 1)
                fn(L["relu"][0:64, b % 2, :], sreg(0)[0:64, 0:1088], ACT.Relu).then_inc(handoff["relu_done"], 1)
                if b + 1 < NB:
                    for g in range(2):
                        tr_copy("A", L["IKT"][0:64, (b + 1) % 2, 512 * g:512 * g + 512], view=lambda t: t[0:64])
            barrier()
            for b, _ in enumerate(blocks("c_qkv")):
                for i, (c0, rows) in enumerate(COLS):
                    for v in banks("A", 1):
                        if b < 2:
                            fn(L["c_tm"][0:rows, i, 512 * b:512 * b + 512], v[0:rows], ACT.Copy).then_inc(proj_act, 1)
                        else:
                            step(fn(L["c_tm"][0:rows, i, 1024:1280], v[0:rows, 0:256], ACT.Copy))
                            fn(L["v_c"][0:rows, i, :], v[0:rows, 256:512], ACT.Copy).then_inc(proj_act, 1)
            barrier()
            for i, (c0, rows) in enumerate(COLS):
                tr_copy("A", L["qT_c"][:, 0:4, c0:c0 + rows], view=lambda t: t.rearrange("p (h t) -> p h t", h=4)[:, :, 0:rows])
                tr("D")
                tr("D")
            store(O["dsa_k_p"].rearrange("(i p) h d -> p i (h d)", p=128), L["c_tm"][:, 0:4, 1024:1280])
            store(O["dsa_v_p"].rearrange("(i p) h d -> p i (h d)", p=128), L["v_c"][:, 0:4, :])
            store(O["dsa_k_s"].rearrange("b t h d -> (b t) (h d)"), L["c_tm"][0:64, 4, 1024:1280])
            store(O["dsa_v_s"].rearrange("b t h d -> (b t) (h d)"), L["v_c"][0:64, 4, :])
            barrier()

            def cp_outs(j):
                i, hp = JOBS_CP[j]
                for e in range(2):
                    tr_copy("A", PT[:, 4 * e:4 * e + i + 1, :],
                            view=lambda t: t[:, 0:(i + 1) * 128].rearrange("p (c q) -> p c q", c=i + 1))

            attend(16, two_exps(128 ** -0.5, lambda j: (JOBS_CP[j][0] + 1) * 128), cp_outs, p=P + [P3])

            def cs_prep(p):
                for bb in range(2):
                    for g in range(2):
                        tr("D")
                        tr_copy("A", L["KT_c"][:, 2 * bb + g, 512:1024])

            attend(NB // 2, one_exp(128 ** -0.5), past_outs, cs_prep, turned=1)
            barrier()
            pass_by("c_out", region(0, D))
            barrier()
            cross_and_ffn(1)
            for i in range(4):
                act.wait_ge(handoff["onorm_done"], KC + i + 1)
                store(O["y_p"][i * 128:i * 128 + 128, :], x[:, i, :])
            act.wait_ge(handoff["onorm_done"], KC + NTILE)
            store(O["y_s"].rearrange("b t d -> (b t) d"), x[0:64, 4, :])
            act.wait_ge(stores, 16 * S["stores"])

        @block.vector
        def _(dve):
            S = {"phase": 0, "job": 0, "norms": 0}
            pj, tj = Turns(), Turns()
            step = Chain(dve, dve_step)
            v_ = nc.vector
            S["split"], S["slot"], S["hi"], S["ffn"] = 0, 0, 0, 0

            def ahead(k):
                while S["split"] < min(k, len(stream)):
                    n = S["split"]
                    S["split"] += 1
                    if POOL0 <= n < POOL1:
                        continue
                    dve.wait_ge(hi_done, n + 1)
                    v_.tensor_tensor(slot_view(WL, NW, n), slot_view(W, NW, n), plain(slot_view(WH, NV, n)), ALU.subtract).then_inc(lo_done, 1)

            def blocks(name):
                for b in ORDER[name]:
                    ahead(S["slot"] + len(b) + 2)
                    S["slot"] += len(b)
                    yield b
                ahead(S["slot"] + 3)

            def pass_by(name, units, between=None):
                for b, _ in enumerate(blocks(name)):
                    for i in range(units):
                        pj.add("A")
                    if b == 0 and between:
                        between()

            def barrier():
                S["phase"] += 1
                dve.drain().then_inc(phase["dve"], 1)
                for e in ("pe", "act"):
                    dve.wait_ge(phase[e], S["phase"])

            def banks(who, count):
                for _ in range(count):
                    n = pj.add(who)
                    if who == "D":
                        dve.wait_ge(proj_done, pj.uses(n + 1))
                        yield bank(n)
                    else:
                        yield None

            def tr(who):
                n = tj.add(who)
                if who != "D":
                    return None
                dve.wait_ge(tr_done, n + 1)
                return tbank(n)

            def tr_copy(who, out, view=None):
                t = tr(who)
                if t is not None:
                    v_.tensor_copy(out, t if view is None else view(t)).then_inc(tr_dve, 1)

            def norm(width=D):
                S["norms"] += 1
                dve.wait_ge(squares, S["norms"])
                v_.tensor_scalar(ms, ss, 1.0 / width, EPS, ALU.mult, ALU.add).then_inc(means, 1)
                dve.wait_ge(roots, S["norms"])
                v_.reciprocal(rstd, sd).then_inc(rstds, 1)

            def normalise(tiles, g, raw=xr, lo=xL, hi=hH):
                pending = []

                def rest():
                    v = pending.pop(0)
                    S["hi"] += 1
                    dve.wait_ge(handoff["h_hi"], S["hi"])
                    v_.tensor_tensor(lo[v], raw[v], plain(hi[v]), ALU.subtract)

                for i, (c0, rows) in enumerate(tiles):
                    for e in range(2):
                        if len(pending) > 3:
                            rest()
                        pending.append((slice(None), slice(4 * e, 4 * e + 4), slice(c0, c0 + rows)))
                        t = tr("D").rearrange("p (c t) -> p c t", c=4)[:, :, 0:rows]
                        gain = gains[:, 4 * e:4 * e + 4, g:g + 1].to_broadcast([128, 4, rows])
                        v_.tensor_tensor(raw[pending[-1]], t, gain, ALU.mult).then_inc(tr_dve, 1)
                while pending:
                    rest()

            def add_to_x(name, then_norm=True):
                for b, _ in enumerate(blocks(name)):
                    for i, (c0, rows) in enumerate(COLS):
                        for v in banks("D", 1):
                            xs = x[0:rows, i, 512 * b:512 * b + 512]
                            v_.tensor_tensor(xs, xs, v[0:rows, :], ALU.add).then_inc(proj_dve, 1)
                    if then_norm and b == len(ORDER[name]) - 1:
                        norm()

            def rotate(t, table, half, heads, tmp="ropet"):
                rows = t.shape[0]
                a = L[tmp][0:rows, 0, 0:heads * 2 * half].rearrange("p (h d) -> p h d", h=heads)
                b = L[tmp][0:rows, 1, 0:heads * 2 * half].rearrange("p (h d) -> p h d", h=heads)
                bc = lambda s, lo, hi: table[:, s, lo:hi].unsqueeze(1).to_broadcast([rows, heads, hi - lo])
                v_.tensor_tensor(a, t[:, :, 0:2 * half], bc(0, 0, 2 * half), ALU.mult)
                v_.tensor_tensor(b[:, :, 0:half], t[:, :, half:2 * half], bc(1, 0, half), ALU.mult)
                step(v_.tensor_tensor(b[:, :, half:2 * half], t[:, :, 0:half], bc(1, half, 2 * half), ALU.mult))
                step(v_.tensor_tensor(t[:, :, 0:2 * half], a, b, ALU.add))

            def attend(count, rowmax, normal, outs, copy, prep=None, p=P, turned=None):
                depth = len(p)

                def start(j):
                    n = S["job"] + j
                    if prep:
                        prep(j)
                    dve.wait_ge(scores_ready, n + 1)
                    rowmax(j, j % depth, job_bank(j, depth))

                def normalised(j):
                    dve.wait_ge(exp_done, S["job"] + j + 1)
                    normal(j, j % depth, p[j % depth])

                for j in range(min(depth - 1, count)):
                    start(j)
                normalised(0)
                for j in range(count):
                    outs(j)
                    if turned and j > 0:
                        turned(j - 1)
                    if depth == 3 and j + 1 < count:
                        normalised(j + 1)
                    if j + depth - 1 < count:
                        start(j + depth - 1)
                    if depth == 2 and j + 1 < count:
                        normalised(j + 1)
                    dve.wait_ge(out_ready, S["job"] + j + 1)
                    copy(j, job_bank(j, depth))
                if turned:
                    turned(count - 1)
                S["job"] += count

            def split_out(at, s, done=None):
                step(v_.tensor_copy(oH[at], s))
                v_.tensor_tensor(xL[at], s, plain(oH[at]), ALU.subtract).then_inc(done or out_copied, 1)

            def biased(n, out, in_, scale, k):
                step(v_.tensor_reduce(out=mxs[n][:, 0:k], in_=in_, axis=AX.X, op=ALU.max))
                v_.tensor_scalar(nms[n][:, 0:k], mxs[n][:, 0:k], -scale, None, ALU.mult).then_inc(rowmax_ready, 1)

            def two_max(scale, width):
                def run(j, n, s):
                    biased(n, None, s[:, 0:1024].rearrange("p (e s) -> p e s", e=2)[:, :, 0:width(j)], scale, 2)
                return run

            def one_max(scale):
                return lambda j, n, s: biased(n, None, s[:, 0:1088], scale, 1)

            v_.memset(misc[:, :], EPS)
            step(v_.memset(stat[:, :], 1.0))
            dve.wait_ge(first_in, FIRST)
            v_.tensor_copy(lev[:, :], L["lev_in"])
            v_.tensor_copy(identb[:, :], ident)
            v_.tensor_copy(causalb[:, :], const("causal"))
            v_.tensor_copy(newmaskb[:, :], const("newmask"))
            tr_copy("D", gains[:, :, :], view=lambda t: t[:, 0:64].rearrange("p (c g) -> p c g", c=8))
            t = tr("D")
            v_.tensor_copy(small[:, :], t[:, 0:10]).then_inc(tr_dve, 1)
            lr = L["lrow"]
            step(v_.tensor_tensor(L["lp"], lr[:, 0:4:2, :], lr[:, 1:4:2, :], ALU.mult))
            v_.tensor_reduce(out=L["ls"][:, 0:2], in_=L["lp"], axis=AX.X, op=ALU.add).then_inc(handoff["lam_in"], 1)
            dve.wait_ge(handoff["lam_e"], 1)
            step(v_.tensor_tensor(L["ld"], L["le"][:, 0:1], L["le"][:, 1:2], ALU.subtract))
            step(v_.tensor_scalar(lam, L["ld"], LAM_INIT, None, ALU.add))
            ms_ = const("mapsel")
            step(v_.tensor_scalar(L["ld"], ms_[:, 1:2], lam, -1.0, ALU.mult, ALU.mult))
            step(v_.tensor_tensor(sgn, L["ld"], ms_[:, 0:1], ALU.add))
            dve.wait_ge(tr_dve, 2)
            v_.tensor_scalar(subg, small[:, 0:1], 1.0 - LAM_INIT, None, ALU.mult)
            step(v_.tensor_tensor(L["lbm"], small[:, 2:6], small[:, 6:10], ALU.max))
            v_.tensor_tensor(L["lbd"][:, 0:4], small[:, 2:6], L["lbm"], ALU.subtract)
            v_.tensor_tensor(L["lbd"][:, 4:8], small[:, 6:10], L["lbm"], ALU.subtract).then_inc(handoff["lam_in"], 1)
            dve.wait_ge(handoff["lam_e"], 2)
            step(v_.tensor_tensor(L["lbm"], L["lbe"][:, 0:4], L["lbe"][:, 4:8], ALU.add))
            step(v_.reciprocal(L["lbr"], L["lbm"]))
            step(v_.tensor_tensor(lb, L["lbe"][:, 0:4], L["lbr"], ALU.mult))
            step(v_.tensor_scalar(omlb, lb, -1.0, 1.0, ALU.mult, ALU.add))
            barrier()

            norm()
            ahead(3)
            normalise(COLS, 0)
            barrier()
            for b, _ in enumerate(blocks("a_in")):
                for i, (c0, rows) in enumerate(COLS):
                    n = pj.add("A")
                    if b == 1:
                        dve.wait_ge(proj_act, pj.count("A", n + 1))
                        rotate(L["a_qk"][0:rows, i, :].rearrange("p (h d) -> p h d", h=16), rope8[0:rows, i], 8, 16)
            barrier()
            for i, (c0, rows) in enumerate(COLS):
                tr_copy("D", L["qT_a"][:, :, c0:c0 + rows], view=lambda t: t.rearrange("p (h t) -> p h t", h=H)[:, :, 0:rows])
                tr("A")
            step(v_.memset(L["qz_a"], 0.0))
            dve.wait_ge(tr_dve, tj.count("D", len(tj.who)))
            for m in range(2):
                r = slice(64 * m, 64 * m + 64)
                for b in range(NB):
                    v_.tensor_copy(L["qz_a"][r, b, :, 8 * m:8 * m + 8], L["qT_a"][r, :, SEQ + 8 * b:SEQ + 8 * b + 8])
            barrier()

            def ap_normal(j, n, p):
                w = (JOBS_AP[j][0] + 1) * 128
                r = rss[n]
                step(v_.reciprocal(r[:, 0:2], sms[n][:, 0:2]))
                step(v_.tensor_scalar(r[:, 2:3], r[:, 1:2], lam, -1.0, ALU.mult, ALU.mult))
                step(v_.tensor_scalar(p[:, 0:w], p[:, 0:w], r[:, 0:1], None, ALU.mult))
                v_.scalar_tensor_tensor(out=p[:, 0:w], in0=p[:, 512:512 + w], scalar=r[:, 2:3], in1=p[:, 0:w],
                                        op0=ALU.mult, op1=ALU.add).then_inc(probs_ready, 1)

            def ap_copy(j, s):
                i, h = JOBS_AP[j]
                v_.tensor_copy(oT[:, h, i * 128:i * 128 + 128], s[:, 0:128]).then_inc(out_copied, 1)

            attend(16, two_max(64 ** -0.5, lambda j: (JOBS_AP[j][0] + 1) * 128), ap_normal, lambda j: tr("A"), ap_copy, p=P + [P3])

            def as_prep(b):
                for half in range(2):
                    for h in range(H):
                        tr_copy("A" if h % 2 else "D", L["KT_a"][:, h, half * 512:half * 512 + 512])

            def as_normal(j, n, p):
                r = rss[n]
                step(v_.reciprocal(r[:, 0:1], sms[n][:, 0:1]))
                v_.tensor_scalar(p[:, 0:1088], p[:, 0:1088], r[:, 0:1], sgn, ALU.mult, ALU.mult).then_inc(probs_ready, 1)

            def past_outs(j):
                tr_copy("D", PT[:, 0:4, :], view=lambda t: t.rearrange("p (c q) -> p c q", c=4))
                tr("A")
                t = tr("D")
                v_.tensor_copy(PT[0:64, 8, :], t[0:64, 0:128]).then_inc(tr_dve, 1)

            def os_copy(j, s):
                v_.tensor_copy(OS, s[:, 0:128]).then_inc(out_copied, 1)

            def as_turned(b):
                o = tr("D")[:, 0:128].rearrange("p (h m q) -> p h q m", h=H, m=4)[:, :, :, 0:2]
                v_.tensor_reduce(out=oT[:, 0:H, SEQ + 8 * b:SEQ + 8 * b + 8], in_=o, axis=AX.X, op=ALU.add).then_inc(tr_dve, 1)

            attend(NB, one_max(64 ** -0.5), as_normal, past_outs, os_copy, as_prep, turned=as_turned)
            barrier()
            pj.align(3)
            pass_by("b_gates", 3)
            pass_by("b_values", 5)
            barrier()
            HQ, HK, QK, B, ATT, SS = (L[k] for k in ("HQ", "HK", "QK", "B", "ATT", "SS"))
            for e in range(H):
                ins = v_.tensor_scalar(HK[:, e, :], HK[:, e, :], omlb[:, e:e + 1], lb[:, e:e + 1], ALU.mult, ALU.add)
            step(ins)
            v_.tensor_scalar(B, HK, 1e-19, None, ALU.max).then_inc(handoff["f_ready"], 1)
            v_.tensor_scalar(HK, HK, -1.0, 1.0, ALU.mult, ALU.add)
            v_.tensor_scalar(HQ, HQ, 128 ** -0.5, None, ALU.mult).then_inc(handoff["qk_ready"], 1)
            v_.memset(ATT, 0.0)
            dve.wait_ge(handoff["logf"], 1)
            for e in range(H):
                ins = v_.tensor_tensor_scan(out=B[:, e, :], data0=const("reset"), data1=QK[:, e, :], initial=0.0,
                                            op0=ALU.mult, op1=ALU.add)
            step(ins)

            def attend_level(n, h):
                mask = levels[:, n, :]
                if n > 0:
                    dve.wait_ge(proj_dve, pj.count("D", len(pj.who)))
                for i, (c0, rows) in enumerate(COLS):
                    if i == 4 and h > 4:
                        continue
                    for v in banks("D", 1):
                        m = mask[0:rows, 0:rows].unsqueeze(1).to_broadcast([rows, H, rows])
                        v_.copy_predicated(ATT[0:rows, i, :, 0:rows], m,
                                           v[0:rows].rearrange("p (h t) -> p h t", h=H)[:, :, 0:rows]).then_inc(proj_dve, 1)

            QKs = [QK, L["QK2"]]

            def cutter(h):
                w = TOK if h <= 4 else SEQ
                return w // (2 * h), lambda t: t[:, :, 0:w].rearrange("p e (n s) -> p e n s", s=2 * h)

            def decays(n):
                h = LEVELS[n]
                nb, cut = cutter(h)
                q = cut(QKs[n % 2])
                anchor = cut(B)[:, :, :, h - 1:h].to_broadcast([128, H, nb, h])
                if n >= 3:
                    dve.wait_ge(handoff["qk_used"], n - 1)
                v_.tensor_tensor(q[:, :, :, h:2 * h], cut(B)[:, :, :, h:2 * h], anchor, ALU.subtract)
                v_.tensor_tensor(q[:, :, :, 0:h], anchor, cut(B)[:, :, :, 0:h], ALU.subtract).then_inc(handoff["decay_d"], 1)

            decays(1)
            for n in range(1, len(LEVELS)):
                h = LEVELS[n]
                if n + 1 < len(LEVELS):
                    decays(n + 1)
                nb, cut = cutter(h)
                q = cut(QKs[n % 2])
                dve.wait_ge(handoff["decay_e"], n)
                v_.tensor_tensor(q[:, :, :, h:2 * h], q[:, :, :, h:2 * h], cut(HQ)[:, :, :, h:2 * h], ALU.mult)
                v_.tensor_tensor(q[:, :, :, 0:h], q[:, :, :, 0:h], cut(HK)[:, :, :, 0:h], ALU.mult)\
                    .then_inc(handoff["qk_ready"], 1)
                attend_level(n - 1, LEVELS[n - 1])
            attend_level(len(LEVELS) - 1, LEVELS[-1])
            barrier()
            for w, n, a in ((128, 4, 0), (TS, NB, SEQ)):
                cut = lambda t: t[:, :, a:a + w * n].rearrange("p e (n s) -> p e n s", s=w)
                ins = v_.tensor_tensor(cut(QK), cut(B)[:, :, :, w - 1:w].to_broadcast([128, H, n, w]), cut(B), ALU.subtract)
            ins.then_inc(handoff["decay_d"], 1)
            dve.wait_ge(handoff["decay_e"], len(LEVELS))
            v_.tensor_tensor(QK, QK, HK, ALU.mult).then_inc(handoff["qk_ready"], 1)
            for i in range(5):
                tr("A")
            barrier()
            dve.wait_ge(handoff["decay_e"], len(LEVELS) + 1)
            for i in range(4):
                for v in banks("D", 1):
                    new = v.rearrange("p (h v) -> p h v", h=H)
                    if i == 0:
                        ins = v_.tensor_copy(SS[:, 0], new)
                        ins.then_inc(proj_dve, 1)
                        dve.wait_ge(proj_dve, pj.count("D", len(pj.who)))
                    else:
                        dec = QK[:, :, i * 128 + 127:i * 128 + 128].to_broadcast([128, H, 128])
                        step(v_.tensor_tensor(SS[:, i], SS[:, i - 1], dec, ALU.mult))
                        v_.tensor_tensor(SS[:, i], SS[:, i], new, ALU.add).then_inc(proj_dve, 1)
                        dve.wait_ge(proj_dve, pj.count("D", len(pj.who)))
            step(v_.tensor_copy(L["edec"], QK[:, :, SEQ + TS - 1:TOK:TS]))
            step(v_.tensor_tensor(QK, QK, HQ, ALU.mult))
            barrier()
            for i in range(5):
                pj.add("A")
            dve.wait_ge(rows_in, ROWS["hgrn"])
            dve.wait_ge(proj_act, pj.count("A", len(pj.who)))
            for e in range(H):
                if e >= 2:
                    dve.wait_ge(proj_done, pj.uses(len(pj.who)))
                v_.tensor_tensor(L["Vz"][0:64, e % 2, :].rearrange("p (b v) -> p b v", b=NB),
                                 L["ib"][0:64, 4, e * 128:e * 128 + 128].unsqueeze(1).to_broadcast([64, NB, 128]),
                                 const("rowmask", 64).unsqueeze(2).to_broadcast([64, NB, 128]), ALU.mult)\
                    .then_inc(handoff["kd_ready"], 1)
                s0 = L["S0"][:, :, e, :]
                step(v_.tensor_tensor(s0, s0, L["edec"][:, e, :].unsqueeze(2).to_broadcast([128, NB, 128]), ALU.mult))
                for c in range(2):
                    for v in banks("D", 1):
                        s = L["S0"][:, 4 * c:4 * c + 4, e, :]
                        v_.tensor_tensor(s, s, v.rearrange("p (b v) -> p b v", b=4), ALU.add).then_inc(proj_dve, 1)
            barrier()
            def o_rest(c):
                dve.wait_ge(handoff["o_hi"], c + 1)
                v_.tensor_tensor(xL[:, c, :], xr[:, c, :], plain(oH[:, c, :]), ALU.subtract).then_inc(handoff["onorm_done"], 1)

            for c in range(KC):
                dve.wait_ge(handoff["onorm_rs"], c // 4 + 1)
                r = xr[:, c, :]
                if c < 4:
                    v_.scalar_tensor_tensor(out=r, in0=oT[:, c, :], scalar=subg, in1=r, op0=ALU.mult,
                                            op1=ALU.mult).then_inc(handoff["o_raw"], 1)
                else:
                    step(v_.scalar_tensor_tensor(out=r, in0=L["OB"][:, c - 4, :], scalar=small[:, 1:2], in1=r,
                                                 op0=ALU.mult, op1=ALU.mult))
                    v_.tensor_tensor(r, oT[:, c, :], r, ALU.mult).then_inc(handoff["o_raw"], 1)
            for c in range(KC):
                o_rest(c)
            barrier()
            add_to_x("ab_out")
            barrier()

            def cross_and_ffn(l):
                normalise(COLS, 2 + l)
                barrier()
                norm()
                pj.align(3)
                pass_by(f"xq{l}", 3, lambda: normalise(COLS[0:2], 4 + l, mR, mX[1], mH))
                barrier()
                step(v_.memset(L["qzx"], 0.0))
                for c in range(KC):
                    v_.tensor_copy(L["qzx"][:, c, :].rearrange("p (b w) -> p b w", w=72)[:, :, 0:8],
                                   L["qxT"][:, c, SEQ:TOK].rearrange("p (b t) -> p b t", b=NB))
                pass_by(f"xk{l}", 2)
                pass_by(f"xv{l}", 2)
                barrier()
                for i in range(4):
                    tr("A")
                barrier()

                def xp_normal(j, n, p):
                    r = rss[n]
                    step(v_.reciprocal(r[:, 0:4], sms[n][:, 0:4]))
                    pv = p[:, 0:1024].rearrange("p (h m) -> p h m", h=4)
                    v_.tensor_tensor(pv, pv, r[:, 0:4].unsqueeze(2).to_broadcast([128, 4, 256]), ALU.mult)\
                        .then_inc(probs_ready, 1)

                def xp_copy(i, s):
                    split_out((slice(None), slice(None), slice(i * 128, i * 128 + 128)),
                              s[:, 0:1024].rearrange("p (c q) -> p c q", c=8))

                attend(4, lambda j, n, s: biased(n, None, s[:, 0:1024].rearrange("p (h m) -> p h m", h=4), 256 ** -0.5, 4),
                       xp_normal, lambda j: (tr("A"), tr("A")), xp_copy, p=P + [P3x])

                def xs_prep(j):
                    for b in range(NB):
                        for g in range(4):
                            tr_copy("A" if g % 2 else "D", [L["mkK"], L["mkT"]][b % 2][:, 2 * g:2 * g + 2, :],
                                    view=lambda t: t.rearrange("p (c m) -> p c m", c=2))

                def xs_normal(j, n, p):
                    r = rss[n]
                    step(v_.reciprocal(r[:, 0:2], sms[n][:, 0:2]))
                    pv = p[:, 0:512].rearrange("p (h m) -> p h m", h=2)
                    v_.tensor_tensor(pv, pv, r[:, 0:2].unsqueeze(2).to_broadcast([128, 2, 256]), ALU.mult)\
                        .then_inc(probs_ready, 1)

                def xs_copy(j, s):
                    v_.tensor_copy(OSx[0:64, :], s[0:64, 0:1024]).then_inc(out_copied, 1)

                def xs_turned(j):
                    for g in range(2):
                        split_out((slice(None), slice(4 * g, 4 * g + 4), slice(SEQ, TOK)),
                                  tr("D")[:, 0:256].rearrange("p (c q) -> p c q", c=4), tr_dve)

                attend(1, lambda j, n, s: biased(n, None, s[:, 0:1024].rearrange("p (h m) -> p h m", h=2)[:, :, 0:256],
                                                 256 ** -0.5, 2), xs_normal, lambda j: tr("A"), xs_copy, xs_prep, turned=xs_turned)
                barrier()
                add_to_x(f"xo{l}")
                barrier()
                for c in range(0, FC, 4):
                    m = min(4, FC - c)
                    tr_copy("D", L["fcol"][:, c:c + m, :], view=lambda t: t[:, 0:m * 20].rearrange("p (c r) -> p c r", c=m))
                normalise(COLS, 6 + l)
                barrier()
                fcol, gc, sil, gs, cst_ = (L[k] for k in ("fcol", "gc", "sil", "gs", "cstate"))

                def act_rest(k, j):
                    dve.wait_ge(handoff["act_hi"], k + 1)
                    v_.tensor_tensor(aL[:, j, :], sil[:, k % 2], plain(aH[:, j, :]), ALU.subtract).then_inc(handoff["rest_done"], 1)

                for part, (first_chunk, _) in enumerate(HALF):
                    pj.align(3)
                    for j, _ in enumerate(blocks(f"up{l}{part}")):
                        first = [pj.add("D") for _ in range(3)][0]
                        k, c = S["ffn"], first_chunk + j
                        S["ffn"] += 1
                        w = lambda r: fcol[:, c, 16 + r:17 + r]
                        dve.wait_ge(proj_done, pj.uses(first + 3))
                        gate, up = fchunks(first)[:, 0], fchunks(first)[:, 1]
                        main, g = gate[:, 0:SEQ], gc[:, k % 2, 0:SEQ]
                        gsm = gc[:, k % 2, SEQ:TOK].rearrange("p (b t) -> p b t", b=NB)
                        if k > 0:
                            dve.wait_ge(handoff["gate_done"], k)
                        if k >= 2:
                            dve.wait_ge(handoff["silu_done"], k - 1)
                        v_.tensor_copy(gs[:, :, 0:2], fcol[:, c, 0:16].rearrange("p (b w) -> p b w", b=NB))
                        v_.tensor_copy(gs[:, :, 2:10], gate[:, SEQ:TOK].rearrange("p (b t) -> p b t", b=NB))
                        step(v_.tensor_scalar(g, main, w(2), w(3), ALU.mult, ALU.add))
                        v_.tensor_copy(cst_[:, c, 2:18].rearrange("p (b w) -> p b w", b=NB), gs[:, :, 8:10])
                        v_.tensor_copy(cst_[:, c, 0:2], main[:, SEQ - 2:SEQ])
                        v_.tensor_scalar(gsm, gs[:, :, 2:10], w(2), w(3), ALU.mult, ALU.add)
                        step(v_.scalar_tensor_tensor(out=g[:, 1:SEQ], in0=main[:, 0:SEQ - 1], scalar=w(1), in1=g[:, 1:SEQ],
                                                     op0=ALU.mult, op1=ALU.add))
                        v_.scalar_tensor_tensor(out=gsm, in0=gs[:, :, 1:9], scalar=w(1), in1=gsm, op0=ALU.mult, op1=ALU.add)
                        step(v_.scalar_tensor_tensor(out=g[:, 2:SEQ], in0=main[:, 0:SEQ - 2], scalar=w(0), in1=g[:, 2:SEQ],
                                                     op0=ALU.mult, op1=ALU.add))
                        v_.scalar_tensor_tensor(out=gsm, in0=gs[:, :, 0:8], scalar=w(0), in1=gsm, op0=ALU.mult, op1=ALU.add)\
                            .then_inc(handoff["gate_done"], 1)
                        if j > 0:
                            act_rest(k - 1, j - 1)
                        dve.wait_ge(handoff["silu_done"], k + 1)
                        v_.tensor_tensor(sil[:, k % 2], sil[:, k % 2], up, ALU.mult).then_inc(handoff["prod_done"], 1)
                        dve.drain().then_inc(proj_dve, 3)
                        if c in (FH - 1, FC - 1):
                            act_rest(k, j)
                    add_to_x(f"down{l}{part}", part == 1)
                for c in range(0, FC, 4):
                    tr("A")
                barrier()

            cross_and_ffn(0)

            normalise(COLS, 1)
            barrier()
            pass_by("c_idx", 5)
            dve.wait_ge(rows_in, ROWS["ikn"])
            S["norms"] += 1
            dve.wait_ge(squares, S["norms"])
            v_.tensor_scalar(ms, ss, 1.0 / 64, EPS, ALU.mult, ALU.add).then_inc(means, 1)
            dve.wait_ge(roots, S["norms"])
            v_.reciprocal(rstd, sd).then_inc(rstds, 1)
            dve.wait_ge(rstds, S["norms"])
            for i, (c0, rows) in enumerate(COLS):
                k = L["i_tm"][0:rows, i, 512:576]
                step(v_.scalar_tensor_tensor(out=k, in0=k, scalar=rstd[0:rows, i:i + 1], in1=L["ikn"][0:rows, :],
                                             op0=ALU.mult, op1=ALU.mult))
                rotate(L["i_tm"][0:rows, i, 0:576].rearrange("p (h d) -> p h d", h=9), rope8[0:rows, i], 8, 9, "ropet_i")
                iw = L["i_tm"][0:rows, i, 576:584]
                step(v_.tensor_scalar(iw, iw, 512 ** -0.5, None, ALU.mult))
            barrier()
            for i, (c0, rows) in enumerate(COLS):
                tr_copy("D", L["iqT"][0:64, 0:4, c0:c0 + rows],
                        view=lambda t: t[0:64].rearrange("p (h t) -> p h t", h=4)[:, :, 0:rows])
                tr("A")
            for i, (c0, rows) in enumerate(COLS):
                tr_copy("D", L["ikT"][0:64, c0:c0 + rows], view=lambda t: t[0:64, 0:rows])
            tr_copy("D", L["iwT"][0:8, :], view=lambda t: t[0:8, 0:64])
            dve.wait_ge(tr_act, tj.count("A", len(tj.who)))
            dve.wait_ge(tr_dve, tj.count("D", len(tj.who)))
            v_.tensor_copy(L["iqs"][0:64].rearrange("p b (h q) -> p h b q", h=8),
                           L["iqT"][0:64, :, SEQ:TOK].rearrange("p h (b q) -> p h b q", b=NB))
            barrier()
            step(v_.memset(L["wz"], 0.0))
            for v in banks("D", 1):
                v_.tensor_tensor(L["wz"][0:64, :].rearrange("p (b w) -> p b w", w=72)[:, :, 0:8],
                                 v[0:64, 0:64].rearrange("p (b t) -> p b t", b=NB),
                                 const("sameq", 64).rearrange("p (b t) -> p b t", b=NB), ALU.mult).then_inc(proj_dve, 1)
            k = 0
            for i in range(1, 4):
                n = (i + 1) * 128
                isc = L["iscp"][i - 1]
                for h in range(8):
                    pj.add("A")
                    dve.wait_ge(proj_act, pj.count("A", len(pj.who)))
                    w = L["i_tm"][:, i, 576 + h:577 + h]
                    r = L["relup"][:, k % 2, 0:n]
                    if h == 0:
                        ins = v_.tensor_scalar(isc, r, w, None, ALU.mult)
                    else:
                        ins = v_.scalar_tensor_tensor(out=isc, in0=r, scalar=w, in1=isc, op0=ALU.mult, op1=ALU.add)
                    k += 1
                    ins.then_inc(handoff["relu_used"], 1)
                    dve.wait_ge(handoff["relu_used"], k)
                step(v_.tensor_tensor(isc[:, n - 128:n], isc[:, n - 128:n], const("causal"), ALU.add))
            dve.drain().then_inc(handoff["wz_ready"], 1)
            barrier()
            def select(isc, out, rows, n, k):
                work, top, eq, rank = L["work"][0:rows, 0:n], L["top"][0:rows, :], L["eq"][0:rows, 0:n], L["rank"][0:rows, 0:n]
                c = L["cnt"][0:rows, :]
                src = isc
                for it in range(k // 8):
                    step(v_.max(out=top, in_=src))
                    if it < k // 8 - 1:
                        step(v_.match_replace(out=work, in_to_replace=top, in_values=src, imm_value=-3e38))
                        src = work
                t = top[:, 7:8]
                step(v_.tensor_scalar(eq, isc, t, None, ALU.is_gt, ALU.add, accum_out=c[:, 0:1]))
                step(v_.tensor_scalar(c[:, 1:2], c[:, 0:1], -1.0, float(k), ALU.mult, ALU.add))
                step(v_.tensor_scalar(work, isc, t, None, ALU.is_equal))
                step(v_.tensor_tensor_scan(out=rank, data0=work, data1=work, initial=0.0, op0=ALU.add, op1=ALU.bypass))
                step(v_.tensor_scalar(rank, rank, c[:, 1:2], None, ALU.is_le))
                step(v_.tensor_tensor(work, work, rank, ALU.mult))
                step(v_.tensor_tensor(work, work, eq, ALU.add))
                step(v_.tensor_scalar(out, work, -NEG, NEG, ALU.mult, ALU.add))

            for i in range(2 * NB):
                tj.add("A")
            for i in range(1, 4):
                select(L["iscp"][i - 1], L["selp"][i - 1], 128, (i + 1) * 128, 128)
            v_.tensor_copy(L["expb"][0:64, :], const("expand", 64))
            dve.wait_ge(handoff["relu_used"], 24 + NB)
            s = sreg(1)
            v_.tensor_copy(L["iscs"][0:64, 0:1024], s[0:64, 0:1024])
            v_.tensor_tensor(L["iscs"][0:64, 1024:1088], s[0:64, 1024:1088], const("block64", 64), ALU.add)
            barrier()
            select(L["iscs"][0:64, :], L["sels"][0:64, :], 64, 1088, 256)
            for b, _ in enumerate(blocks("c_qkv")):
                for i, (c0, rows) in enumerate(COLS):
                    n = pj.add("A")
                    if b == 2:
                        dve.wait_ge(proj_act, pj.count("A", n + 1))
                        rotate(L["c_tm"][0:rows, i, :].rearrange("p (h d) -> p h d", h=10), rope16[0:rows, i], 16, 10, "ropet_c")
            barrier()
            for i, (c0, rows) in enumerate(COLS):
                tr("A")
                tr_copy("D", L["qT_c"][:, 4:8, c0:c0 + rows], view=lambda t: t.rearrange("p (h t) -> p h t", h=4)[:, :, 0:rows])
                tr_copy("D", L["kT_c"][:, :, c0:c0 + rows],
                        view=lambda t: t[:, 0:256].rearrange("p (h t) -> p h t", h=2)[:, :, 0:rows])
            dve.wait_ge(tr_act, tj.count("A", len(tj.who)))
            dve.wait_ge(tr_dve, tj.count("D", len(tj.who)))
            v_.tensor_copy(L["qs_c"].rearrange("p b g (h q) -> p (g h) b q", h=4),
                           L["qT_c"][:, :, SEQ:TOK].rearrange("p h (b q) -> p h b q", b=NB))
            barrier()

            def cp_normal(j, n, p):
                w = (JOBS_CP[j][0] + 1) * 128
                r = rss[n]
                step(v_.reciprocal(r[:, 0:2], sms[n][:, 0:2]))
                for e in range(2):
                    ins = v_.tensor_scalar(p[:, 512 * e:512 * e + w], p[:, 512 * e:512 * e + w], r[:, e:e + 1], None, ALU.mult)
                ins.then_inc(probs_ready, 1)

            def cp_copy(j, s):
                i, hp = JOBS_CP[j]
                split_out((slice(None), slice(2 * hp, 2 * hp + 2), slice(i * 128, i * 128 + 128)),
                          s[:, 0:256].rearrange("p (e q) -> p e q", e=2))

            attend(16, two_max(128 ** -0.5, lambda j: (JOBS_CP[j][0] + 1) * 128), cp_normal, lambda j: (tr("A"), tr("A")), cp_copy,
                   p=P + [P3])

            def cs_prep(p):
                for bb in range(2):
                    for g in range(2):
                        tr_copy("D", L["KT_c"][:, 2 * bb + g, 0:512])
                        tr("A")

            def cs_normal(j, n, p):
                r = rss[n]
                step(v_.reciprocal(r[:, 0:1], sms[n][:, 0:1]))
                v_.tensor_scalar(p[:, 0:1088], p[:, 0:1088], r[:, 0:1], None, ALU.mult).then_inc(probs_ready, 1)

            def cs_turned(p):
                at = (slice(None), slice(None), slice(SEQ + 16 * p, SEQ + 16 * p + 16))
                v = lambda t: t[at].rearrange("p h (b q) -> p b h q", b=2)
                s = tr("D")[:, 0:128].rearrange("p (b h q) -> p b h q", b=2, h=8)
                for bb in range(2):
                    ins = v_.tensor_copy(v(oH)[:, bb], s[:, bb])
                step(ins)
                for bb in range(2):
                    ins = v_.tensor_tensor(v(xL)[:, bb], s[:, bb], plain(v(oH)[:, bb]), ALU.subtract)
                ins.then_inc(tr_dve, 1)

            attend(NB // 2, one_max(128 ** -0.5), cs_normal, past_outs, os_copy, cs_prep, turned=cs_turned)
            barrier()
            add_to_x("c_out")
            barrier()
            cross_and_ffn(1)
            dve.wait_ge(rstds, S["norms"])
            dve.wait_ge(fin_in, 16)
            for i, (c0, rows) in enumerate(COLS):
                xs = x[0:rows, i, :]
                v_.scalar_tensor_tensor(out=xs, in0=xs, scalar=rstd[0:rows, i:i + 1], in1=L["fin"][0:rows, :],
                                        op0=ALU.mult, op1=ALU.mult).then_inc(handoff["onorm_done"], 1)


_INS = ["x_prompt", "x_sample", "cache_diff_k", "cache_diff_v", "state_hgrn", "cache_dsa_k", "cache_dsa_v", "cache_dsa_ik",
        "cache_mem_k", "cache_mem_v", "state_ffn_conv", "page_table", "mem_prompt", "norm_mix", "w_in_ab", "diff_lq1",
        "diff_lk1", "diff_lq2", "diff_lk2", "diff_subln", "hgrn_lb_logits", "hgrn_onorm", "w_out_ab", "w_in_c",
        "idx_k_norm", "w_out_c", "norm_x", "norm_mem", "w_xq", "w_xk", "w_xv", "w_xo", "norm_ffn", "w_ffn_in",
        "conv_ffn_w", "conv_ffn_b", "w_ffn_out", "norm_final"]
_OUTS = [("y_p", (1, 512, 1024)), ("y_s", (8, 8, 1024)), ("diff_k_p", (1, 1, 512, 4, 128)), ("diff_v_p", (1, 1, 512, 4, 128)),
         ("hgrn_p", (1, 1, 4, 128, 128)), ("dsa_k_p", (1, 1, 512, 2, 128)), ("dsa_v_p", (1, 1, 512, 2, 128)),
         ("dsa_ik_p", (1, 1, 512, 64)), ("mem_k", (2, 1, 256, 4, 256)), ("mem_v", (2, 1, 256, 4, 256)),
         ("conv_p", (2, 1, 2, 2816)), ("diff_k_s", (1, 8, 8, 4, 128)), ("diff_v_s", (1, 8, 8, 4, 128)),
         ("hgrn_s", (1, 8, 4, 128, 128)), ("dsa_k_s", (1, 8, 8, 2, 128)), ("dsa_v_s", (1, 8, 8, 2, 128)),
         ("dsa_ik_s", (1, 8, 8, 64)), ("conv_s", (2, 8, 2, 2816))]


def kernel(**inputs):
    import concourse.bacc as _bacc
    from concourse.bass_utils import run_bass_kernel_spmd as _run

    nc = _bacc.Bacc("TRN2", target_bir_lowering=False, num_devices=1)
    arrays, A, O = {}, {}, {}
    for name in _INS:
        a = np.ascontiguousarray(inputs[name])
        arrays[f"in_{name}"] = a
        A[name] = nc.dram_tensor(f"in_{name}", a.shape, mybir.dt.from_np(a.dtype), kind="ExternalInput").ap()
    for name, a in zip(("consts", "levels"), constants()):
        arrays[f"in_{name}"] = a
        A[name] = nc.dram_tensor(f"in_{name}", a.shape, mybir.dt.from_np(a.dtype), kind="ExternalInput").ap()
    for name, shape in _OUTS:
        ap = nc.dram_tensor(f"out_{name}", shape, mybir.dt.float32, kind="ExternalOutput").ap()
        if name in ("diff_k_p", "diff_v_p", "hgrn_p", "dsa_k_p", "dsa_v_p", "dsa_ik_p"):
            ap = ap[0, 0]
        elif name in ("y_p", "diff_k_s", "diff_v_s", "hgrn_s", "dsa_k_s", "dsa_v_s", "dsa_ik_s"):
            ap = ap[0]
        elif name in ("mem_k", "mem_v", "conv_p"):
            ap = ap[:, 0]
        O[name] = ap
    build(nc, A, O)
    r = _run(nc, [arrays], core_ids=[0])
    return tuple(r.results[0][f"out_{name}"] for name, _ in _OUTS)
```
